# Optimizing a Trainium2 kernel written in Bass

```python
import math
import numpy as np
import jax
import jax.numpy as jnp
from jax import lax

D_MODEL = 1024
BATCH = 1
SEQ = 256
DEPTH = 2

N_A_LAYERS = DEPTH // 2
N_B_LAYERS = DEPTH - N_A_LAYERS

NSA_HEADS = 16
NSA_KV_HEADS = 4
NSA_GROUP = NSA_HEADS // NSA_KV_HEADS
HEAD_DIM = 64
CMP_BLOCK = 32
CMP_STRIDE = 16
SEL_BLOCK = 64
SEL_TOP_N = 16
WINDOW = 512
PHI_HIDDEN = 256
NSA_Q_W = NSA_HEADS * HEAD_DIM
NSA_KV_W = NSA_KV_HEADS * HEAD_DIM
NSA_IN_W = NSA_Q_W + 6 * NSA_KV_W + 3 * NSA_HEADS

DIFF_HEADS = 8
DIFF_QK_DIM = 64
DIFF_V_DIM = 128
DIFF_Q_W = DIFF_HEADS * 2 * DIFF_QK_DIM
DIFF_V_W = DIFF_HEADS * DIFF_V_DIM

ROT_DIM = HEAD_DIM // 4
ROPE_THETA = 500000.0

FFN_DIM = 2752
CONV_WIDTH = 3

Q_BLOCK = 128
EPS = 1e-6
NEG = -1e30
FORCE = 1e4

kernel_name = "yoco_nsa_diffattn_convglu_trunk"

def rmsnorm(x, g):
    xf = x.astype(jnp.float32)
    y = xf * lax.rsqrt(jnp.mean(xf * xf, axis=-1, keepdims=True) + EPS)
    return (y * g.astype(jnp.float32)).astype(x.dtype)

def partial_rope(x, pos):
    half = ROT_DIM // 2
    inv = ROPE_THETA ** (-jnp.arange(half, dtype=jnp.float32) / half)
    ang = pos.astype(jnp.float32)[:, None] * inv[None, :]
    cos = jnp.cos(ang)[None, :, None, :].astype(x.dtype)
    sin = jnp.sin(ang)[None, :, None, :].astype(x.dtype)
    x1 = x[..., :half]
    x2 = x[..., half:ROT_DIM]
    return jnp.concatenate([x1 * cos - x2 * sin, x2 * cos + x1 * sin, x[..., ROT_DIM:]], axis=-1)

def masked_softmax(s, mask, axis=-1):
    s = jnp.where(mask, s.astype(jnp.float32), NEG)
    p = jax.nn.softmax(s, axis=axis)
    return jnp.where(mask, p, 0.0)

def compress(kv, pe, w1, b1, w2):
    B, S, Hk, d = kv.shape
    ch = kv.reshape(B, S // CMP_STRIDE, CMP_STRIDE, Hk, d)
    blocks = jnp.concatenate([ch[:, :-1], ch[:, 1:]], axis=2)
    blocks = blocks + pe[None, None, :, None, :]
    nc = blocks.shape[1]
    flat = blocks.transpose(0, 1, 3, 2, 4).reshape(B, nc, Hk, CMP_BLOCK * d)
    hid = jax.nn.gelu(flat @ w1 + b1)
    return hid @ w2

def nsa_mixer(h, w_in, w_out, phi_pe, phi_w1, phi_b1, phi_w2):
    B, S, _ = h.shape
    Hk, G, hd = NSA_KV_HEADS, NSA_GROUP, HEAD_DIM
    proj = h @ w_in
    q = proj[..., :NSA_Q_W].reshape(B, S, NSA_HEADS, hd)
    kv6 = proj[..., NSA_Q_W:NSA_Q_W + 6 * NSA_KV_W].reshape(B, S, 6, Hk, hd)
    kc, vc, ks, vs, kw, vw = (kv6[:, :, i] for i in range(6))
    gates = jax.nn.sigmoid(proj[..., NSA_Q_W + 6 * NSA_KV_W:].astype(jnp.float32)).astype(h.dtype)
    gates = gates.reshape(B, S, NSA_HEADS, 3)

    pos = jnp.arange(S)
    qr = partial_rope(q, pos)
    ks = partial_rope(ks, pos)
    kw = partial_rope(kw, pos)

    k_cmp = compress(kc, phi_pe[0], phi_w1[0], phi_b1[0], phi_w2[0])
    v_cmp = compress(vc, phi_pe[1], phi_w1[1], phi_b1[1], phi_w2[1])
    n_cmp = S // CMP_STRIDE - 1
    n_sel = S // SEL_BLOCK
    top_n = min(SEL_TOP_N, n_sel)
    cmp_end = jnp.arange(n_cmp) * CMP_STRIDE + CMP_BLOCK - 1
    ci = np.arange(n_cmp)[:, None]
    sj = np.arange(n_sel)[None, :]
    overlap = jnp.asarray(((ci * CMP_STRIDE < (sj + 1) * SEL_BLOCK)
                           & (ci * CMP_STRIDE + CMP_BLOCK > sj * SEL_BLOCK)).astype(np.float32))

    ks_blocks = ks.reshape(B, n_sel, SEL_BLOCK, Hk, hd).transpose(0, 3, 1, 2, 4)
    vs_blocks = vs.reshape(B, n_sel, SEL_BLOCK, Hk, hd).transpose(0, 3, 1, 2, 4)
    kw_pad = jnp.pad(kw, ((0, 0), (WINDOW, 0), (0, 0), (0, 0)))
    vw_pad = jnp.pad(vw, ((0, 0), (WINDOW, 0), (0, 0), (0, 0)))
    scale = HEAD_DIM ** -0.5
    b_ix = jnp.arange(B)[:, None, None, None]
    h_ix = jnp.arange(Hk)[None, None, :, None]
    blk = jnp.arange(n_sel)

    def block_fn(i):
        qs = i * Q_BLOCK
        t = qs + jnp.arange(Q_BLOCK)
        qb = lax.dynamic_slice_in_dim(q, qs, Q_BLOCK, axis=1).reshape(B, Q_BLOCK, Hk, G, hd)
        qrb = lax.dynamic_slice_in_dim(qr, qs, Q_BLOCK, axis=1).reshape(B, Q_BLOCK, Hk, G, hd)
        gb = lax.dynamic_slice_in_dim(gates, qs, Q_BLOCK, axis=1).reshape(B, Q_BLOCK, Hk, G, 3)

        s_c = jnp.einsum('bqkgd,bckd->bqkgc', qb, k_cmp) * scale
        m_c = cmp_end[None, :] <= t[:, None]
        p_c = masked_softmax(s_c, m_c[None, :, None, None, :])
        o_c = jnp.einsum('bqkgc,bckd->bqkgd', p_c.astype(v_cmp.dtype), v_cmp)

        imp = jnp.einsum('bqkgc,cn->bqkn', p_c, overlap)
        cur = t // SEL_BLOCK
        valid = blk[None, :] <= cur[:, None]
        forced = (blk[None, :] == 0) | (blk[None, :] == cur[:, None]) | (blk[None, :] == cur[:, None] - 1)
        imp = jnp.where(valid[None, :, None, :],
                        jnp.where(forced[None, :, None, :], FORCE, imp), NEG)
        _, idx = lax.top_k(imp, top_n)

        k_sel = ks_blocks[b_ix, h_ix, idx]
        v_sel = vs_blocks[b_ix, h_ix, idx]
        s_s = jnp.einsum('bqkgd,bqknjd->bqkgnj', qrb, k_sel) * scale
        tok = idx[..., None] * SEL_BLOCK + jnp.arange(SEL_BLOCK)
        m_s = tok <= t[None, :, None, None, None]
        p_s = masked_softmax(s_s, m_s[:, :, :, None], axis=(-2, -1))
        o_s = jnp.einsum('bqkgnj,bqknjd->bqkgd', p_s.astype(v_sel.dtype), v_sel)

        kwb = lax.dynamic_slice_in_dim(kw_pad, qs, Q_BLOCK + WINDOW, axis=1)
        vwb = lax.dynamic_slice_in_dim(vw_pad, qs, Q_BLOCK + WINDOW, axis=1)
        kpos = qs - WINDOW + jnp.arange(Q_BLOCK + WINDOW)
        m_w = (kpos[None, :] <= t[:, None]) & (kpos[None, :] > t[:, None] - WINDOW) & (kpos[None, :] >= 0)
        s_w = jnp.einsum('bqkgd,bwkd->bqkgw', qrb, kwb) * scale
        p_w = masked_softmax(s_w, m_w[None, :, None, None, :])
        o_w = jnp.einsum('bqkgw,bwkd->bqkgd', p_w.astype(vwb.dtype), vwb)

        o = gb[..., 0:1] * o_c + gb[..., 1:2] * o_s + gb[..., 2:3] * o_w
        return o.reshape(B, Q_BLOCK, NSA_Q_W)

    out = lax.map(block_fn, jnp.arange(S // Q_BLOCK))
    out = out.transpose(1, 0, 2, 3).reshape(B, S, NSA_Q_W)
    return out @ w_out

def shared_kv(x, kv_norm_g, kv_w):
    B, S, _ = x.shape
    hkv = rmsnorm(x, kv_norm_g)
    kv = hkv @ kv_w
    k = kv[..., :DIFF_Q_W].reshape(B, S, DIFF_HEADS * 2, DIFF_QK_DIM)
    k = partial_rope(k, jnp.arange(S)).reshape(B, S, DIFF_HEADS, 2, DIFF_QK_DIM)
    v = kv[..., DIFF_Q_W:].reshape(B, S, DIFF_HEADS, DIFF_V_DIM)
    return k, v

def diff_mixer(h, w_q, lam_vec, subln_g, w_out, k, v, lam_init):
    B, S, _ = h.shape
    q = (h @ w_q).reshape(B, S, DIFF_HEADS * 2, DIFF_QK_DIM)
    q = partial_rope(q, jnp.arange(S)).reshape(B, S, DIFF_HEADS, 2, DIFF_QK_DIM)
    lv = lam_vec.astype(jnp.float32)
    lam = jnp.exp(jnp.sum(lv[0] * lv[1])) - jnp.exp(jnp.sum(lv[2] * lv[3])) + lam_init
    scale = DIFF_QK_DIM ** -0.5
    kpos = jnp.arange(S)

    def block_fn(i):
        qs = i * Q_BLOCK
        t = qs + jnp.arange(Q_BLOCK)
        qb = lax.dynamic_slice_in_dim(q, qs, Q_BLOCK, axis=1)
        s = jnp.einsum('bqhcd,bkhcd->bhcqk', qb, k) * scale
        mask = kpos[None, :] <= t[:, None]
        p = masked_softmax(s, mask[None, None, None])
        a = p[:, :, 0] - lam * p[:, :, 1]
        return jnp.einsum('bhqk,bkhd->bqhd', a.astype(v.dtype), v)

    o = lax.map(block_fn, jnp.arange(S // Q_BLOCK))
    o = jnp.moveaxis(o, 0, 1).reshape(B, S, DIFF_HEADS, DIFF_V_DIM)
    o = rmsnorm(o, subln_g) * (1.0 - lam_init)
    return o.reshape(B, S, DIFF_V_W) @ w_out

def conv_glu_ffn(h, w_in, conv_w, conv_b, w_out):
    S = h.shape[1]
    u = h @ w_in
    up = jnp.pad(u, ((0, 0), (CONV_WIDTH - 1, 0), (0, 0)))
    c = conv_b
    for tap in range(CONV_WIDTH):
        c = c + up[:, tap:tap + S] * conv_w[tap]
    gate = c[..., :FFN_DIM]
    val = c[..., FFN_DIM:]
    return (jax.nn.silu(gate) * val) @ w_out

def setup_inputs(seed: int = 0) -> dict:
    key = jax.random.key(seed)
    ks = jax.random.split(key, 24)
    f32 = jnp.float32

    def nrm(k, shape, fan):
        return jax.random.normal(k, shape, f32) * (fan ** -0.5)

    def gain(k, shape):
        return 1.0 + 0.02 * jax.random.normal(k, shape, f32)

    NA, NB = N_A_LAYERS, N_B_LAYERS
    return {
        "x": jax.random.normal(ks[0], (BATCH, SEQ, D_MODEL), f32),
        "attn_norm_g": gain(ks[1], (DEPTH, D_MODEL)),
        "ffn_norm_g": gain(ks[2], (DEPTH, D_MODEL)),
        "nsa_w_in": nrm(ks[3], (NA, D_MODEL, NSA_IN_W), D_MODEL),
        "nsa_w_out": nrm(ks[4], (NA, NSA_Q_W, D_MODEL), NSA_Q_W),
        "nsa_phi_pe": 0.1 * jax.random.normal(ks[5], (NA, 2, CMP_BLOCK, HEAD_DIM), f32),
        "nsa_phi_w1": nrm(ks[6], (NA, 2, CMP_BLOCK * HEAD_DIM, PHI_HIDDEN), CMP_BLOCK * HEAD_DIM),
        "nsa_phi_b1": 0.02 * jax.random.normal(ks[7], (NA, 2, PHI_HIDDEN), f32),
        "nsa_phi_w2": nrm(ks[8], (NA, 2, PHI_HIDDEN, HEAD_DIM), PHI_HIDDEN),
        "kv_norm_g": gain(ks[9], (D_MODEL,)),
        "kv_w": nrm(ks[10], (D_MODEL, DIFF_Q_W + DIFF_V_W), D_MODEL),
        "diff_w_q": nrm(ks[11], (NB, D_MODEL, DIFF_Q_W), D_MODEL),
        "diff_lambda": 0.1 * jax.random.normal(ks[12], (NB, 4, DIFF_QK_DIM), f32),
        "diff_subln_g": gain(ks[13], (NB, DIFF_V_DIM)),
        "diff_w_out": nrm(ks[14], (NB, DIFF_V_W, D_MODEL), DIFF_V_W),
        "ffn_w_in": nrm(ks[15], (DEPTH, D_MODEL, 2 * FFN_DIM), D_MODEL),
        "ffn_conv_w": nrm(ks[16], (DEPTH, CONV_WIDTH, 2 * FFN_DIM), CONV_WIDTH),
        "ffn_conv_b": 0.02 * jax.random.normal(ks[17], (DEPTH, 2 * FFN_DIM), f32),
        "ffn_w_out": nrm(ks[18], (DEPTH, FFN_DIM, D_MODEL), FFN_DIM),
        "final_norm_g": gain(ks[19], (D_MODEL,)),
    }

def reference(x, attn_norm_g, ffn_norm_g, nsa_w_in, nsa_w_out, nsa_phi_pe, nsa_phi_w1, nsa_phi_b1,
              nsa_phi_w2, kv_norm_g, kv_w, diff_w_q, diff_lambda, diff_subln_g, diff_w_out,
              ffn_w_in, ffn_conv_w, ffn_conv_b, ffn_w_out, final_norm_g):
    k_sh = None
    v_sh = None
    for l in range(DEPTH):
        h = rmsnorm(x, attn_norm_g[l])
        if l < N_A_LAYERS:
            x = x + nsa_mixer(h, nsa_w_in[l], nsa_w_out[l], nsa_phi_pe[l], nsa_phi_w1[l],
                              nsa_phi_b1[l], nsa_phi_w2[l])
        else:
            j = l - N_A_LAYERS
            lam_init = 0.8 - 0.6 * math.exp(-0.3 * l)
            x = x + diff_mixer(h, diff_w_q[j], diff_lambda[j], diff_subln_g[j], diff_w_out[j],
                               k_sh, v_sh, lam_init)
        h = rmsnorm(x, ffn_norm_g[l])
        x = x + conv_glu_ffn(h, ffn_w_in[l], ffn_conv_w[l], ffn_conv_b[l], ffn_w_out[l])
        if l == N_A_LAYERS - 1:
            k_sh, v_sh = shared_kv(x, kv_norm_g, kv_w)
    return rmsnorm(x, final_norm_g)


_drawn_inputs = setup_inputs


def setup_inputs(seed=0):
    import zlib

    import numpy as np

    out = dict(_drawn_inputs(seed))
    spreads = {}
    factors = {'attn_norm_g': 3.997,
     'nsa_phi_b1': 5.357,
     'kv_norm_g': 4.29,
     'diff_subln_g': 22.225,
     'final_norm_g': 8.031,
     'ffn_norm_g': 2.855,
     'ffn_conv_b': 3.061}
    for name, (base, spread) in spreads.items():
        noise = np.random.default_rng([zlib.crc32(name.encode()), seed]).standard_normal(out[name].shape)
        drawn = base * np.exp(spread * noise) if base else spread * noise
        out[name] = jnp.asarray(drawn.astype(out[name].dtype))
    for name, factor in factors.items():
        out[name] = (out[name] * factor).astype(out[name].dtype)
    return out
```

```python
import math
from contextlib import ExitStack

import numpy as np

import concourse.bass as bass
from concourse import mybir

F32 = mybir.dt.float32
F32R = mybir.dt.float32r
BF16 = mybir.dt.bfloat16
ALU = mybir.AluOpType
ACT = mybir.ActivationFunctionType
AX = mybir.AxisListType

P = 128
D, S = 1024, 256
TT = S // P
KT = D // P
HEADS, KVH, GROUP, HD = 16, 4, 4, 64
CMP_BLOCK, CMP_STRIDE = 32, 16
NCMP = S // CMP_STRIDE - 1
CP = NCMP + 1
PHI = 256
DH, DV = 8, 128
ROT = HD // 4
FFN = 2752
NJ = -(-FFN // P)
LAM_INIT = 0.8 - 0.6 * math.exp(-0.3)
LAM_OUT = 1 - LAM_INIT
EPS = 1e-6
NEG = -1e30
SCALE = HD ** -0.5

KV_W = KVH * HD
GROUPS = [("cmp", 2 * KV_W), ("q", 6 * HD), ("q", 5 * HD), ("q", 5 * HD + 3 * HEADS), ("k", 2 * KV_W), ("v", 2 * KV_W)]
Q_HEAD0 = [0, 0, 6, 11]
Q_HEADS = [0, 6, 5, 5]
NG = len(GROUPS)

W = 2048
WO = D
NPRM = 8
FW = W + WO + NPRM

C_A, N_A = 0, 2 * NG
C_WO, N_WO = C_A + N_A, 4
C_F0 = C_WO + N_WO
C_KV, N_KV = C_F0 + NJ, 8
C_DQ, N_DQ = C_KV + N_KV, 4
C_DO, N_DO = C_DQ + N_DQ, 4
C_F1 = C_DO + N_DO
C_END = C_F1 + NJ
N_PHI = 4
O_AG, O_FG, O_KG, O_SG = 0, 2 * KT, 4 * KT, 5 * KT
O_PE = O_SG + 1
O_W2 = O_PE + 2 * CP
O_RM = O_W2 + 2 * 2 * P
O_LAM = O_RM + 8
O_COS = O_LAM + 4 * HD
O_SIN = O_COS + TT * ROT
O_CM = O_SIN + TT * ROT
O_CV = O_CM + TT * CP
O_B1 = O_CV + TT
NCOL = O_B1 + 2 * PHI


def width_of(s):
    return 4 * GROUPS[s // 2][1] if s < N_A else W


def stage_of(s):
    return s if s < C_WO else s + N_PHI


def is_ffn(s):
    return C_F0 <= s < C_KV or C_F1 <= s < C_END


def ffn_before(s):
    return max(0, min(s - C_F0, NJ)) + max(0, min(s - C_F1, NJ))


SEMS = """x_in params_in ident_in mask_in identb_in final_in stage0_full stage1_full phi_used
in_hi in_lo in_used out_hi out_lo out_used conv_params
newton xT_bank xT_hi xT_lo square mean_sq root rstd scaled
proj proj_act proj_dve rope_ready rope_t1 rope_t2 rope_done gate_z gate_e gate_e1 gates_ready
pair_T pair_act pair_dve blocks_ready zero
qT_bank qT_act qT_dve kT_bank kT_act kT_dve
hid_pre hid_z hid_z2 hid_w hid_y hid_t hid_ready hidT_bank hidT_ready kcmp_bank kcmp_ready vcmp_bank vcmp_ready
cmp_scores cmp_masked cmp_max cmp_shift cmp_exp cmp_sum cmp_recip cmp_gate cmp_valid cmp_p cmpT_bank cmpT_ready
scores smax negmax probs recip factor scaled_p pT_bank pT_act pT_dve oT_bank oT_act oT_hi oT_lo
x_new u_bank conv0 gate1 val1 gate2 val2 silu prod a_hi a_lo
dk_bank dk_act dk_dve dq_bank dq_done dv_done
lam_prod lam_sum lam_exp lam_diff lam_ready
dscores dsmax dnegmax dprobs drecip dfactor dscaled dmixed dT_bank dT_ready do_bank do_sq do_ready
sub_ms sub_root sub_rstd sub_scaled oT2_bank
out_scaled out_ready stored""".split()


def build(nc, a_x, a_cols, a_ident, a_identb, a_mask, a_groups, a_phi, a_wo, a_ffn, a_kv, a_dq, a_do, a_final, a_out):
    with ExitStack() as ctx:
        def sb(name, shape, dt=F32):
            return ctx.enter_context(nc.sbuf_tensor(name, shape, dt))

        sem = {n: ctx.enter_context(nc.semaphore(n)) for n in SEMS}
        stage_full = [sem["stage0_full"], sem["stage1_full"]]

        x = sb("x", [P, TT, D])
        cols = sb("cols", [P, NCOL])
        ident = sb("ident", [P, P])
        identb = sb("identb", [P, P], BF16)
        cmask = sb("cmask", [P, P], BF16)
        stage = sb("stage", [P, 2, FW])
        win_hi = sb("win_hi", [P, 2, W], F32R)
        win_lo = sb("win_lo", [P, 2, W], F32R)
        wout_hi = sb("wout_hi", [P, 2, WO], F32R)
        wout_lo = sb("wout_lo", [P, 2, WO], F32R)
        hA_hi = sb("hA_hi", [P, KT, S], F32R)
        hA_lo = sb("hA_lo", [P, KT, S], F32R)
        hB_hi = sb("hB_hi", [P, KT, S], F32R)
        hB_lo = sb("hB_lo", [P, KT, S], F32R)
        act_hi = sb("act_hi", [P, 2, S], F32R)
        act_lo = sb("act_lo", [P, 2, S], F32R)
        prm = sb("prm", [P, 2, NPRM])
        keysT = sb("keysT", [P, 2, 2048])
        qT = sb("qT", [P, KT, S])
        qrT = sb("qrT", [P, KT, S])
        tokA = sb("tokA", [P, TT, 16, HD])
        tokB = sb("tokB", [P, TT, 16, HD])
        vals = sb("vals", [P, TT, 1024])
        arena = sb("arena", [P, 6144])
        stat = sb("stat", [P, 660])
        gates = sb("gates", [P, TT, HEADS, 3])
        rope_t = sb("rope_t", [P, 2, TT, 8, ROT])

        psA = ctx.enter_context(nc.psum_tensor("psA", [P, 4, 512], F32))
        psT = ctx.enter_context(nc.psum_tensor("psT", [P, 2, 512], F32))
        psO = ctx.enter_context(nc.psum_tensor("psO", [P, 2, 512], F32))
        free_banks = [psT[:, 0], psT[:, 1], psO[:, 0], psO[:, 1]]

        kvc = arena[:, 0:1024].rearrange("p (t c) -> p t c", t=TT)
        k_tok = arena[:, 1024:2048].rearrange("p (t h d) -> p t h d", t=TT, d=HD)
        pairs = arena[:, 2048:3072].rearrange("p (v h u) -> p v h u", v=2, h=KVH)
        blocks = arena[:, 3072:5120].rearrange("p (v m h i) -> p v m h i", v=2, m=CP, h=KVH)
        kcT = arena[:, 5120:5120 + 2 * KVH * CP].rearrange("p (e g c) -> p e g c", e=2, g=KVH)
        probs = arena[:, 0:2048].rearrange("p (s h t k) -> p s h t k", s=2, h=2, t=2)
        pT = arena[:, 2048:6144].rearrange("p (s t h q) -> p s t h q", s=2, t=4, h=4)
        aT = arena[:, 2048:3072].rearrange("p (s h b q) -> p s h b q", s=2, h=2, b=2)
        conv = arena[:, 0:1024].rearrange("p (s g q) -> p s g q", s=2, g=2)
        silu = arena[:, 1024:1536].rearrange("p (s q) -> p s q", s=2)
        prod = arena[:, 1536:2048].rearrange("p (s q) -> p s q", s=2)
        squares = arena[:, 2048:4096].rearrange("p (t c) -> p t c", t=TT)
        tokA_flat = tokA[:, :, :, :].rearrange("p t h d -> p (t h d)")
        tokB_flat = tokB[:, :, :, :].rearrange("p t h d -> p (t h d)")
        cmp_s = tokA_flat[:, 0:512].rearrange("p (t h c) -> p t h c", t=TT, h=HEADS)
        cmp_p = tokA_flat[:, 512:1024].rearrange("p (t h c) -> p t h c", t=TT, h=HEADS)
        cmp_pT = tokA_flat[:, 1024:1536].rearrange("p (t b q) -> p t b q", t=TT, b=2)
        hid = tokA_flat[:, 0:512].rearrange("p (v f) -> p v f", v=2)[0:64]
        hid_a = tokA_flat[:, 512:1024].rearrange("p (v f) -> p v f", v=2)[0:64]
        hid_b = tokA_flat[:, 1024:1536].rearrange("p (v f) -> p v f", v=2)[0:64]
        hidT = tokA_flat[:, 1536:1664].rearrange("p (t c) -> p t c", t=2)
        hidTv = tokA_flat[:, 512:1536].rearrange("p (t g r c) -> p t g r c", t=2, g=KVH, r=8)
        vcmp = tokB_flat.rearrange("p (h d) -> p h d", h=HEADS)
        xs = tokB_flat.rearrange("p (t c) -> p t c", t=TT)
        o_tok = tokB_flat.rearrange("p (t h d) -> p t h d", t=TT, h=DH)
        final_g = tokA_flat[:, 0:D]
        vals_nsa = vals[:, :, :].rearrange("p t (y g u d) -> p t y g u d", y=2, g=KVH, u=2)

        ssq = stat[:, 0:TT]
        ms = stat[:, 2:2 + TT]
        rstd = stat[:, 4:4 + TT]
        root = stat[:, 6:6 + TT]
        rough = stat[:, 608:608 + TT]
        newton = stat[:, 610:610 + TT]
        mx = stat[:, 8:72].rearrange("p (u c) -> p u c", c=4)
        nmx = stat[:, 72:136].rearrange("p (u c) -> p u c", c=4)
        den = stat[:, 136:200].rearrange("p (u c) -> p u c", c=4)
        rec = stat[:, 200:264].rearrange("p (u c) -> p u c", c=4)
        fac = stat[:, 264:328].rearrange("p (u c) -> p u c", c=4)
        cmx = stat[:, 328:360].rearrange("p (t h) -> p t h", t=TT)
        csum = stat[:, 360:392].rearrange("p (t h) -> p t h", t=TT)
        crec = stat[:, 392:424].rearrange("p (t h) -> p t h", t=TT)
        cfac = stat[:, 424:456].rearrange("p (t h) -> p t h", t=TT)
        gz = stat[:, 456:552].rearrange("p (t c) -> p t c", t=TT)
        lam2 = stat[:, 552:554]
        lame = stat[:, 554:556]
        neg_lam = stat[:, 556:557]
        sq_sub = stat[:, 560:576]
        ms_sub = stat[:, 576:592]
        rstd_sub = stat[:, 592:608]
        root_sub = stat[:, 612:628]
        newton_sub = stat[:, 628:644]
        rough_sub = stat[:, 644:660]

        cosv = cols[:, O_COS:O_SIN].rearrange("p (t r) -> p t r", t=TT)
        sinv = cols[:, O_SIN:O_CM].rearrange("p (t r) -> p t r", t=TT)
        pe = cols[:, O_PE:O_W2].rearrange("p (v m) -> p v m", v=2)
        w2 = cols[:, O_W2:O_RM].rearrange("p (v t d) -> p v t d", v=2, t=2)
        rowmask = cols[:, O_RM:O_LAM]
        b1 = cols[:, O_B1:NCOL].rearrange("p (v f) -> p v f", v=2)[0:64]

        def gain(off, k):
            return cols[:, off + k:off + k + 1]

        block = ctx.enter_context(nc.Block())

        @block.sync
        def _(sp):
            for t in range(TT):
                sp.dma_start(x[:, t, :], a_x[t]).then_inc(sem["x_in"], 16)
            sp.dma_start(ident[:, :], a_ident).then_inc(sem["ident_in"], 16)
            sp.dma_start(cols[:, :], a_cols).then_inc(sem["params_in"], 16)

            def load(n, dst, src, prev_s, prev_phi):
                if prev_s is not None:
                    sp.wait_ge(sem["in_lo"], 2 * (prev_s + 1))
                    if is_ffn(prev_s):
                        sp.wait_ge(sem["conv_params"], ffn_before(prev_s) + 1)
                if prev_phi is not None:
                    sp.wait_ge(sem["phi_used"], prev_phi + 1)
                sp.dma_start(dst, src).then_inc(stage_full[n % 2], 16)

            def load_main(s, src, width):
                n = stage_of(s)
                prev_phi = n - 2 - N_A if C_WO <= s < C_WO + 2 else None
                prev_s = s - 2 if s >= 2 and prev_phi is None else None
                if prev_s is not None and s >= C_WO and prev_s < C_WO:
                    prev_s = None
                load(n, stage[:, n % 2, 0:width], src, prev_s, prev_phi)

            for s in range(N_A):
                w4 = width_of(s)
                load_main(s, a_groups[s // 2][s % 2], w4)
                if s == 1:
                    sp.dma_start(identb[:, :], a_identb).then_inc(sem["identb_in"], 16)
                    sp.dma_start(cmask[:, :], a_mask).then_inc(sem["mask_in"], 16)
            for i in range(N_PHI):
                load(N_A + i, stage[:, i % 2, 0:W], a_phi[i], N_A - 2 + i if i < 2 else None, i - 2 if i >= 2 else None)
            for i in range(N_WO):
                load_main(C_WO + i, a_wo[i], W)

            ffn_after_first = a_ffn.rearrange("l j p c -> (l j) p c")[1:]

            def load_ffn(layer, first):
                for j in range(2):
                    load_main(first + j, a_ffn[layer, j], FW)
                with sp.Fori(layer * NJ + 1, layer * NJ + NJ - 2, 2) as n:
                    for b in range(2):
                        slot = (first + b) % 2
                        sp.wait_ge(sem["conv_params"], n + b)
                        sp.dma_start(stage[:, slot, 0:FW], ffn_after_first[n + b]).then_inc(stage_full[slot], 16)

            load_ffn(0, C_F0)
            for i in range(N_KV):
                load_main(C_KV + i, a_kv[i], W)
            for i in range(N_DQ):
                load_main(C_DQ + i, a_dq[i], W)
            for i in range(N_DO):
                load_main(C_DO + i, a_do[i], W)
            sp.wait_ge(sem["dk_bank"], 4)
            sp.dma_start(final_g, a_final).then_inc(sem["final_in"], 16)
            load_ffn(1, C_F1)
            for t in range(TT):
                sp.wait_ge(sem["out_ready"], t + 1)
                sp.dma_start(a_out[t], x[:, t, :]).then_inc(sem["stored"], 16)
            sp.wait_ge(sem["stored"], 16 * TT)

        @block.tensor
        def _(pe_):
            mm = pe_.matmul

            def three(out, xh, xl, wh, wl, start, stop):
                mm(out, xh, wh, start=start, stop=False)
                mm(out, xh, wl, start=False, stop=False)
                return mm(out, xl, wh, start=False, stop=stop)

            def wait_chunk(s):
                pe_.wait_ge(sem["in_hi"], 2 * (s + 1))
                pe_.wait_ge(sem["in_lo"], 2 * (s + 1))

            def xT(inst, src, waits):
                for b in range(4):
                    for kk in range(2):
                        for t in range(TT):
                            if b == 0 and kk == 0:
                                waits(t)
                            k = 2 * b + kk
                            last = pe_.transpose(free_banks[b][:, (kk * TT + t) * P:(kk * TT + t + 1) * P],
                                                 src[:, t, k * P:(k + 1) * P], ident[:, :])
                    last.then_inc(sem["xT_bank"], 1)

            def project(s0, h_hi, h_lo, out, width, k_tiles):
                for half in range(2):
                    wait_chunk(s0 + half)
                    slot = (s0 + half) % 2
                    wh = win_hi[:, slot, 0:k_tiles * width].rearrange("p (k c) -> p k c", k=k_tiles)
                    wl = win_lo[:, slot, 0:k_tiles * width].rearrange("p (k c) -> p k c", k=k_tiles)
                    for k in range(k_tiles):
                        kk = half * k_tiles + k
                        for t in range(TT):
                            last = three(out[t], h_hi[:, kk, t * P:(t + 1) * P], h_lo[:, kk, t * P:(t + 1) * P],
                                         wh[:, k, :], wl[:, k, :], kk == 0, kk == 2 * k_tiles - 1)
                    last.then_inc(sem["in_used"], 1)

            def out_project(s0, h_hi, h_lo):
                for c in range(4):
                    wait_chunk(s0 + c)
                    slot = (s0 + c) % 2
                    for k in range(2):
                        kk = 2 * c + k
                        for t in range(TT):
                            for n in range(2):
                                cs = slice(k * D + n * 512, k * D + n * 512 + 512)
                                last = three(psA[:, 2 * t + n, :], h_hi[:, kk, t * P:(t + 1) * P], h_lo[:, kk, t * P:(t + 1) * P],
                                             win_hi[:, slot, cs], win_lo[:, slot, cs], kk == 0, kk == KT - 1)
                    last.then_inc(sem["in_used"], 1)

            def ffn(layer, first):
                f0 = layer * NJ

                def up(j, b):
                    slot = (first + b) % 2
                    pe_.wait_ge(sem["in_hi"], 2 * j + 2 * (first + 1))
                    pe_.wait_ge(sem["in_lo"], 2 * j + 2 * (first + 1))
                    for g in range(2):
                        for k in range(KT):
                            cs = slice(k * 2 * P + g * P, k * 2 * P + g * P + P)
                            o = (psT, psO)[g][:, b, 0:S]
                            mm(o, win_hi[:, slot, cs], hA_hi[:, k, :], start=k == 0, stop=False)
                            mm(o, win_hi[:, slot, cs], hA_lo[:, k, :], start=False, stop=False)
                            last = mm(o, win_lo[:, slot, cs], hA_hi[:, k, :], start=False, stop=k == KT - 1)
                        if g == 0:
                            last.then_inc(sem["u_bank"], 1)
                    last.then_inc(sem["in_used"], 1)

                def down(j, b, start, stop):
                    pe_.wait_ge(sem["a_lo"], j + (f0 + 1))
                    pe_.wait_ge(sem["out_lo"], j + (f0 + 1))
                    for t in range(TT):
                        for n in range(2):
                            last = three(psA[:, 2 * t + n, :], act_hi[:, b, t * P:(t + 1) * P], act_lo[:, b, t * P:(t + 1) * P],
                                         wout_hi[:, b, n * 512:(n + 1) * 512], wout_lo[:, b, n * 512:(n + 1) * 512], start, stop)
                    last.then_inc(sem["out_used"], 1)

                pe_.wait_ge(sem["xT_hi"], KT * (2 if layer == 0 else 5))
                pe_.wait_ge(sem["xT_lo"], KT * (2 if layer == 0 else 5))
                up(0, 0)
                up(1, 1)
                down(0, 0, True, False)
                with pe_.Fori(0, NJ // 2 - 1) as i:
                    for b in range(2):
                        pe_.wait_ge(sem["val2"], 2 * i + (f0 + b + 1))
                        pe_.wait_ge(sem["gate2"], 2 * i + (f0 + b + 1))
                        up(2 * i + (2 + b), b)
                        down(2 * i + (1 + b), 1 - b, False, False)
                down(NJ - 1, 1, False, True)

            pe_.wait_ge(sem["ident_in"], 16)

            def wait_x(t):
                pe_.wait_ge(sem["x_in"], 16 * TT)
            xT(0, x, wait_x)
            pe_.wait_ge(sem["xT_lo"], KT)
            pe_.wait_ge(sem["xT_hi"], KT)
            for g, (kind, width) in enumerate(GROUPS):
                if g >= 2:
                    pe_.wait_ge(sem["proj_act"], g - 1)
                    pe_.wait_ge(sem["proj_dve"], g - 1)
                project(2 * g, hA_hi, hA_lo, [psA[:, 2 * (g % 2) + t, 0:width] for t in range(TT)], width, 4)
                if g == 1:
                    pe_.wait_ge(sem["proj_act"], 1)
                    perm = ident[:, :].rearrange("p (u r) -> p r u", r=2)
                    for v in range(2):
                        for pr in range(2):
                            for t in range(TT):
                                last = pe_.transpose(psT[:, v, (pr * TT + t) * P:(pr * TT + t + 1) * P],
                                                     kvc[:, t, v * KV_W + pr * P:v * KV_W + (pr + 1) * P], perm)
                        last.then_inc(sem["pair_T"], 1)
                if g == 4:
                    pe_.wait_ge(sem["proj_act"], 4)
                    pe_.wait_ge(sem["rope_done"], 3)
                    for i in range(8):
                        if i < 2:
                            pe_.wait_ge(sem["pair_act"], 4)
                            pe_.wait_ge(sem["pair_dve"], 4)
                        if i >= 4:
                            pe_.wait_ge(sem["qT_act"], i // 2 - 1)
                            pe_.wait_ge(sem["qT_dve"], i // 2 - 1)
                        src = tokB if i % 2 else tokA
                        for mi in range(2):
                            m = 2 * (i // 2) + mi
                            for t in range(TT):
                                last = pe_.transpose(free_banks[i % 4][:, (mi * TT + t) * P:(mi * TT + t + 1) * P],
                                                     src[:, t, 2 * m:2 * m + 2, :].rearrange("p h d -> p (h d)"), ident[:, :])
                        last.then_inc(sem["qT_bank"], 1)
            pe_.wait_ge(sem["rope_done"], 4)
            for pr in range(2):
                pe_.wait_ge(sem["qT_act"], 4)
                pe_.wait_ge(sem["qT_dve"], 4)
                for y in range(2):
                    for t in range(TT):
                        last = pe_.transpose(psT[:, pr, (y * TT + t) * P:(y * TT + t + 1) * P],
                                             k_tok[:, t, 4 * y + 2 * pr:4 * y + 2 * pr + 2, :].rearrange("p h d -> p (h d)"), ident[:, :])
                last.then_inc(sem["kT_bank"], 1)
            pe_.wait_ge(sem["blocks_ready"], 4)
            pe_.wait_ge(sem["proj_act"], NG)
            pe_.wait_ge(sem["proj_dve"], NG)
            for v in range(2):
                for half in range(2):
                    i = 2 * v + half
                    pe_.wait_ge(stage_full[i % 2], 16 * ((N_A + i) // 2 + 1))
                    for m in range(8):
                        mg = 8 * half + m
                        last = mm(psA[0:64, 0, v * PHI:(v + 1) * PHI], blocks[:, v, mg, :, :].rearrange("p h i -> p (h i)"),
                                  stage[:, i % 2, m * PHI:(m + 1) * PHI], start=mg == 0, stop=mg == CP - 1)
                    last.then_inc(sem["phi_used"], 1)
            pe_.wait_ge(sem["hid_ready"], 1)
            for v in range(2):
                for c in range(2):
                    last = pe_.transpose(psA[:, 1, (2 * v + c) * 64:(2 * v + c + 1) * 64], hid[:, v, c * P:(c + 1) * P], ident[0:64, 0:64])
            last.then_inc(sem["hidT_bank"], 1)
            pe_.wait_ge(sem["hidT_ready"], 1)
            for c in range(2):
                last = mm(psA[:, 2, 0:64], w2[:, 0, c, :], hidT[:, c, :], start=c == 0, stop=c == 1)
            last.then_inc(sem["kcmp_bank"], 1)
            pe_.wait_ge(sem["hidT_ready"], 2)
            for g in range(KVH):
                for c in range(2):
                    last = mm(psA[:, 3, g * P:(g + 1) * P],
                              hidTv[:, c, g, :, :].rearrange("p r c -> p (r c)"),
                              w2[:, 1, c, :], start=c == 0, stop=c == 1)
            last.then_inc(sem["vcmp_bank"], 1)
            pe_.wait_ge(sem["kcmp_ready"], 2)
            pe_.wait_ge(sem["vcmp_ready"], 2)
            for t in range(TT):
                for m in range(KT):
                    last = mm(psA[:, 2 * t + m // 4, (m % 4) * P:(m % 4 + 1) * P], qT[:, m, t * P:(t + 1) * P],
                              kcT.rearrange("p e g c -> p (e g c)"), start=True, stop=True)
            last.then_inc(sem["cmp_scores"], 1)

            pe_.wait_ge(sem["kT_act"], 4)
            pe_.wait_ge(sem["kT_dve"], 4)
            pe_.wait_ge(sem["identb_in"], 16)
            pe_.wait_ge(sem["mask_in"], 16)

            UNITS = [(g, t, m2) for g in range(KVH) for t in range(TT) for m2 in range(2)]

            def nsa_scores(u):
                g, t, m2 = UNITS[u]
                m, nk = 2 * g + m2, (t + 1) * P
                if u < 2:
                    pe_.wait_ge(sem["cmp_masked"], 8)
                else:
                    pe_.wait_ge(sem["smax"], u - 1)
                    pe_.wait_ge(sem["probs"], 4 * (u - 1))
                for e in range(2):
                    bank = psA[:, 2 * (u % 2) + e, :].rearrange("p (y k) -> p y k", y=2)
                    keys = keysT[:, e, g * 512:(g + 1) * 512].rearrange("p (y k) -> p y k", y=2)
                    mm(bank[:, :, 0:nk], qrT[:, m, t * P:(t + 1) * P], keys[:, :, 0:nk], start=True, stop=False)
                    for y in range(2):
                        last = mm(bank[:, y, t * P:nk], identb[:, :], cmask[:, :], start=False, stop=y == 1)
                last.then_inc(sem["scores"], 1)

            def nsa_transpose(u):
                g, t, m2 = UNITS[u]
                nb = t + 1
                pe_.wait_ge(sem["scaled_p"], 4 * (u + 1))
                if u >= 1:
                    pe_.wait_ge(sem["pT_act"], u)
                    pe_.wait_ge(sem["pT_dve"], u)
                for e in range(2):
                    for y in range(2):
                        for b in range(nb):
                            i = y * nb + b
                            last = pe_.transpose(psT[:, e, i * P:(i + 1) * P], probs[:, u % 2, e, y, b * P:(b + 1) * P], ident[:, :])
                last.then_inc(sem["pT_bank"], 1)

            def nsa_pv(w):
                g, t = w // TT, w % TT
                nb = t + 1
                pe_.wait_ge(sem["pT_act"], 2 * w + 2)
                pe_.wait_ge(sem["pT_dve"], 2 * w + 2)
                if w >= 2:
                    pe_.wait_ge(sem["oT_lo"], 2 * (w - 1))
                o = psO[:, w % 2, :]
                for y in range(2):
                    for b in range(nb):
                        mm(o, vals_nsa[:, b, y, g, :, :].rearrange("p u d -> p (u d)"),
                           pT[:, w % 2, y * nb + b, :, :].rearrange("p h q -> p (h q)"), start=y == 0 and b == 0, stop=False)
                for j in range(GROUP):
                    last = mm(o[:, j * P:(j + 1) * P], vcmp[:, 4 * g + j, :], cmp_pT[:, t, g // 2, :], start=False, stop=j == GROUP - 1)
                last.then_inc(sem["oT_bank"], 1)

            nsa_scores(0)
            nsa_scores(1)
            pe_.wait_ge(sem["cmp_p"], 1)
            for t in range(TT):
                for b in range(2):
                    last = pe_.transpose(psO[:, 0, (2 * t + b) * P:(2 * t + b + 1) * P],
                                         cmp_p[:, t, 8 * b:8 * b + 8, :].rearrange("p h c -> p (h c)"), ident[:, :])
            last.then_inc(sem["cmpT_bank"], 1)
            pe_.wait_ge(sem["cmpT_ready"], 1)
            for u in range(len(UNITS)):
                if u >= 1 and u + 1 < len(UNITS):
                    nsa_scores(u + 1)
                nsa_transpose(u)
                if u % 2 == 0 and u >= 2:
                    nsa_pv(u // 2 - 1)
            nsa_pv(len(UNITS) // 2 - 1)
            pe_.wait_ge(sem["oT_lo"], 2 * KVH * TT)
            pe_.wait_ge(sem["oT_hi"], 2 * KVH * TT)
            out_project(C_WO, hB_hi, hB_lo)

            def wait_scaled(n):
                def f(t):
                    pe_.wait_ge(sem["scaled"], TT * n)
                return f
            xT(1, xs, wait_scaled(1))
            ffn(0, C_F0)

            def wait_x1(t):
                pe_.wait_ge(sem["x_new"], 2 * TT)
            xT(2, x, wait_x1)
            for g in range(6):
                if g == 0:
                    pe_.wait_ge(sem["xT_hi"], 3 * KT)
                    pe_.wait_ge(sem["xT_lo"], 3 * KT)
                if g == 4:
                    pe_.wait_ge(sem["xT_hi"], 4 * KT)
                    pe_.wait_ge(sem["xT_lo"], 4 * KT)
                if g >= 2:
                    pe_.wait_ge(sem["proj_act"], NG + g - 1)
                    pe_.wait_ge(sem["proj_dve"], NG + g - 1)
                hh, hl = (hA_hi, hA_lo) if g < 4 else (hB_hi, hB_lo)
                project(C_KV + 2 * g, hh, hl, [psA[:, 2 * (g % 2) + t, :] for t in range(TT)], 512, 4)
                if g == 3:
                    pe_.wait_ge(sem["rope_done"], 4 + 2)
                    pe_.wait_ge(sem["xT_hi"], 4 * KT)
                    pe_.wait_ge(sem["xT_lo"], 4 * KT)
                    for i in range(4):
                        for mi in range(2):
                            for t in range(TT):
                                last = pe_.transpose(free_banks[i][:, (mi * TT + t) * P:(mi * TT + t + 1) * P],
                                                     tokA[:, t, 2 * (2 * i + mi):2 * (2 * i + mi) + 2, :].rearrange("p h d -> p (h d)"), ident[:, :])
                        last.then_inc(sem["dk_bank"], 1)
            pe_.wait_ge(sem["rope_done"], 4 + 4)
            for i in range(4):
                pe_.wait_ge(sem["dk_act"], i + 1)
                pe_.wait_ge(sem["dk_dve"], i + 1)
                for mi in range(2):
                    for t in range(TT):
                        last = pe_.transpose(free_banks[i][:, (mi * TT + t) * P:(mi * TT + t + 1) * P],
                                             tokB[:, t, 2 * (2 * i + mi):2 * (2 * i + mi) + 2, :].rearrange("p h d -> p (h d)"), ident[:, :])
                last.then_inc(sem["dq_bank"], 1)
            pe_.wait_ge(sem["dq_done"], 4)
            pe_.wait_ge(sem["proj_act"], NG + 6)
            pe_.wait_ge(sem["proj_dve"], NG + 6)

            def diff_scores(u):
                hp, t = u // TT, u % TT
                nk = (t + 1) * P
                if u >= 2:
                    pe_.wait_ge(sem["dsmax"], u - 1)
                    pe_.wait_ge(sem["dprobs"], 4 * (u - 1))
                for e in range(2):
                    h = 2 * hp + e
                    bank = psA[:, 2 * (u % 2) + e, :].rearrange("p (c k) -> p c k", c=2)
                    for c in range(2):
                        mm(bank[:, c, 0:nk], qrT[:, h, t * P:(t + 1) * P], keysT[:, c, h * S:h * S + nk], start=True, stop=False)
                        last = mm(bank[:, c, t * P:nk], identb[:, :], cmask[:, :], start=False, stop=True)
                last.then_inc(sem["dscores"], 1)

            def diff_transpose(u):
                hp, t = u // TT, u % TT
                pe_.wait_ge(sem["dmixed"], 2 * (u + 1))
                if u >= 2:
                    pe_.wait_ge(sem["dT_ready"], u - 1)
                for e in range(2):
                    for b in range(t + 1):
                        last = pe_.transpose(psT[:, u % 2, (e * 2 + b) * P:(e * 2 + b + 1) * P], probs[:, u % 2, e, 0, b * P:(b + 1) * P], ident[:, :])
                last.then_inc(sem["dT_bank"], 1)

            def diff_pv(u):
                hp, t = u // TT, u % TT
                pe_.wait_ge(sem["dT_ready"], u + 1)
                if u >= 2:
                    pe_.wait_ge(sem["do_ready"], u - 1)
                for e in range(2):
                    h = 2 * hp + e
                    for b in range(t + 1):
                        last = mm(psO[:, u % 2, e * DV:(e + 1) * DV], aT[:, u % 2, e, b, :], vals[:, b, h * DV:(h + 1) * DV],
                                  start=b == 0, stop=b == t)
                last.then_inc(sem["do_bank"], 1)

            ND = DH // 2 * TT
            diff_scores(0)
            for u in range(ND):
                if u + 1 < ND:
                    diff_scores(u + 1)
                if u >= 1:
                    diff_pv(u - 1)
                diff_transpose(u)
            diff_pv(ND - 1)
            pe_.wait_ge(sem["sub_scaled"], TT)
            for b in range(4):
                for kk in range(2):
                    for t in range(TT):
                        last = pe_.transpose(free_banks[b][:, (kk * TT + t) * P:(kk * TT + t + 1) * P], o_tok[:, t, 2 * b + kk, :], ident[:, :])
                last.then_inc(sem["oT2_bank"], 1)
            pe_.wait_ge(sem["oT_hi"], 2 * KVH * TT + 4)
            pe_.wait_ge(sem["oT_lo"], 2 * KVH * TT + 4)
            out_project(C_DO, hB_hi, hB_lo)

            xT(3, xs, wait_scaled(2))
            ffn(1, C_F1)

        @block.scalar
        def _(act):
            def split(s):
                n, w = stage_of(s), width_of(s)
                act.wait_ge(stage_full[n % 2], 16 * (n // 2 + 1))
                if s >= 2:
                    act.wait_ge(sem["in_used"], s - 1)
                for h in range(2):
                    cs = slice(h * w // 2, (h + 1) * w // 2)
                    act.activation(win_hi[:, s % 2, cs], stage[:, n % 2, cs], ACT.Copy).then_inc(sem["in_hi"], 1)

            def h_hi(dst, off, inst, lo_done=0):
                for k in range(KT):
                    if k % 2 == 0:
                        act.wait_ge(sem["xT_bank"], 4 * inst + k // 2 + 1)
                        if lo_done:
                            act.wait_ge(sem["xT_lo"], lo_done + k + 2)
                    act.activation(dst[:, k, :], free_banks[k // 2][:, (k % 2) * S:(k % 2 + 1) * S], ACT.Copy,
                                   scale=gain(off, k)).then_inc(sem["xT_hi"], 1)

            def norm(n, wait_x):
                for t in range(TT):
                    wait_x(t)
                    act.activation(squares[:, t, :], x[:, t, :], ACT.Square, accum_out=ssq[:, t:t + 1]).then_inc(sem["square"], 1)
                act.wait_ge(sem["mean_sq"], n + 1)
                act.activation(root, ms, ACT.Sqrt).then_inc(sem["root"], 1)

            def x_in(t):
                act.wait_ge(sem["x_in"], 16 * TT)

            def x_new(n):
                def f(t):
                    act.wait_ge(sem["x_new"], TT * n + t + 1)
                return f

            def ffn(layer, first):
                f0 = layer * NJ

                def split_in(j, b, h):
                    slot = (first + b) % 2
                    if h == 0:
                        act.wait_ge(stage_full[slot], 8 * j + (16 * (stage_of(first + b) // 2 + 1) - 8 * b))
                        act.wait_ge(sem["in_used"], j + (first - 1))
                    act.activation(win_hi[:, slot, h * W // 2:(h + 1) * W // 2], stage[:, slot, h * W // 2:(h + 1) * W // 2],
                                   ACT.Copy).then_inc(sem["in_hi"], 1)

                def split_out(j, b, wait=True):
                    slot = (first + b) % 2
                    if wait:
                        act.wait_ge(sem["out_used"], j + (f0 - 1))
                    act.activation(wout_hi[:, b, :], stage[:, slot, W:W + WO], ACT.Copy).then_inc(sem["out_hi"], 1)

                def step(j, b, nxt):
                    act.wait_ge(sem["u_bank"], j + (f0 + 1))
                    act.wait_ge(sem["conv_params"], j + (f0 + 1))
                    act.wait_ge(sem["prod"], j + f0) if not (isinstance(j, int) and j + f0 == 0) else None
                    for g in range(2):
                        if g == 1:
                            act.wait_ge(sem["in_used"], j + (first + 1))
                        act.activation(conv[:, b, g, :], (psT, psO)[g][:, b, 0:S], ACT.Identity,
                                       bias=prm[:, b, 4 * g + 3:4 * g + 4], scale=prm[:, b, 4 * g + 2:4 * g + 3]).then_inc(sem["conv0"], 1)
                    if nxt:
                        split_in(j + 1, 1 - b, 0)
                    act.wait_ge(sem["gate2"], j + (f0 + 1))
                    act.activation(silu[:, b, :], conv[:, b, 0, :], ACT.Silu).then_inc(sem["silu"], 1)
                    if nxt:
                        split_in(j + 1, 1 - b, 1)
                    act.wait_ge(sem["prod"], j + (f0 + 1))
                    if not (isinstance(j, int) and j + f0 < 2):
                        act.wait_ge(sem["out_used"], j + (f0 - 1))
                    act.activation(act_hi[:, b, :], prod[:, b, :], ACT.Copy).then_inc(sem["a_hi"], 1)
                    if nxt:
                        split_out(j + 1, 1 - b, not (isinstance(j, int) and j + 1 + f0 < 2))

                split_in(0, 0, 0)
                split_in(0, 0, 1)
                split_out(0, 0, layer > 0)
                h_hi(hA_hi, O_FG + layer * KT, 1 if layer == 0 else 3)
                step(0, 0, True)
                step(1, 1, True)
                with act.Fori(0, NJ // 2 - 2) as i:
                    for b in range(2):
                        step(2 * i + (2 + b), b, True)
                step(NJ - 2, 0, True)
                step(NJ - 1, 1, False)

            act.wait_ge(sem["params_in"], 16)
            h_hi(hA_hi, O_AG, 0)
            split(0)
            split(1)
            norm(0, x_in)
            for c in range(N_A):
                if c % 2:
                    g = c // 2
                    kind, width = GROUPS[g]
                    if g == 0:
                        act.wait_ge(sem["rstd"], 1)
                    act.wait_ge(sem["in_used"], c + 1)
                    for t in range(TT):
                        bank = psA[:, 2 * (g % 2) + t, :]
                        r = rstd[:, t:t + 1]
                        if kind == "cmp":
                            last = act.activation(kvc[:, t, :], bank, ACT.Copy, scale=r)
                        if kind == "q":
                            nh, h0 = Q_HEADS[g], Q_HEAD0[g]
                            if g == 3:
                                act.activation(gz[:, t, :], bank[:, nh * HD:width], ACT.Copy, scale=r).then_inc(sem["gate_z"], 1)
                            last = act.activation(tokA[:, t, h0:h0 + nh, :], bank[:, 0:nh * HD].rearrange("p (h d) -> p h d", d=HD),
                                                  ACT.Copy, scale=r)
                        if kind == "k":
                            last = act.activation(k_tok[:, t, :, :], bank.rearrange("p (h d) -> p h d", d=HD), ACT.Copy, scale=r)
                        if kind == "v" and t == 1:
                            last = act.activation(vals_nsa[:, t, :, :, :, :].rearrange("p y g u d -> p (y g) u d"),
                                                  bank.rearrange("p (h d) -> p h d", d=HD).unsqueeze(2).to_broadcast([P, 8, 2, HD]),
                                                  ACT.Copy, scale=r)
                    last.then_inc(sem["proj_act"], 1)
                    if g == 3:
                        act.wait_ge(sem["gate_z"], 2)
                        act.activation(gz, gz, ACT.Exp, scale=-1.0).then_inc(sem["gate_e"], 1)
                if c + 2 < N_A:
                    split(c + 2)
                if c == 3:
                    for v in range(2):
                        act.wait_ge(sem["pair_T"], v + 1)
                        for r in range(2):
                            act.activation(pairs[r * 64:r * 64 + 64, v, 0:KVH:2, :].rearrange("p h (t u) -> p h t u", t=TT),
                                           psT[0:64, v, :].rearrange("p (h t r u) -> p r h t u", h=2, t=TT, r=2)[:, r],
                                           ACT.Copy).then_inc(sem["pair_act"], 1)
                if c == 9:
                    for i in range(0, 8, 2):
                        act.wait_ge(sem["qT_bank"], i + 1)
                        act.activation(qT[:, i:i + 2, :].rearrange("p m q -> p (m q)"), free_banks[i % 4], ACT.Copy).then_inc(sem["qT_act"], 1)
            act.wait_ge(sem["zero"], 3)
            for pr in range(2):
                act.wait_ge(sem["kT_bank"], pr + 1)
                for e in range(2):
                    act.activation(keysT[e * 64:e * 64 + 64, e, 2 * pr * 512:(2 * pr + 1) * 512], psT[0:64, pr, :],
                                   ACT.Copy).then_inc(sem["kT_act"], 1)
            act.wait_ge(sem["hid_y"], 1)
            act.activation(hid_b, hid_a, ACT.Tanh, scale=math.sqrt(2 / math.pi)).then_inc(sem["hid_t"], 1)
            act.wait_ge(sem["hidT_bank"], 1)
            act.activation(hidT.rearrange("p t c -> p (t c)"), psA[:, 1, 0:128], ACT.Copy, scale=0.5).then_inc(sem["hidT_ready"], 1)
            act.activation(hidTv.rearrange("p t g r c -> p (t g) r c"),
                           psA[:, 1, 128:256].rearrange("p (x c) -> p x c", c=CP).unsqueeze(2).to_broadcast([P, 2 * KVH, 8, CP]),
                           ACT.Copy, scale=0.5).then_inc(sem["hidT_ready"], 1)
            act.wait_ge(sem["kcmp_bank"], 1)
            for e in range(2):
                act.activation(kcT[e * 64:e * 64 + 64, e, :, :].rearrange("p g c -> p (g c)"), psA[e * 64:e * 64 + 64, 2, 0:64],
                               ACT.Copy).then_inc(sem["kcmp_ready"], 1)
            split(C_WO)
            split(C_WO + 1)
            act.wait_ge(sem["cmp_shift"], 1)
            act.activation(cmp_p, cmp_s, ACT.Exp, scale=SCALE).then_inc(sem["cmp_exp"], 1)

            def exps(u, t, pre, waits_free):
                nk = (t + 1) * P
                act.wait_ge(sem[pre + "negmax"], u + 1)
                waits_free(u)
                for e in range(2):
                    for y in range(2):
                        act.activation(probs[:, u % 2, e, y, 0:nk], psA[:, 2 * (u % 2) + e, y * S:y * S + nk], ACT.Exp,
                                       bias=nmx[:, u, 2 * e + y:2 * e + y + 1], scale=SCALE,
                                       accum_out=den[:, u, 2 * e + y:2 * e + y + 1]).then_inc(sem[pre + "probs"], 1)

            def free_nsa(u):
                if u >= 2:
                    act.wait_ge(sem["pT_bank"], u - 1)

            NU = KVH * TT * 2

            def nsa_rest(u):
                g, t, m2 = u // 4, (u // 2) % 2, u % 2
                nb = t + 1
                act.wait_ge(sem["pT_bank"], u + 1)
                if u >= 4 and m2 == 0:
                    act.wait_ge(sem["oT_bank"], u // 2 - 1)
                act.activation(pT[:, (u // 2) % 2, 0:2 * nb, 2 * m2, :], psT[:, 0, 0:2 * nb * P].rearrange("p (i q) -> p i q", q=P),
                               ACT.Copy).then_inc(sem["pT_act"], 1)

            def oT_hi(w):
                g, t = w // TT, w % TT
                act.wait_ge(sem["oT_bank"], w + 1)
                for e in range(2):
                    act.activation(hB_hi[e * 64:e * 64 + 64, 2 * g:2 * g + 2, t * P:(t + 1) * P],
                                   psO[e * 64:e * 64 + 64, w % 2, :].rearrange("p (m e q) -> p e m q", m=2, e=2)[:, e],
                                   ACT.Copy).then_inc(sem["oT_hi"], 1)

            for u in range(NU):
                exps(u, (u // 2) % 2, "", free_nsa)
                if u == 0:
                    act.wait_ge(sem["cmpT_bank"], 1)
                    act.activation(cmp_pT.rearrange("p t b q -> p (t b q)"), psO[:, 0, :], ACT.Copy).then_inc(sem["cmpT_ready"], 1)
                if u >= 1:
                    nsa_rest(u - 1)
                if u >= 4 and u % 2 == 0:
                    oT_hi(u // 2 - 2)
            nsa_rest(NU - 1)
            oT_hi(NU // 2 - 2)
            oT_hi(NU // 2 - 1)
            split(C_WO + 2)
            split(C_WO + 3)

            norm(1, x_new(0))
            act.wait_ge(sem["rstd"], 2)
            act.activation(xs[:, 1, :], x[:, 1, :], ACT.Copy, scale=rstd[:, 1:2]).then_inc(sem["scaled"], 1)
            ffn(0, C_F0)

            split(C_KV)
            split(C_KV + 1)
            h_hi(hA_hi, O_KG, 2)
            h_hi(hB_hi, O_AG + KT, 2, 2 * KT)
            norm(2, x_new(1))
            act.wait_ge(sem["rstd"], 3)
            for c in range(12):
                g = c // 2
                if c % 2:
                    act.wait_ge(sem["in_used"], C_KV + c + 1)
                    for t in range(TT):
                        bank = psA[:, 2 * (g % 2) + t, :]
                        r = rstd[:, t:t + 1]
                        if g in (0, 1, 4, 5):
                            dst = tokA if g < 2 else tokB
                            last = act.activation(dst[:, t, 8 * (g % 2):8 * (g % 2) + 8, :], bank.rearrange("p (h d) -> p h d", d=HD),
                                                  ACT.Copy, scale=r)
                        elif t == 1:
                            last = act.activation(vals[:, t, (g - 2) * 512:(g - 1) * 512], bank, ACT.Copy, scale=r)
                    last.then_inc(sem["proj_act"], 1)
                if c == 7:
                    for i in range(4):
                        act.wait_ge(sem["dk_bank"], i + 1)
                        act.activation(keysT[0:64, 0, i * 512:(i + 1) * 512], free_banks[i][0:64, :], ACT.Copy).then_inc(sem["dk_act"], 1)
                split(C_KV + c + 2)
            for i in range(0, 4):
                act.wait_ge(sem["dq_bank"], i + 1)
                act.activation(qrT[:, 2 * i:2 * i + 2, :].rearrange("p m q -> p (m q)"), free_banks[i], ACT.Copy).then_inc(sem["dq_done"], 1)
            act.wait_ge(sem["lam_sum"], 2)
            act.activation(lame, lam2, ACT.Exp).then_inc(sem["lam_exp"], 1)

            def free_diff(u):
                if u >= 2:
                    act.wait_ge(sem["dT_bank"], u - 1)
            ND = DH // 2 * TT

            def head_squares(u):
                hp, t = u // TT, u % TT
                act.wait_ge(sem["do_ready"], u + 1)
                for e in range(2):
                    h = 2 * hp + e
                    act.activation(squares[:, 1, (2 * u + e) % 8 * P:((2 * u + e) % 8 + 1) * P], o_tok[:, t, h, :], ACT.Square,
                                   accum_out=sq_sub[:, t * DH + h:t * DH + h + 1]).then_inc(sem["do_sq"], 1)
            for u in range(ND):
                exps(u, u % TT, "d", free_diff)
                if u >= 2:
                    head_squares(u - 2)
            head_squares(ND - 2)
            head_squares(ND - 1)
            act.wait_ge(sem["sub_ms"], 1)
            act.activation(root_sub, ms_sub, ACT.Sqrt).then_inc(sem["sub_root"], 1)
            for b in range(4):
                act.wait_ge(sem["oT2_bank"], b + 1)
                act.activation(hB_hi[:, 2 * b:2 * b + 2, :].rearrange("p m q -> p (m q)"), free_banks[b], ACT.Copy,
                               scale=gain(O_SG, 0)).then_inc(sem["oT_hi"], 1)
            split(C_DO + 2)
            split(C_DO + 3)
            norm(3, x_new(2))
            act.wait_ge(sem["rstd"], 4)
            act.activation(xs[:, 1, :], x[:, 1, :], ACT.Copy, scale=rstd[:, 1:2]).then_inc(sem["scaled"], 1)
            ffn(1, C_F1)
            norm(4, x_new(3))

        @block.vector
        def _(dve):
            sub = ALU.subtract

            def split(s):
                n, w = stage_of(s), width_of(s)
                for h in range(2):
                    cs = slice(h * w // 2, (h + 1) * w // 2)
                    dve.wait_ge(sem["in_hi"], 2 * s + h + 1)
                    dve.tensor_tensor(win_lo[:, s % 2, cs], stage[:, n % 2, cs], win_hi[:, s % 2, cs].bitcast(F32), sub).then_inc(sem["in_lo"], 1)

            n_hi = [0]
            n_newton = [0]

            def h_lo(dst, src_hi, off, inst):
                for k in range(KT):
                    n_hi[0] += 1
                    dve.wait_ge(sem["xT_hi"], n_hi[0] + n_hi[0] % 2)
                    dve.scalar_tensor_tensor(dst[:, k, :], free_banks[k // 2][:, (k % 2) * S:(k % 2 + 1) * S], gain(off, k),
                                             src_hi[:, k, :].bitcast(F32), ALU.mult, sub).then_inc(sem["xT_lo"], 1)

            def norm(n):
                dve.wait_ge(sem["square"], TT * (n + 1))
                dve.tensor_scalar(ms, ssq, 1.0 / D, EPS, ALU.mult, ALU.add).then_inc(sem["mean_sq"], 1)
                refined_rsqrt(n, ms, root, rough, newton, rstd, "root", "rstd")
                dve.wait_ge(sem["rstd"], n + 1)

            def refined_rsqrt(n, m, root_, r0, t, out, root_sem, out_sem):
                dve.wait_ge(sem[root_sem], n + 1)
                dve.reciprocal(r0, root_).then_inc(sem["newton"], 1)
                n_newton[0] += 3
                dve.wait_ge(sem["newton"], n_newton[0] - 2)
                dve.scalar_tensor_tensor(t, r0, -0.5, r0, ALU.mult, ALU.mult).then_inc(sem["newton"], 1)
                dve.wait_ge(sem["newton"], n_newton[0] - 1)
                dve.tensor_tensor(t, t, m, ALU.mult).then_inc(sem["newton"], 1)
                dve.wait_ge(sem["newton"], n_newton[0])
                dve.scalar_tensor_tensor(out, t, 1.5, r0, ALU.add, ALU.mult).then_inc(sem[out_sem], 1)

            n_rope = [0]

            def rope(src, dst, nh):
                n_rope[0] += 1
                half = ROT // 2
                t1, t2 = rope_t[:, 0, :, 0:nh, :], rope_t[:, 1, :, 0:nh, :]
                c = cosv.unsqueeze(2).to_broadcast([P, TT, nh, ROT])
                dve.tensor_tensor(t1, src[:, :, :, 0:ROT], c, ALU.mult).then_inc(sem["rope_t1"], 1)
                for a in range(2):
                    sn = sinv[:, :, a * half:(a + 1) * half].unsqueeze(2).to_broadcast([P, TT, nh, half])
                    dve.tensor_tensor(t2[:, :, :, a * half:(a + 1) * half], src[:, :, :, (1 - a) * half:(2 - a) * half], sn,
                                      ALU.mult).then_inc(sem["rope_t2"], 1)
                dve.wait_ge(sem["rope_t1"], n_rope[0])
                dve.wait_ge(sem["rope_t2"], 2 * n_rope[0])
                dve.tensor_tensor(dst[:, :, :, 0:ROT], t1, t2, ALU.add).then_inc(sem["rope_done"], 1)
                dve.wait_ge(sem["rope_done"], n_rope[0])

            def add_y(done, count):
                dve.wait_ge(sem[done], count)
                for t in range(TT):
                    dve.tensor_tensor(x[:, t, :], psA[:, 2 * t:2 * t + 2, :].rearrange("p n c -> p (n c)"), x[:, t, :], ALU.add).then_inc(sem["x_new"], 1)

            def ffn(layer, first):
                f0 = layer * NJ

                def split_in(j, b, h):
                    slot = (first + b) % 2
                    dve.wait_ge(sem["in_hi"], 2 * j + (2 * first + h + 1))
                    cs = slice(h * W // 2, (h + 1) * W // 2)
                    dve.tensor_tensor(win_lo[:, slot, cs], stage[:, slot, cs], win_hi[:, slot, cs].bitcast(F32), sub).then_inc(sem["in_lo"], 1)

                def split_out(j, b):
                    slot = (first + b) % 2
                    dve.wait_ge(sem["out_hi"], j + (f0 + 1))
                    dve.tensor_tensor(wout_lo[:, b, :], stage[:, slot, W:W + WO], wout_hi[:, b, :].bitcast(F32), sub).then_inc(sem["out_lo"], 1)
                    dve.tensor_copy(prm[:, b, :], stage[:, slot, W + WO:FW]).then_inc(sem["conv_params"], 1)

                def tap(j, b, g, k, wait, done):
                    wait()
                    dve.scalar_tensor_tensor(conv[:, b, g, k:S], (psT, psO)[g][:, b, 0:S - k], prm[:, b, 4 * g + 2 - k:4 * g + 3 - k],
                                             conv[:, b, g, k:S], ALU.mult, ALU.add).then_inc(sem[done], 1)

                def step(j, b, nxt):
                    tap(j, b, 0, 1, lambda: dve.wait_ge(sem["conv0"], 2 * j + (2 * f0 + 1)), "gate1")
                    tap(j, b, 1, 1, lambda: dve.wait_ge(sem["conv0"], 2 * j + (2 * f0 + 2)), "val1")
                    tap(j, b, 0, 2, lambda: dve.wait_ge(sem["gate1"], j + (f0 + 1)), "gate2")
                    tap(j, b, 1, 2, lambda: dve.wait_ge(sem["val1"], j + (f0 + 1)), "val2")
                    if nxt:
                        split_in(j + 1, 1 - b, 0)
                    dve.wait_ge(sem["silu"], j + (f0 + 1))
                    dve.wait_ge(sem["val2"], j + (f0 + 1))
                    dve.tensor_tensor(prod[:, b, :], silu[:, b, :], conv[:, b, 1, :], ALU.mult).then_inc(sem["prod"], 1)
                    if nxt:
                        split_in(j + 1, 1 - b, 1)
                    dve.wait_ge(sem["a_hi"], j + (f0 + 1))
                    dve.tensor_tensor(act_lo[:, b, :], prod[:, b, :], act_hi[:, b, :].bitcast(F32), sub).then_inc(sem["a_lo"], 1)
                    if nxt:
                        split_out(j + 1, 1 - b)

                split_in(0, 0, 0)
                split_in(0, 0, 1)
                split_out(0, 0)
                h_lo(hA_lo, hA_hi, O_FG + layer * KT, 0)
                with dve.Fori(0, NJ // 2 - 1) as i:
                    for b in range(2):
                        step(2 * i + b, b, True)
                step(NJ - 2, 0, True)
                step(NJ - 1, 1, False)

            dve.memset(keysT[64:128, 0, :], 0.0).then_inc(sem["zero"], 1)
            dve.memset(keysT[0:64, 1, :], 0.0).then_inc(sem["zero"], 1)
            dve.wait_ge(sem["params_in"], 16)
            h_lo(hA_lo, hA_hi, O_AG, 0)
            split(0)
            norm(0)
            dve.memset(kcT, 0.0).then_inc(sem["zero"], 1)
            dve.memset(blocks[:, :, :, :, NCMP:CP], 0.0).then_inc(sem["zero"], 1)
            split(1)
            for c in range(N_A):
                g = c // 2
                kind, width = GROUPS[g]
                if c % 2:
                    dve.wait_ge(sem["in_used"], c + 1)
                    if kind == "q":
                        nh, h0 = Q_HEADS[g], Q_HEAD0[g]
                        dve.wait_ge(sem["proj_act"], g + 1)
                        for t in range(TT):
                            last = dve.tensor_copy(tokB[:, t, h0:h0 + nh, ROT:HD], tokA[:, t, h0:h0 + nh, ROT:HD])
                        last.then_inc(sem["proj_dve"], 1)
                        rope(tokA[:, :, h0:h0 + nh, :], tokB[:, :, h0:h0 + nh, :], nh)
                    elif kind == "k":
                        dve.wait_ge(sem["proj_act"], g + 1)
                        dve.sem_inc(sem["proj_dve"], 1)
                        rope(k_tok, k_tok, 8)
                    elif kind == "v":
                        dve.tensor_scalar(vals_nsa[:, 0, :, :, :, :].rearrange("p y g u d -> p (y g) u d"),
                                          psA[:, 2 * (g % 2), :].rearrange("p (h d) -> p h d", d=HD).unsqueeze(2).to_broadcast([P, 8, 2, HD]),
                                          rstd[:, 0:1], None, ALU.mult).then_inc(sem["proj_dve"], 1)
                    else:
                        dve.sem_inc(sem["proj_dve"], 1)
                if c + 2 < N_A:
                    split(c + 2)
                if c == 3:
                    for v in range(2):
                        dve.wait_ge(sem["pair_T"], v + 1)
                        for r in range(2):
                            dve.tensor_copy(pairs[r * 64:r * 64 + 64, v, 1:KVH:2, :].rearrange("p h (t u) -> p h t u", t=TT),
                                            psT[64:128, v, :].rearrange("p (h t r u) -> p r h t u", h=2, t=TT, r=2)[:, r]).then_inc(sem["pair_dve"], 1)
                    dve.wait_ge(sem["pair_act"], 4)
                    dve.wait_ge(sem["pair_dve"], 4)
                    for v in range(2):
                        for mh in range(2):
                            src = pairs[:, v, :, 8 * mh:8 * mh + 8 * NCMP].rearrange("p h (i m) -> p m h i", m=8)
                            for h in range(KVH):
                                last = dve.tensor_tensor(blocks[:, v, 8 * mh:8 * mh + 8, h, 0:NCMP], src[:, :, h, :],
                                                  pe[:, v, 8 * mh:8 * mh + 8].unsqueeze(2).to_broadcast([P, 8, NCMP]), ALU.add)
                            last.then_inc(sem["blocks_ready"], 1)
                if c == 7:
                    dve.wait_ge(sem["gate_e"], 1)
                    dve.tensor_scalar(gz, gz, 1.0, None, ALU.add).then_inc(sem["gate_e1"], 1)
                    dve.wait_ge(sem["gate_e1"], 1)
                    dve.reciprocal(gates[:, :, :, :].rearrange("p t h c -> p t (h c)"), gz).then_inc(sem["gates_ready"], 1)
                if c == 9:
                    for i in range(1, 8, 2):
                        dve.wait_ge(sem["qT_bank"], i + 1)
                        dve.tensor_copy(qrT[:, i - 1:i + 1, :].rearrange("p m q -> p (m q)"), free_banks[i % 4]).then_inc(sem["qT_dve"], 1)
            dve.wait_ge(sem["zero"], 4)
            for pr in range(2):
                dve.wait_ge(sem["kT_bank"], pr + 1)
                for e in range(2):
                    dve.tensor_copy(keysT[e * 64:e * 64 + 64, e, (2 * pr + 1) * 512:(2 * pr + 2) * 512], psT[64:128, pr, :]).then_inc(sem["kT_dve"], 1)
            lam_in = cols[:, O_LAM:O_COS].rearrange("p (a b d) -> p a b d", a=2, b=2)
            dve.tensor_tensor(rope_t[:, 0, :, 0:4, :].rearrange("p a h r -> p a (h r)"), lam_in[:, :, 0, :], lam_in[:, :, 1, :], ALU.mult).then_inc(sem["lam_prod"], 1)
            dve.wait_ge(sem["lam_prod"], 1)
            dve.tensor_reduce(lam2, rope_t[:, 0, :, 0:4, :].rearrange("p a h r -> p a (h r)"), AX.X, ALU.add).then_inc(sem["lam_sum"], 2)
            dve.wait_ge(sem["phi_used"], N_PHI)
            dve.tensor_tensor(hid, psA[0:64, 0, :].rearrange("p (v f) -> p v f", v=2), b1, ALU.add).then_inc(sem["hid_z"], 1)
            dve.wait_ge(sem["hid_z"], 1)
            dve.tensor_tensor(hid_a, hid, hid, ALU.mult).then_inc(sem["hid_z2"], 1)
            dve.wait_ge(sem["hid_z2"], 1)
            dve.tensor_scalar(hid_b, hid_a, 0.044715, 1.0, ALU.mult, ALU.add).then_inc(sem["hid_w"], 1)
            dve.wait_ge(sem["hid_w"], 1)
            dve.tensor_tensor(hid_a, hid_b, hid, ALU.mult).then_inc(sem["hid_y"], 1)
            dve.wait_ge(sem["hid_t"], 1)
            dve.scalar_tensor_tensor(hid, hid_b, 1.0, hid, ALU.add, ALU.mult).then_inc(sem["hid_ready"], 1)
            dve.wait_ge(sem["vcmp_bank"], 1)
            for b in range(2):
                dve.tensor_tensor(vcmp[:, 8 * b:8 * b + 8, :].rearrange("p (g j) d -> p g j d", g=2),
                                  psA[:, 3, 2 * b * P:(2 * b + 2) * P].rearrange("p (g d) -> p g d", g=2).unsqueeze(2).to_broadcast([P, 2, 4, P]),
                                  rowmask.rearrange("p (g j) -> p g j", g=2).unsqueeze(3).to_broadcast([P, 2, 4, P]),
                                  ALU.mult).then_inc(sem["vcmp_ready"], 1)
            dve.wait_ge(sem["cmp_scores"], 1)
            for t in range(TT):
                mk = cols[:, O_CM + t * CP:O_CM + (t + 1) * CP].unsqueeze(1).unsqueeze(1).to_broadcast([P, 2, 2, CP])
                for mq in range(2):
                    for a in range(2):
                        g = 2 * mq + a
                        src = psA[:, 2 * t + mq, a * 256:(a + 1) * 256].rearrange("p (m e g c) -> p g m e c", m=2, e=2, g=KVH)[:, g]
                        dst = cmp_s[:, t, 4 * g:4 * g + 4, :].rearrange("p (m e) c -> p m e c", e=2)
                        dve.tensor_tensor(dst, src, mk, ALU.add).then_inc(sem["cmp_masked"], 1)
            dve.wait_ge(sem["cmp_masked"], 8)
            dve.tensor_reduce(cmx, cmp_s, AX.X, ALU.max).then_inc(sem["cmp_max"], 1)
            dve.wait_ge(sem["cmp_max"], 1)
            bc = [P, TT, HEADS, CP]
            dve.tensor_tensor(cmp_s, cmp_s, cmx.unsqueeze(3).to_broadcast(bc), sub).then_inc(sem["cmp_shift"], 1)
            split(C_WO)
            split(C_WO + 1)

            def maxima(u, t, pre):
                nk = (t + 1) * P
                dve.wait_ge(sem[pre + "scores"], u + 1)
                dve.tensor_reduce(mx[:, u, :], psA[:, 2 * (u % 2):2 * (u % 2) + 2, :].rearrange("p e (y k) -> p (e y) k", y=2)[:, :, 0:nk],
                                  AX.X, ALU.max).then_inc(sem[pre + "smax"], 1)
                dve.wait_ge(sem[pre + "smax"], u + 1)
                dve.tensor_scalar(nmx[:, u, :], mx[:, u, :], -SCALE, None, ALU.mult).then_inc(sem[pre + "negmax"], 1)

            def reciprocals(u, pre):
                dve.wait_ge(sem[pre + "probs"], 4 * (u + 1))
                dve.reciprocal(rec[:, u, :], den[:, u, :]).then_inc(sem[pre + "recip"], 1)
                dve.wait_ge(sem[pre + "recip"], u + 1)

            NU = KVH * TT * 2
            maxima(0, 0, "")
            dve.wait_ge(sem["cmp_exp"], 1)
            dve.tensor_reduce(csum, cmp_p, AX.X, ALU.add).then_inc(sem["cmp_sum"], 1)
            dve.wait_ge(sem["cmp_sum"], 1)
            dve.reciprocal(crec, csum).then_inc(sem["cmp_recip"], 1)
            dve.wait_ge(sem["cmp_recip"], 1)
            dve.wait_ge(sem["gates_ready"], 1)
            dve.tensor_tensor(cfac, crec, gates[:, :, :, 0], ALU.mult).then_inc(sem["cmp_gate"], 1)
            dve.wait_ge(sem["cmp_gate"], 1)
            dve.tensor_tensor(cfac, cfac, cols[:, O_CV:O_CV + TT].unsqueeze(2).to_broadcast([P, TT, HEADS]), ALU.mult).then_inc(sem["cmp_valid"], 1)
            dve.wait_ge(sem["cmp_valid"], 1)
            dve.tensor_tensor(cmp_p, cmp_p, cfac.unsqueeze(3).to_broadcast(bc), ALU.mult).then_inc(sem["cmp_p"], 1)

            def oT_lo(w):
                g, t = w // TT, w % TT
                for e in range(2):
                    dve.wait_ge(sem["oT_hi"], 2 * w + e + 1)
                    dst = slice(e * 64, e * 64 + 64)
                    dve.tensor_tensor(hB_lo[dst, 2 * g:2 * g + 2, t * P:(t + 1) * P],
                                      psO[dst, w % 2, :].rearrange("p (m e q) -> p e m q", m=2, e=2)[:, e],
                                      hB_hi[dst, 2 * g:2 * g + 2, t * P:(t + 1) * P].bitcast(F32), sub).then_inc(sem["oT_lo"], 1)

            for u in range(NU):
                g, t, m2 = u // 4, (u // 2) % 2, u % 2
                nb, nk = t + 1, (t + 1) * P
                if u + 1 < NU:
                    maxima(u + 1, ((u + 1) // 2) % 2, "")
                reciprocals(u, "")
                h0 = 2 * (2 * g + m2)
                dve.tensor_tensor(fac[:, u, :].rearrange("p (e y) -> p e y", e=2), rec[:, u, :].rearrange("p (e y) -> p e y", e=2),
                                  gates[:, t, h0:h0 + 2, 1:3], ALU.mult).then_inc(sem["factor"], 1)
                dve.wait_ge(sem["factor"], u + 1)
                for e in range(2):
                    for y in range(2):
                        pr_ = probs[:, u % 2, e, y, 0:nk]
                        dve.tensor_scalar(pr_, pr_, fac[:, u, 2 * e + y:2 * e + y + 1], None, ALU.mult).then_inc(sem["scaled_p"], 1)
                if u >= 5 and u % 2 == 1:
                    oT_lo((u - 1) // 2 - 2)
                dve.wait_ge(sem["pT_bank"], u + 1)
                if u >= 4 and m2 == 0:
                    dve.wait_ge(sem["oT_bank"], u // 2 - 1)
                dve.tensor_copy(pT[:, (u // 2) % 2, 0:2 * nb, 2 * m2 + 1, :], psT[:, 1, 0:2 * nb * P].rearrange("p (i q) -> p i q", q=P)).then_inc(sem["pT_dve"], 1)
            oT_lo(NU // 2 - 2)
            oT_lo(NU // 2 - 1)
            split(C_WO + 2)
            split(C_WO + 3)

            add_y("in_used", C_WO + N_WO)
            norm(1)
            dve.tensor_scalar(xs[:, 0, :], x[:, 0, :], rstd[:, 0:1], None, ALU.mult).then_inc(sem["scaled"], 1)
            ffn(0, C_F0)

            add_y("out_used", NJ)
            split(C_KV)
            split(C_KV + 1)
            h_lo(hA_lo, hA_hi, O_KG, 2)
            h_lo(hB_lo, hB_hi, O_AG + KT, 2)
            norm(2)
            for c in range(12):
                g = c // 2
                if c % 2:
                    dve.wait_ge(sem["in_used"], C_KV + c + 1)
                    if g in (0, 1, 4, 5):
                        dst = tokA if g < 2 else tokB
                        dve.wait_ge(sem["proj_act"], NG + g + 1)
                        dve.sem_inc(sem["proj_dve"], 1)
                        v8 = dst[:, :, 8 * (g % 2):8 * (g % 2) + 8, :]
                        rope(v8, v8, 8)
                    else:
                        dve.tensor_scalar(vals[:, 0, (g - 2) * 512:(g - 1) * 512], psA[:, 2 * (g % 2), :], rstd[:, 0:1], None, ALU.mult).then_inc(sem["proj_dve"], 1)
                if c == 7:
                    for i in range(4):
                        dve.wait_ge(sem["dk_bank"], i + 1)
                        dve.tensor_copy(keysT[64:128, 1, i * 512:(i + 1) * 512], free_banks[i][64:128, :]).then_inc(sem["dk_dve"], 1)
                split(C_KV + c + 2)
            dve.wait_ge(sem["lam_exp"], 1)
            dve.tensor_tensor(neg_lam, lame[:, 1:2], lame[:, 0:1], sub).then_inc(sem["lam_diff"], 1)
            dve.wait_ge(sem["lam_diff"], 1)
            dve.tensor_scalar(neg_lam, neg_lam, -LAM_INIT, None, ALU.add).then_inc(sem["lam_ready"], 1)
            dve.wait_ge(sem["lam_ready"], 1)
            ND = DH // 2 * TT

            def out_heads(u):
                hp, t = u // TT, u % TT
                dve.wait_ge(sem["do_bank"], u + 1)
                dve.tensor_copy(o_tok[:, t, 2 * hp:2 * hp + 2, :], psO[:, u % 2, 0:2 * DV].rearrange("p (h d) -> p h d", h=2)).then_inc(sem["do_ready"], 1)

            maxima(0, 0, "d")
            for u in range(ND):
                hp, t = u // TT, u % TT
                nb, nk = t + 1, (t + 1) * P
                if u + 1 < ND:
                    maxima(u + 1, (u + 1) % TT, "d")
                reciprocals(u, "d")
                r2 = rec[:, u, :].rearrange("p (e c) -> p e c", e=2)
                dve.tensor_scalar(fac[:, u, 0:2], r2[:, :, 1], neg_lam, None, ALU.mult).then_inc(sem["dfactor"], 1)
                dve.wait_ge(sem["dfactor"], u + 1)
                for e in range(2):
                    p1 = probs[:, u % 2, e, 1, 0:nk]
                    dve.tensor_scalar(p1, p1, fac[:, u, e:e + 1], None, ALU.mult).then_inc(sem["dscaled"], 1)
                for e in range(2):
                    p0 = probs[:, u % 2, e, 0, 0:nk]
                    dve.wait_ge(sem["dscaled"], 2 * u + e + 1)
                    dve.scalar_tensor_tensor(p0, p0, rec[:, u, 2 * e:2 * e + 1], probs[:, u % 2, e, 1, 0:nk], ALU.mult, ALU.add).then_inc(sem["dmixed"], 1)
                if u >= 2:
                    out_heads(u - 2)
                dve.wait_ge(sem["dT_bank"], u + 1)
                if u >= 2:
                    dve.wait_ge(sem["do_bank"], u - 1)
                dve.tensor_copy(aT[:, u % 2, :, 0:nb, :], psT[:, u % 2, :].rearrange("p (e b q) -> p e b q", e=2, b=2)[:, :, 0:nb, :]).then_inc(sem["dT_ready"], 1)
            out_heads(ND - 2)
            out_heads(ND - 1)
            dve.wait_ge(sem["do_sq"], 2 * ND)
            dve.tensor_scalar(ms_sub, sq_sub, 1.0 / (DV * LAM_OUT ** 2), EPS / LAM_OUT ** 2, ALU.mult, ALU.add).then_inc(sem["sub_ms"], 1)
            refined_rsqrt(0, ms_sub, root_sub, rough_sub, newton_sub, rstd_sub, "sub_root", "sub_rstd")
            dve.wait_ge(sem["sub_rstd"], 1)
            dve.wait_ge(sem["do_ready"], ND)
            for t in range(TT):
                dve.tensor_tensor(o_tok[:, t, :, :], o_tok[:, t, :, :],
                                  rstd_sub[:, t * DH:(t + 1) * DH].unsqueeze(2).to_broadcast([P, DH, DV]), ALU.mult).then_inc(sem["sub_scaled"], 1)
            for b in range(4):
                dve.wait_ge(sem["oT_hi"], 2 * KVH * TT + b + 1)
                dve.scalar_tensor_tensor(hB_lo[:, 2 * b:2 * b + 2, :].rearrange("p m q -> p (m q)"), free_banks[b], gain(O_SG, 0),
                                         hB_hi[:, 2 * b:2 * b + 2, :].rearrange("p m q -> p (m q)").bitcast(F32), ALU.mult, sub).then_inc(sem["oT_lo"], 1)
            split(C_DO + 2)
            split(C_DO + 3)
            add_y("in_used", C_DO + N_DO)
            norm(3)
            dve.tensor_scalar(xs[:, 0, :], x[:, 0, :], rstd[:, 0:1], None, ALU.mult).then_inc(sem["scaled"], 1)
            ffn(1, C_F1)
            add_y("out_used", 2 * NJ)
            norm(4)
            dve.wait_ge(sem["final_in"], 16)
            for t in range(TT):
                dve.scalar_tensor_tensor(x[:, t, :], x[:, t, :], rstd[:, t:t + 1], final_g, ALU.mult, ALU.mult).then_inc(sem["out_ready"], 1)


def _layout(i):
    f = np.float32

    def ktiles(w, per):
        k, n = w.shape
        return np.ascontiguousarray(w.reshape(k // P // per, per, P, n).transpose(0, 2, 1, 3).reshape(-1, P, per * n))

    def col(v):
        return v.reshape(-1, P).T

    win = i["nsa_w_in"][0]
    q, kv, gt = win[:, :HEADS * HD], win[:, HEADS * HD:HEADS * HD + 6 * KV_W], win[:, HEADS * HD + 6 * KV_W:]
    kc, vc, ks, vs, kw, vw = (kv[:, n * KV_W:(n + 1) * KV_W] for n in range(6))
    groups = [np.concatenate([kc, vc], 1), q[:, :6 * HD], q[:, 6 * HD:11 * HD], np.concatenate([q[:, 11 * HD:], gt], 1),
              np.concatenate([ks, kw], 1), np.concatenate([vs, vw], 1)]
    arrays = {f"w_group{n}": ktiles(g, 4) for n, g in enumerate(groups)}
    arrays["x_tiles"] = i["x"].reshape(TT, P, D)
    arrays["w_phi"] = ktiles(i["nsa_phi_w1"][0].reshape(2 * CMP_BLOCK * HD, PHI), 8)
    arrays["w_nsa_out"] = ktiles(i["nsa_w_out"][0], 2)

    def column_groups(w):
        return np.concatenate([ktiles(w[:, n:n + 512], 4) for n in range(0, w.shape[1], 512)], 0)

    arrays["w_kv"] = column_groups(i["kv_w"])
    arrays["w_dq"] = column_groups(i["diff_w_q"][0])
    arrays["w_dout"] = ktiles(i["diff_w_out"][0], 2)
    pad = NJ * P - FFN
    fin = np.pad(i["ffn_w_in"].reshape(2, D, 2, FFN), ((0, 0), (0, 0), (0, 0), (0, pad)))
    fin = fin.reshape(2, KT, P, 2, NJ, P).transpose(0, 4, 2, 1, 3, 5).reshape(2, NJ, P, W)
    fout = np.pad(i["ffn_w_out"], ((0, 0), (0, pad), (0, 0))).reshape(2, NJ, P, D)
    taps = np.concatenate([i["ffn_conv_w"], i["ffn_conv_b"][:, None]], 1).reshape(2, 4, 2, FFN)
    taps = np.pad(taps, ((0, 0), (0, 0), (0, 0), (0, pad))).reshape(2, 4, 2, NJ, P).transpose(0, 3, 4, 2, 1).reshape(2, NJ, P, NPRM)
    arrays["w_ffn"] = np.ascontiguousarray(np.concatenate([fin, fout, taps], 3))
    pe = i["nsa_phi_pe"][0].reshape(2, CP, P).transpose(2, 0, 1).reshape(P, -1)
    w2 = i["nsa_phi_w2"][0].reshape(2, 2, P, 1, HD)
    w2 = np.broadcast_to(w2, (2, 2, P, 2, HD)).transpose(2, 0, 1, 3, 4).reshape(P, -1)
    rows = np.arange(P)
    rowmask = ((rows[:, None] // CP == np.arange(8)[None, :]) & (rows[:, None] % CP < NCMP)).astype(f)
    lam = np.broadcast_to(i["diff_lambda"][0].reshape(1, -1), (P, 4 * HD))
    inv = np.float32(500000.0) ** (-np.arange(ROT // 2, dtype=f) / f(ROT // 2))
    ang = np.arange(S, dtype=f)[:, None] * inv[None, :]
    cos, sin = np.cos(ang).astype(f), np.sin(ang).astype(f)

    def tok(v):
        return v.reshape(TT, P, -1).transpose(1, 0, 2).reshape(P, -1)

    pos = np.arange(S)
    visible = (np.arange(CP)[None, :] * CMP_STRIDE + CMP_BLOCK - 1 <= pos[:, None]) & (np.arange(CP)[None, :] < NCMP)
    cmp_mask = np.where(visible, 0.0, NEG).astype(f)
    cmp_any = visible.any(1, keepdims=True).astype(f)
    b1 = np.broadcast_to(i["nsa_phi_b1"][0].reshape(1, -1), (P, 2 * PHI))
    table = [col(i["attn_norm_g"][0]), col(i["attn_norm_g"][1]), col(i["ffn_norm_g"][0]), col(i["ffn_norm_g"][1]), col(i["kv_norm_g"]),
             i["diff_subln_g"][0][:, None], pe, w2, rowmask, lam, tok(np.concatenate([cos, cos], 1)), tok(np.concatenate([-sin, sin], 1)),
             tok(cmp_mask), tok(cmp_any), b1]
    arrays["param_cols"] = np.ascontiguousarray(np.concatenate(table, 1).astype(f))
    assert arrays["param_cols"].shape == (P, NCOL)
    arrays["ident"] = np.eye(P, dtype=f)
    arrays["final_g"] = np.ascontiguousarray(np.broadcast_to(i["final_norm_g"][None, :], (P, D)))
    return arrays


def kernel(**inputs):
    import ml_dtypes
    import concourse.bacc as bacc
    from concourse.bass_utils import run_bass_kernel_spmd

    arrays = _layout({k: np.asarray(v) for k, v in inputs.items()})
    arrays["identb"] = np.eye(P).astype(ml_dtypes.bfloat16)
    arrays["causal"] = np.where(np.arange(P)[None, :] <= np.arange(P)[:, None], 0.0, NEG).astype(ml_dtypes.bfloat16)
    nc = bacc.Bacc("TRN2", target_bir_lowering=False, num_devices=1)
    arrays = {f"in_{n}": a for n, a in arrays.items()}
    ap = {n[3:]: nc.dram_tensor(n, a.shape, mybir.dt.from_np(a.dtype), kind="ExternalInput").ap() for n, a in arrays.items()}
    out = nc.dram_tensor("out", (TT, P, D), F32, kind="ExternalOutput").ap()
    build(nc, ap["x_tiles"], ap["param_cols"], ap["ident"], ap["identb"], ap["causal"], [ap[f"w_group{g}"] for g in range(NG)],
          ap["w_phi"], ap["w_nsa_out"], ap["w_ffn"], ap["w_kv"], ap["w_dq"], ap["w_dout"], ap["final_g"], out)
    r = run_bass_kernel_spmd(nc, [arrays], core_ids=[0])
    return r.results[0]["out"].reshape(1, S, D)
```

```python
import math
from contextlib import ExitStack

import numpy as np

import concourse.bass as bass
from concourse import mybir

F32 = mybir.dt.float32
F32R = mybir.dt.float32r
BF16 = mybir.dt.bfloat16
I32 = mybir.dt.int32
ALU = mybir.AluOpType
ACT = mybir.ActivationFunctionType
AX = mybir.AxisListType

P = 128
D, S = 1024, 256
TT = S // P
KT = D // P
HEADS, KVH, GROUP, HD = 16, 4, 4, 64
CMP_BLOCK, CMP_STRIDE = 32, 16
NCMP = S // CMP_STRIDE - 1
CP = NCMP + 1
PHI = 256
DH, DV = 8, 128
ROT = HD // 4
FFN = 2752
NJ = -(-FFN // P)
LAM_INIT = 0.8 - 0.6 * math.exp(-0.3)
LAM_OUT = 1 - LAM_INIT
EPS = 1e-6
NEG = -1e30
SCALE = HD ** -0.5

KV_W = KVH * HD
GROUPS = [("cmp", 2 * KV_W), ("q", 6 * HD), ("q", 5 * HD), ("q", 5 * HD + 3 * HEADS), ("k", 2 * KV_W), ("v", 2 * KV_W)]
Q_HEAD0 = [0, 0, 6, 11]
Q_HEADS = [0, 6, 5, 5]
NG = len(GROUPS)

W = 2048
NPRM = 8
OW = D + NPRM

C_A, N_A = 0, 2 * NG
C_WO, N_WO = C_A + N_A, 4
C_F0 = C_WO + N_WO
C_KV, N_KV = C_F0 + NJ, 8
C_DQ, N_DQ = C_KV + N_KV, 4
C_DO, N_DO = C_DQ + N_DQ, 4
C_F1 = C_DO + N_DO
C_END = C_F1 + NJ
N_PHI = 4
O_AG, O_FG, O_KG, O_SG = 0, 2 * KT, 4 * KT, 5 * KT
O_PE = O_SG + 1
O_W2 = O_PE + 2 * CP
O_RM = O_W2 + 2 * 2 * P
O_LAM = O_RM + 8
O_COS = O_LAM + 4 * HD
O_SIN = O_COS + TT * ROT
O_CM = O_SIN + TT * ROT
O_CV = O_CM + TT * CP
O_B1 = O_CV + TT
NCOL = O_B1 + 2 * PHI


def width_of(s):
    return 4 * GROUPS[s // 2][1] if s < N_A else W


def stage_of(s):
    return s if s < C_WO else s + N_PHI


def is_ffn(s):
    return C_F0 <= s < C_KV or C_F1 <= s < C_END


def ffn_before(s):
    return max(0, min(s - C_F0, NJ)) + max(0, min(s - C_F1, NJ))


SEMS = """x_in params_in ident_in mask_in identb_in final_in stage0_full stage1_full stage_out0_full stage_out1_full phi_used
in_hi in_lo in_used out_hi out_lo out_used conv_params
newton xT_bank xT_hi xT_lo square mean_sq root rstd scaled_dve scaled_act y0_ready
proj proj_act proj_dve rope_ready rope_t1 rope_t2 rope_done gate_z gate_e gate_e1 gates_ready
pair_T pair_act pair_dve blocks_ready zero
qT_bank qT_act qT_dve kT_bank kT_act kT_dve
hid_pre hid_z hid_z2 hid_w hid_y hid_t hid_ready hidT_bank hidT_ready kcmp_bank kcmp_ready vcmp_bank vcmp_ready
cmp_scores cmp_masked cmp_max cmp_shift cmp_exp cmp_sum cmp_recip cmp_gate cmp_valid cmp_p cmpT_bank cmpT_ready
scores smax negmax probs recip factor scaled_p pT_bank pT_act pT_dve oT_bank oT_act oT_hi oT_lo
x_new u_bank conv0 gate1 val1 gate2 val2 silu prod a_hi a_lo
dk_bank dk_act dk_dve dq_bank dq_done dv_done
lam_prod lam_sum lam_exp lam_diff lam_ready
dscores dsmax dnegmax dprobs drecip dfactor dscaled dmixed dT_bank dT_ready do_bank do_sq do_ready
sub_ms sub_root sub_rstd sub_scaled oT2_bank
out_scaled out_ready stored""".split()


def build(nc, a_x, a_cols, a_ident, a_identb, a_mask, a_groups, a_phi, a_wo, a_ffn_in, a_ffn_out, a_kv, a_dq, a_do, a_final, a_out):
    with ExitStack() as ctx:
        def sb(name, shape, dt=F32):
            return ctx.enter_context(nc.sbuf_tensor(name, shape, dt))

        sem = {n: ctx.enter_context(nc.semaphore(n)) for n in SEMS}
        stage_full = [sem["stage0_full"], sem["stage1_full"]]
        stage_out_full = [sem["stage_out0_full"], sem["stage_out1_full"]]

        x = sb("x", [P, TT, D])
        cols = sb("cols", [P, NCOL])
        ident = sb("ident", [P, P])
        identb = sb("identb", [P, P], BF16)
        cmask = sb("cmask", [P, P], BF16)
        stage = sb("stage", [P, 2, W])
        stage_out = sb("stage_out", [P, 2, OW])
        win_hi = sb("win_hi", [P, 2, W], F32R)
        win_lo = sb("win_lo", [P, 2, W], F32R)
        wout_hi = sb("wout_hi", [P, 2, D], F32R)
        wout_lo = sb("wout_lo", [P, 2, D], F32R)
        hA_hi = sb("hA_hi", [P, KT, S], F32R)
        hA_lo = sb("hA_lo", [P, KT, S], F32R)
        hB_hi = sb("hB_hi", [P, KT, S], F32R)
        hB_lo = sb("hB_lo", [P, KT, S], F32R)
        act_hi = sb("act_hi", [P, 2, S], F32R)
        act_lo = sb("act_lo", [P, 2, S], F32R)
        prm = sb("prm", [P, 2, NPRM])
        keysT = sb("keysT", [P, 2, 2048])
        qT = sb("qT", [P, KT, S])
        qrT = sb("qrT", [P, KT, S])
        tokA = sb("tokA", [P, TT, 16, HD])
        tokB = sb("tokB", [P, TT, 16, HD])
        vals = sb("vals", [P, TT, 1024])
        arena = sb("arena", [P, 6144])
        stat = sb("stat", [P, 660])
        gates = sb("gates", [P, TT, HEADS, 3])
        rope_t = sb("rope_t", [P, 2, TT, 8, ROT])

        psA = ctx.enter_context(nc.psum_tensor("psA", [P, 4, 512], F32))
        psT = ctx.enter_context(nc.psum_tensor("psT", [P, 2, 512], F32))
        psO = ctx.enter_context(nc.psum_tensor("psO", [P, 2, 512], F32))
        free_banks = [psT[:, 0], psT[:, 1], psO[:, 0], psO[:, 1]]

        kvc = arena[:, 0:1024].rearrange("p (t c) -> p t c", t=TT)
        k_tok = arena[:, 1024:2048].rearrange("p (t h d) -> p t h d", t=TT, d=HD)
        pairs = arena[:, 2048:3072].rearrange("p (v h u) -> p v h u", v=2, h=KVH)
        blocks = arena[:, 3072:5120].rearrange("p (v m h i) -> p v m h i", v=2, m=CP, h=KVH)
        kcT = arena[:, 5120:5120 + 2 * KVH * CP].rearrange("p (e g c) -> p e g c", e=2, g=KVH)
        probs = arena[:, 0:2048].rearrange("p (s h t k) -> p s h t k", s=2, h=2, t=2)
        pT = arena[:, 2048:6144].rearrange("p (s t h q) -> p s t h q", s=2, t=4, h=4)
        aT = arena[:, 2048:3072].rearrange("p (s h b q) -> p s h b q", s=2, h=2, b=2)
        conv = arena[:, 0:1024].rearrange("p (s g q) -> p s g q", s=2, g=2)
        silu = arena[:, 1024:1536].rearrange("p (s q) -> p s q", s=2)
        prod = arena[:, 1536:2048].rearrange("p (s q) -> p s q", s=2)
        squares = arena[:, 2048:4096].rearrange("p (t c) -> p t c", t=TT)
        tokA_flat = tokA[:, :, :, :].rearrange("p t h d -> p (t h d)")
        tokB_flat = tokB[:, :, :, :].rearrange("p t h d -> p (t h d)")
        cmp_s = tokA_flat[:, 0:512].rearrange("p (t h c) -> p t h c", t=TT, h=HEADS)
        cmp_p = tokA_flat[:, 512:1024].rearrange("p (t h c) -> p t h c", t=TT, h=HEADS)
        cmp_pT = tokA_flat[:, 1024:1536].rearrange("p (t b q) -> p t b q", t=TT, b=2)
        hid = tokA_flat[:, 0:512].rearrange("p (v f) -> p v f", v=2)[0:64]
        hid_a = tokA_flat[:, 512:1024].rearrange("p (v f) -> p v f", v=2)[0:64]
        hid_b = tokA_flat[:, 1024:1536].rearrange("p (v f) -> p v f", v=2)[0:64]
        hidT = tokA_flat[:, 1536:1664].rearrange("p (t c) -> p t c", t=2)
        hidTv = tokA_flat[:, 512:1536].rearrange("p (t g r c) -> p t g r c", t=2, g=KVH, r=8)
        vcmp = tokB_flat.rearrange("p (h d) -> p h d", h=HEADS)
        xs = tokB_flat.rearrange("p (t c) -> p t c", t=TT)
        o_tok = tokB_flat.rearrange("p (t h d) -> p t h d", t=TT, h=DH)
        final_g = tokA_flat[:, 0:D]
        vals_nsa = vals[:, :, :].rearrange("p t (y g u d) -> p t y g u d", y=2, g=KVH, u=2)

        ssq = stat[:, 0:TT]
        ms = stat[:, 2:2 + TT]
        rstd = stat[:, 4:4 + TT]
        newton = stat[:, 610:610 + TT]
        mx = stat[:, 8:72].rearrange("p (u c) -> p u c", c=4)
        nmx = stat[:, 72:136].rearrange("p (u c) -> p u c", c=4)
        den = stat[:, 136:200].rearrange("p (u c) -> p u c", c=4)
        rec = stat[:, 200:264].rearrange("p (u c) -> p u c", c=4)
        fac = stat[:, 264:328].rearrange("p (u c) -> p u c", c=4)
        cmx = stat[:, 328:360].rearrange("p (t h) -> p t h", t=TT)
        csum = stat[:, 360:392].rearrange("p (t h) -> p t h", t=TT)
        crec = stat[:, 392:424].rearrange("p (t h) -> p t h", t=TT)
        cfac = stat[:, 424:456].rearrange("p (t h) -> p t h", t=TT)
        gz = stat[:, 456:552].rearrange("p (t c) -> p t c", t=TT)
        lam2 = stat[:, 552:554]
        lame = stat[:, 554:556]
        neg_lam = stat[:, 556:557]
        sq_sub = stat[:, 560:576]
        ms_sub = stat[:, 576:592]
        rstd_sub = stat[:, 592:608]
        newton_sub = stat[:, 628:644]

        cosv = cols[:, O_COS:O_SIN].rearrange("p (t r) -> p t r", t=TT)
        sinv = cols[:, O_SIN:O_CM].rearrange("p (t r) -> p t r", t=TT)
        pe = cols[:, O_PE:O_W2].rearrange("p (v m) -> p v m", v=2)
        w2 = cols[:, O_W2:O_RM].rearrange("p (v t d) -> p v t d", v=2, t=2)
        rowmask = cols[:, O_RM:O_LAM]
        b1 = cols[:, O_B1:NCOL].rearrange("p (v f) -> p v f", v=2)[0:64]

        def gain(off, k):
            return cols[:, off + k:off + k + 1]

        block = ctx.enter_context(nc.Block())

        @block.sync
        def _(sp):
            for t in range(TT):
                sp.dma_start(x[:, t, :], a_x[t]).then_inc(sem["x_in"], 16)
            sp.dma_start(ident[:, :], a_ident).then_inc(sem["ident_in"], 16)
            sp.dma_start(cols[:, :], a_cols).then_inc(sem["params_in"], 16)

            def load(n, dst, src, prev_s, prev_phi):
                if prev_s is not None:
                    sp.wait_ge(sem["in_lo"], prev_s + 1)
                if prev_phi is not None:
                    sp.wait_ge(sem["phi_used"], prev_phi + 1)
                sp.dma_start(dst, src).then_inc(stage_full[n % 2], 16)

            def load_main(s, src, width):
                n = stage_of(s)
                prev_phi = n - 2 - N_A if C_WO <= s < C_WO + 2 else None
                prev_s = s - 2 if s >= 2 and prev_phi is None else None
                load(n, stage[:, n % 2, 0:width], src, prev_s, prev_phi)

            for s in range(N_A):
                w4 = width_of(s)
                load_main(s, a_groups[s // 2][s % 2], w4)
                if s == 1:
                    sp.dma_start(identb[:, :], a_identb).then_inc(sem["identb_in"], 16)
                    sp.dma_start(cmask[:, :], a_mask).then_inc(sem["mask_in"], 16)
            for i in range(N_PHI):
                load(N_A + i, stage[:, i % 2, 0:W], a_phi[i], N_A - 2 + i if i < 2 else None, i - 2 if i >= 2 else None)
            for i in range(N_WO):
                load_main(C_WO + i, a_wo[i], W)

            ffn_in = a_ffn_in.rearrange("l j p c -> (l j) p c")
            ffn_out = a_ffn_out.rearrange("l j p c -> (l j) p c")

            def load_ffn(layer, first):
                f0 = layer * NJ
                for j in range(2):
                    load_main(first + j, a_ffn_in[layer, j], W)
                    if layer:
                        sp.wait_ge(sem["conv_params"], f0 + j - 1)
                    sp.dma_start(stage_out[:, j, :], a_ffn_out[layer, j]).then_inc(stage_out_full[j], 16)
                with sp.Fori(f0, f0 + NJ - 3, 2) as n:
                    for b in range(2):
                        sp.wait_ge(sem["in_lo"], n + (first - f0 + b + 1))
                        sp.dma_start(stage[:, b, :], ffn_in[2 + b:][n]).then_inc(stage_full[b], 16)
                        sp.wait_ge(sem["conv_params"], n + (b + 1))
                        sp.dma_start(stage_out[:, b, :], ffn_out[2 + b:][n]).then_inc(stage_out_full[b], 16)

            load_ffn(0, C_F0)
            for i in range(N_KV):
                load_main(C_KV + i, a_kv[i], W)
            for i in range(N_DQ):
                load_main(C_DQ + i, a_dq[i], W)
            for i in range(N_DO):
                load_main(C_DO + i, a_do[i], W)
            sp.wait_ge(sem["dk_bank"], 4)
            sp.dma_start(final_g, a_final).then_inc(sem["final_in"], 16)
            load_ffn(1, C_F1)
            for t in range(TT):
                sp.wait_ge(sem["out_ready"], t + 1)
                sp.dma_start(a_out[t], x[:, t, :]).then_inc(sem["stored"], 16)
            sp.wait_ge(sem["stored"], 16 * TT)

        @block.tensor
        def _(pe_):
            mm = pe_.matmul

            def three(out, xh, xl, wh, wl, start, stop):
                mm(out, xh, wh, start=start, stop=False)
                mm(out, xh, wl, start=False, stop=False)
                return mm(out, xl, wh, start=False, stop=stop)

            def wait_chunk(s):
                pe_.wait_ge(sem["in_hi"], 2 * (s + 1))
                pe_.wait_ge(sem["in_lo"], s + 1)

            def xT(inst, src, waits):
                for b in range(4):
                    waits(b)
                    for kk in range(2):
                        for t in range(TT):
                            k = 2 * b + kk
                            last = pe_.transpose(free_banks[b][:, (kk * TT + t) * P:(kk * TT + t + 1) * P],
                                                 src[:, t, k * P:(k + 1) * P], ident[:, :])
                    last.then_inc(sem["xT_bank"], 1)

            def project(s0, h_hi, h_lo, out, width, k_tiles, h_waits=None):
                for half in range(2):
                    wait_chunk(s0 + half)
                    slot = (s0 + half) % 2
                    wh = win_hi[:, slot, 0:k_tiles * width].rearrange("p (k c) -> p k c", k=k_tiles)
                    wl = win_lo[:, slot, 0:k_tiles * width].rearrange("p (k c) -> p k c", k=k_tiles)
                    for k in range(k_tiles):
                        kk = half * k_tiles + k
                        if h_waits is not None:
                            pe_.wait_ge(sem["xT_hi"], h_waits + kk + 1)
                            pe_.wait_ge(sem["xT_lo"], h_waits + kk + 1)
                        for t in range(TT):
                            last = three(out[t], h_hi[:, kk, t * P:(t + 1) * P], h_lo[:, kk, t * P:(t + 1) * P],
                                         wh[:, k, :], wl[:, k, :], kk == 0, kk == 2 * k_tiles - 1)
                    last.then_inc(sem["in_used"], 1)

            def out_project(s0, h_hi, h_lo, h_waits, per_chunk, between=None):
                for c in range(4):
                    pe_.wait_ge(sem["oT_hi"], h_waits + per_chunk * (c + 1))
                    pe_.wait_ge(sem["oT_lo"], h_waits + per_chunk * (c + 1))
                    wait_chunk(s0 + c)
                    slot = (s0 + c) % 2
                    for t in range(TT):
                        for k in range(2):
                            kk = 2 * c + k
                            for n in range(2):
                                cs = slice(k * D + n * 512, k * D + n * 512 + 512)
                                last = three(psA[:, 2 * t + n, :], h_hi[:, kk, t * P:(t + 1) * P], h_lo[:, kk, t * P:(t + 1) * P],
                                             win_hi[:, slot, cs], win_lo[:, slot, cs], kk == 0, kk == KT - 1)
                        if c == 3 and t == 0:
                            last.then_inc(sem["y0_ready"], 1)
                    last.then_inc(sem["in_used"], 1)
                    if between is not None:
                        between(c)

            def ffn(layer, first):
                f0 = layer * NJ

                def up(j, b, h_waits=None):
                    slot = (first + b) % 2
                    pe_.wait_ge(sem["in_hi"], 2 * j + 2 * (first + 1))
                    pe_.wait_ge(sem["in_lo"], j + (first + 1))
                    for g in range(2):
                        for k in range(KT):
                            if h_waits is not None and g == 0:
                                pe_.wait_ge(sem["xT_hi"], h_waits + max(k + 1, 2))
                                pe_.wait_ge(sem["xT_lo"], h_waits + max(k + 1, 2))
                            cs = slice(k * 2 * P + g * P, k * 2 * P + g * P + P)
                            o = (psT, psO)[g][:, b, 0:S]
                            mm(o, win_hi[:, slot, cs], hA_hi[:, k, :], start=k == 0, stop=False)
                            mm(o, win_hi[:, slot, cs], hA_lo[:, k, :], start=False, stop=False)
                            last = mm(o, win_lo[:, slot, cs], hA_hi[:, k, :], start=False, stop=k == KT - 1)
                        if g == 0:
                            last.then_inc(sem["u_bank"], 1)
                    last.then_inc(sem["in_used"], 1)

                def down(j, b, start, stop):
                    pe_.wait_ge(sem["a_lo"], j + (f0 + 1))
                    pe_.wait_ge(sem["out_lo"], j + (f0 + 1))
                    for t in range(TT):
                        for n in range(2):
                            last = three(psA[:, 2 * t + n, :], act_hi[:, b, t * P:(t + 1) * P], act_lo[:, b, t * P:(t + 1) * P],
                                         wout_hi[:, b, n * 512:(n + 1) * 512], wout_lo[:, b, n * 512:(n + 1) * 512], start, stop)
                        if stop and t == 0:
                            last.then_inc(sem["y0_ready"], 1)
                    last.then_inc(sem["out_used"], 1)

                up(0, 0, KT * (1 if layer == 0 else 4))
                up(1, 1)
                down(0, 0, True, False)
                with pe_.Fori(0, NJ // 2 - 1) as i:
                    for b in range(2):
                        pe_.wait_ge(sem["val2"], 2 * i + (f0 + b + 1))
                        pe_.wait_ge(sem["gate2"], 2 * i + (f0 + b + 1))
                        up(2 * i + (2 + b), b)
                        down(2 * i + (1 + b), 1 - b, False, False)
                down(NJ - 1, 1, False, True)

            pe_.wait_ge(sem["ident_in"], 16)

            def wait_x(b):
                if b == 0:
                    pe_.wait_ge(sem["x_in"], 16 * TT)
            xT(0, x, wait_x)
            for g, (kind, width) in enumerate(GROUPS):
                if g >= 2:
                    pe_.wait_ge(sem["proj_act"], g - 1)
                    pe_.wait_ge(sem["proj_dve"], g - 1)
                project(2 * g, hA_hi, hA_lo, [psA[:, 2 * (g % 2) + t, 0:width] for t in range(TT)], width, 4,
                        0 if g == 0 else None)
                if g == 1:
                    pe_.wait_ge(sem["proj_act"], 1)
                    perm = ident[:, :].rearrange("p (u r) -> p r u", r=2)
                    for v in range(2):
                        for pr in range(2):
                            for t in range(TT):
                                last = pe_.transpose(psT[:, v, (pr * TT + t) * P:(pr * TT + t + 1) * P],
                                                     kvc[:, t, v * KV_W + pr * P:v * KV_W + (pr + 1) * P], perm)
                        last.then_inc(sem["pair_T"], 1)
                if g == 4:
                    pe_.wait_ge(sem["proj_act"], 4)
                    pe_.wait_ge(sem["rope_done"], 3)
                    for i in range(8):
                        if i < 2:
                            pe_.wait_ge(sem["pair_act"], 4)
                            pe_.wait_ge(sem["pair_dve"], 4)
                        if i >= 4:
                            pe_.wait_ge(sem["qT_act"], i // 2 - 1)
                            pe_.wait_ge(sem["qT_dve"], i // 2 - 1)
                        src = tokB if i % 2 else tokA
                        for mi in range(2):
                            m = 2 * (i // 2) + mi
                            for t in range(TT):
                                last = pe_.transpose(free_banks[i % 4][:, (mi * TT + t) * P:(mi * TT + t + 1) * P],
                                                     src[:, t, 2 * m:2 * m + 2, :].rearrange("p h d -> p (h d)"), ident[:, :])
                        last.then_inc(sem["qT_bank"], 1)
            pe_.wait_ge(sem["rope_done"], 4)
            for pr in range(2):
                pe_.wait_ge(sem["qT_act"], 4)
                pe_.wait_ge(sem["qT_dve"], 4)
                for y in range(2):
                    for t in range(TT):
                        last = pe_.transpose(psT[:, pr, (y * TT + t) * P:(y * TT + t + 1) * P],
                                             k_tok[:, t, 4 * y + 2 * pr:4 * y + 2 * pr + 2, :].rearrange("p h d -> p (h d)"), ident[:, :])
                last.then_inc(sem["kT_bank"], 1)
            pe_.wait_ge(sem["blocks_ready"], 4)
            pe_.wait_ge(sem["proj_act"], NG)
            pe_.wait_ge(sem["proj_dve"], NG)
            for v in range(2):
                for half in range(2):
                    i = 2 * v + half
                    pe_.wait_ge(stage_full[i % 2], 16 * ((N_A + i) // 2 + 1))
                    for m in range(8):
                        mg = 8 * half + m
                        last = mm(psA[0:64, 0, v * PHI:(v + 1) * PHI], blocks[:, v, mg, :, :].rearrange("p h i -> p (h i)"),
                                  stage[:, i % 2, m * PHI:(m + 1) * PHI], start=mg == 0, stop=mg == CP - 1)
                    last.then_inc(sem["phi_used"], 1)
            pe_.wait_ge(sem["hid_ready"], 1)
            for v in range(2):
                for c in range(2):
                    last = pe_.transpose(psA[:, 1, (2 * v + c) * 64:(2 * v + c + 1) * 64], hid[:, v, c * P:(c + 1) * P], ident[0:64, 0:64])
            last.then_inc(sem["hidT_bank"], 1)
            pe_.wait_ge(sem["hidT_ready"], 1)
            for c in range(2):
                last = mm(psA[:, 2, 0:64], w2[:, 0, c, :], hidT[:, c, :], start=c == 0, stop=c == 1)
            last.then_inc(sem["kcmp_bank"], 1)
            pe_.wait_ge(sem["hidT_ready"], 2)
            for g in range(KVH):
                for c in range(2):
                    last = mm(psA[:, 3, g * P:(g + 1) * P],
                              hidTv[:, c, g, :, :].rearrange("p r c -> p (r c)"),
                              w2[:, 1, c, :], start=c == 0, stop=c == 1)
            last.then_inc(sem["vcmp_bank"], 1)
            pe_.wait_ge(sem["kcmp_ready"], 2)
            pe_.wait_ge(sem["vcmp_ready"], 2)
            for t in range(TT):
                for m in range(KT):
                    last = mm(psA[:, 2 * t + m // 4, (m % 4) * P:(m % 4 + 1) * P], qT[:, m, t * P:(t + 1) * P],
                              kcT.rearrange("p e g c -> p (e g c)"), start=True, stop=True)
            last.then_inc(sem["cmp_scores"], 1)

            pe_.wait_ge(sem["kT_act"], 4)
            pe_.wait_ge(sem["kT_dve"], 4)
            pe_.wait_ge(sem["identb_in"], 16)
            pe_.wait_ge(sem["mask_in"], 16)

            UNITS = [(g, t, m2) for g in range(KVH) for t in range(TT) for m2 in range(2)]

            def nsa_scores(u):
                g, t, m2 = UNITS[u]
                m, nk = 2 * g + m2, (t + 1) * P
                if u < 2:
                    pe_.wait_ge(sem["cmp_masked"], 8)
                else:
                    pe_.wait_ge(sem["smax"], u - 1)
                    pe_.wait_ge(sem["probs"], 4 * (u - 1))
                for e in range(2):
                    bank = psA[:, 2 * (u % 2) + e, :].rearrange("p (y k) -> p y k", y=2)
                    keys = keysT[:, e, g * 512:(g + 1) * 512].rearrange("p (y k) -> p y k", y=2)
                    mm(bank[:, :, 0:nk], qrT[:, m, t * P:(t + 1) * P], keys[:, :, 0:nk], start=True, stop=False)
                    for y in range(2):
                        last = mm(bank[:, y, t * P:nk], identb[:, :], cmask[:, :], start=False, stop=y == 1)
                last.then_inc(sem["scores"], 1)

            def nsa_transpose(u):
                g, t, m2 = UNITS[u]
                nb = t + 1
                pe_.wait_ge(sem["scaled_p"], 4 * (u + 1))
                if u >= 1:
                    pe_.wait_ge(sem["pT_act"], u)
                    pe_.wait_ge(sem["pT_dve"], u)
                for e in range(2):
                    for y in range(2):
                        for b in range(nb):
                            i = y * nb + b
                            last = pe_.transpose(psT[:, e, i * P:(i + 1) * P], probs[:, u % 2, e, y, b * P:(b + 1) * P], ident[:, :])
                last.then_inc(sem["pT_bank"], 1)

            def nsa_pv(w, y):
                g, t = w // TT, w % TT
                nb = t + 1
                if y == 0:
                    pe_.wait_ge(sem["pT_act"], 2 * w + 2)
                    pe_.wait_ge(sem["pT_dve"], 2 * w + 2)
                    if w >= 2:
                        pe_.wait_ge(sem["oT_lo"], 2 * (w - 1))
                o = psO[:, w % 2, :]
                for b in range(nb):
                    mm(o, vals_nsa[:, b, y, g, :, :].rearrange("p u d -> p (u d)"),
                       pT[:, w % 2, y * nb + b, :, :].rearrange("p h q -> p (h q)"), start=y == 0 and b == 0, stop=False)
                if y == 1:
                    for j in range(GROUP):
                        last = mm(o[:, j * P:(j + 1) * P], vcmp[:, 4 * g + j, :], cmp_pT[:, t, g // 2, :], start=False, stop=j == GROUP - 1)
                    last.then_inc(sem["oT_bank"], 1)

            nsa_scores(0)
            nsa_scores(1)
            pe_.wait_ge(sem["cmp_p"], 1)
            for t in range(TT):
                for b in range(2):
                    last = pe_.transpose(psO[:, 0, (2 * t + b) * P:(2 * t + b + 1) * P],
                                         cmp_p[:, t, 8 * b:8 * b + 8, :].rearrange("p h c -> p (h c)"), ident[:, :])
            last.then_inc(sem["cmpT_bank"], 1)
            pe_.wait_ge(sem["cmpT_ready"], 1)
            for u in range(len(UNITS)):
                nsa_transpose(u)
                if u + 2 < len(UNITS):
                    nsa_scores(u + 2)
                if u >= 2:
                    nsa_pv(u // 2 - 1, u % 2)
            for y in range(2):
                nsa_pv(len(UNITS) // 2 - 1, y)
            out_project(C_WO, hB_hi, hB_lo, 0, 2 * TT)

            def wait_scaled(n):
                def f(b):
                    pe_.wait_ge(sem["scaled_dve" if b < 2 else "scaled_act"], TT * n)
                return f
            xT(1, xs, wait_scaled(1))
            ffn(0, C_F0)

            def wait_x1(b):
                if b == 0:
                    pe_.wait_ge(sem["x_new"], 2 * TT)
            xT(2, x, wait_x1)
            for g in range(6):
                if g >= 2:
                    pe_.wait_ge(sem["proj_act"], NG + g - 1)
                    pe_.wait_ge(sem["proj_dve"], NG + g - 1)
                hh, hl = (hA_hi, hA_lo) if g < 4 else (hB_hi, hB_lo)
                project(C_KV + 2 * g, hh, hl, [psA[:, 2 * (g % 2) + t, :] for t in range(TT)], 512, 4,
                        {0: 2 * KT, 4: 3 * KT}.get(g))
                if g == 3:
                    pe_.wait_ge(sem["rope_done"], 4 + 2)
                    pe_.wait_ge(sem["xT_hi"], 4 * KT)
                    pe_.wait_ge(sem["xT_lo"], 4 * KT)
                    for i in range(4):
                        for mi in range(2):
                            for t in range(TT):
                                last = pe_.transpose(free_banks[i][:, (mi * TT + t) * P:(mi * TT + t + 1) * P],
                                                     tokA[:, t, 2 * (2 * i + mi):2 * (2 * i + mi) + 2, :].rearrange("p h d -> p (h d)"), ident[:, :])
                        last.then_inc(sem["dk_bank"], 1)
            pe_.wait_ge(sem["rope_done"], 4 + 4)
            for i in range(4):
                pe_.wait_ge(sem["dk_act"], i + 1)
                pe_.wait_ge(sem["dk_dve"], i + 1)
                for mi in range(2):
                    for t in range(TT):
                        last = pe_.transpose(free_banks[i][:, (mi * TT + t) * P:(mi * TT + t + 1) * P],
                                             tokB[:, t, 2 * (2 * i + mi):2 * (2 * i + mi) + 2, :].rearrange("p h d -> p (h d)"), ident[:, :])
                last.then_inc(sem["dq_bank"], 1)
            pe_.wait_ge(sem["dq_done"], 4)
            pe_.wait_ge(sem["proj_act"], NG + 6)
            pe_.wait_ge(sem["proj_dve"], NG + 6)

            def diff_scores(u):
                hp, t = u // TT, u % TT
                nk = (t + 1) * P
                if u >= 2:
                    pe_.wait_ge(sem["dsmax"], u - 1)
                    pe_.wait_ge(sem["dprobs"], 4 * (u - 1))
                for e in range(2):
                    h = 2 * hp + e
                    bank = psA[:, 2 * (u % 2) + e, :].rearrange("p (c k) -> p c k", c=2)
                    for c in range(2):
                        mm(bank[:, c, 0:nk], qrT[:, h, t * P:(t + 1) * P], keysT[:, c, h * S:h * S + nk], start=True, stop=False)
                        last = mm(bank[:, c, t * P:nk], identb[:, :], cmask[:, :], start=False, stop=True)
                last.then_inc(sem["dscores"], 1)

            def diff_transpose(u):
                hp, t = u // TT, u % TT
                pe_.wait_ge(sem["dmixed"], 2 * (u + 1))
                if u >= 2:
                    pe_.wait_ge(sem["dT_ready"], u - 1)
                for e in range(2):
                    for b in range(t + 1):
                        last = pe_.transpose(psT[:, u % 2, (e * 2 + b) * P:(e * 2 + b + 1) * P], probs[:, u % 2, e, 0, b * P:(b + 1) * P], ident[:, :])
                last.then_inc(sem["dT_bank"], 1)

            def diff_pv(u):
                hp, t = u // TT, u % TT
                pe_.wait_ge(sem["dT_ready"], u + 1)
                if u >= 2:
                    pe_.wait_ge(sem["do_ready"], u - 1)
                for e in range(2):
                    h = 2 * hp + e
                    for b in range(t + 1):
                        last = mm(psO[:, u % 2, e * DV:(e + 1) * DV], aT[:, u % 2, e, b, :], vals[:, b, h * DV:(h + 1) * DV],
                                  start=b == 0, stop=b == t)
                last.then_inc(sem["do_bank"], 1)

            ND = DH // 2 * TT
            diff_scores(0)
            diff_scores(1)
            for u in range(ND):
                diff_transpose(u)
                if u + 2 < ND:
                    diff_scores(u + 2)
                if u >= 1:
                    diff_pv(u - 1)
            diff_pv(ND - 1)
            def heads_T(b):
                pe_.wait_ge(sem["sub_scaled"], b + 1)
                for kk in range(2):
                    for t in range(TT):
                        last = pe_.transpose(free_banks[b][:, (kk * TT + t) * P:(kk * TT + t + 1) * P], o_tok[:, t, 2 * b + kk, :], ident[:, :])
                last.then_inc(sem["oT2_bank"], 1)

            def next_heads(c):
                if c < 2:
                    heads_T(c + 2)

            heads_T(0)
            heads_T(1)
            out_project(C_DO, hB_hi, hB_lo, 2 * KVH * TT, 1, next_heads)

            xT(3, xs, wait_scaled(2))
            ffn(1, C_F1)

        @block.scalar
        def _(act):
            def split(s):
                n, w = stage_of(s), width_of(s)
                act.wait_ge(stage_full[n % 2], 16 * (n // 2 + 1))
                if s >= 2:
                    act.wait_ge(sem["in_used"], s - 1)
                for h in range(2):
                    cs = slice(h * w // 2, (h + 1) * w // 2)
                    act.activation(win_hi[:, s % 2, cs], stage[:, n % 2, cs], ACT.Copy).then_inc(sem["in_hi"], 1)

            def h_hi(dst, off, inst, lo_done=0):
                for k in range(KT):
                    if k % 2 == 0:
                        act.wait_ge(sem["xT_bank"], 4 * inst + k // 2 + 1)
                        if lo_done:
                            act.wait_ge(sem["xT_lo"], lo_done + k + 2)
                    act.activation(dst[:, k, :], free_banks[k // 2][:, (k % 2) * S:(k % 2 + 1) * S], ACT.Copy,
                                   scale=gain(off, k)).then_inc(sem["xT_hi"], 1)

            def norm(n, wait_x):
                for t in range(TT):
                    wait_x(t)
                    act.activation(squares[:, t, :], x[:, t, :], ACT.Square, accum_out=ssq[:, t:t + 1]).then_inc(sem["square"], 1)

            def normalise(n, wait_x):
                norm(n, wait_x)
                act.wait_ge(sem["rstd"], n + 1)
                for t in range(TT):
                    act.activation(xs[:, t, D // 2:D], x[:, t, D // 2:D], ACT.Copy, scale=rstd[:, t:t + 1]).then_inc(sem["scaled_act"], 1)

            def x_in(t):
                act.wait_ge(sem["x_in"], 16 * TT)

            def x_new(n):
                def f(t):
                    act.wait_ge(sem["x_new"], TT * n + t + 1)
                return f

            def ffn(layer, first, normalise):
                f0 = layer * NJ

                def split_in(j, b, h):
                    slot = (first + b) % 2
                    if h == 0:
                        act.wait_ge(stage_full[slot], 8 * j + (16 * (stage_of(first + b) // 2 + 1) - 8 * b))
                        act.wait_ge(sem["in_used"], j + (first - 1))
                    act.activation(win_hi[:, slot, h * W // 2:(h + 1) * W // 2], stage[:, slot, h * W // 2:(h + 1) * W // 2],
                                   ACT.Copy).then_inc(sem["in_hi"], 1)

                def split_out(j, b, wait=True):
                    act.wait_ge(stage_out_full[b], 8 * j + (8 * f0 + 16 - 8 * b))
                    if wait:
                        act.wait_ge(sem["out_used"], j + (f0 - 1))
                    act.activation(wout_hi[:, b, :], stage_out[:, b, 0:D], ACT.Copy).then_inc(sem["out_hi"], 1)

                def step(j, b, split_next=True, split_wout=True, late=False):
                    act.wait_ge(sem["u_bank"], j + (f0 + 1))
                    act.wait_ge(sem["conv_params"], j + (f0 + 1))
                    act.wait_ge(sem["prod"], j + f0) if not (isinstance(j, int) and j + f0 == 0) else None
                    for g in range(2):
                        if g == 1:
                            act.wait_ge(sem["in_used"], j + (first + 1))
                        act.activation(conv[:, b, g, :], (psT, psO)[g][:, b, 0:S], ACT.Identity,
                                       bias=prm[:, b, 4 * g + 3:4 * g + 4], scale=prm[:, b, 4 * g + 2:4 * g + 3]).then_inc(sem["conv0"], 1)
                    if split_next and not late:
                        split_in(j + 2, b, 0)
                    act.wait_ge(sem["gate2"], j + (f0 + 1))
                    act.activation(silu[:, b, :], conv[:, b, 0, :], ACT.Silu).then_inc(sem["silu"], 1)
                    if split_next and not late:
                        split_in(j + 2, b, 1)
                    act.wait_ge(sem["prod"], j + (f0 + 1))
                    if not (isinstance(j, int) and j + f0 < 2):
                        act.wait_ge(sem["out_used"], j + (f0 - 1))
                    act.activation(act_hi[:, b, :], prod[:, b, :], ACT.Copy).then_inc(sem["a_hi"], 1)
                    if split_wout:
                        split_out(j + 1, 1 - b, not (isinstance(j, int) and j + 1 + f0 < 2))
                    if late:
                        split_in(j + 2, b, 0)
                        split_in(j + 2, b, 1)

                split_in(0, 0, 0)
                split_in(0, 0, 1)
                split_out(0, 0, layer > 0)
                normalise()
                h_hi(hA_hi, O_FG + layer * KT, 1 if layer == 0 else 3)
                split_in(1, 1, 0)
                split_in(1, 1, 1)
                step(0, 0)
                step(1, 1)
                with act.Fori(0, NJ // 2 - 2) as i:
                    for b in range(2):
                        step(2 * i + (2 + b), b)
                step(NJ - 2, 0, layer == 0)
                step(NJ - 1, 1, layer == 0, False, layer == 0)

            act.wait_ge(sem["params_in"], 16)
            h_hi(hA_hi, O_AG, 0)
            split(0)
            split(1)
            norm(0, x_in)
            for c in range(N_A):
                if c % 2:
                    g = c // 2
                    kind, width = GROUPS[g]
                    if g == 0:
                        act.wait_ge(sem["rstd"], 1)
                    act.wait_ge(sem["in_used"], c + 1)
                    for t in range(TT):
                        bank = psA[:, 2 * (g % 2) + t, :]
                        r = rstd[:, t:t + 1]
                        if kind == "cmp":
                            last = act.activation(kvc[:, t, :], bank, ACT.Copy, scale=r)
                        if kind == "q":
                            nh, h0 = Q_HEADS[g], Q_HEAD0[g]
                            if g == 3:
                                act.activation(gz[:, t, :], bank[:, nh * HD:width], ACT.Copy, scale=r).then_inc(sem["gate_z"], 1)
                            last = act.activation(tokA[:, t, h0:h0 + nh, :], bank[:, 0:nh * HD].rearrange("p (h d) -> p h d", d=HD),
                                                  ACT.Copy, scale=r)
                        if kind == "k":
                            last = act.activation(k_tok[:, t, :, :], bank.rearrange("p (h d) -> p h d", d=HD), ACT.Copy, scale=r)
                        if kind == "v" and t == 1:
                            last = act.activation(vals_nsa[:, t, :, :, :, :].rearrange("p y g u d -> p (y g) u d"),
                                                  bank.rearrange("p (h d) -> p h d", d=HD).unsqueeze(2).to_broadcast([P, 8, 2, HD]),
                                                  ACT.Copy, scale=r)
                    last.then_inc(sem["proj_act"], 1)
                    if g == 3:
                        act.wait_ge(sem["gate_z"], 2)
                        act.activation(gz, gz, ACT.Exp, scale=-1.0).then_inc(sem["gate_e"], 1)
                if c + 2 < N_A:
                    split(c + 2)
                if c == 3:
                    for v in range(2):
                        act.wait_ge(sem["pair_T"], v + 1)
                        for r in range(2):
                            act.activation(pairs[r * 64:r * 64 + 64, v, 0:KVH:2, :].rearrange("p h (t u) -> p h t u", t=TT),
                                           psT[0:64, v, :].rearrange("p (h t r u) -> p r h t u", h=2, t=TT, r=2)[:, r],
                                           ACT.Copy).then_inc(sem["pair_act"], 1)
                if c == 9:
                    for i in range(0, 8, 2):
                        act.wait_ge(sem["qT_bank"], i + 1)
                        act.activation(qT[:, i:i + 2, :].rearrange("p m q -> p (m q)"), free_banks[i % 4], ACT.Copy).then_inc(sem["qT_act"], 1)
            act.wait_ge(sem["zero"], 3)
            for pr in range(2):
                act.wait_ge(sem["kT_bank"], pr + 1)
                for e in range(2):
                    act.activation(keysT[e * 64:e * 64 + 64, e, 2 * pr * 512:(2 * pr + 1) * 512], psT[0:64, pr, :],
                                   ACT.Copy).then_inc(sem["kT_act"], 1)
            act.wait_ge(sem["hid_y"], 1)
            act.activation(hid_b, hid_a, ACT.Tanh, scale=math.sqrt(2 / math.pi)).then_inc(sem["hid_t"], 1)
            act.wait_ge(sem["hidT_bank"], 1)
            act.activation(hidT.rearrange("p t c -> p (t c)"), psA[:, 1, 0:128], ACT.Copy, scale=0.5).then_inc(sem["hidT_ready"], 1)
            act.activation(hidTv.rearrange("p t g r c -> p (t g) r c"),
                           psA[:, 1, 128:256].rearrange("p (x c) -> p x c", c=CP).unsqueeze(2).to_broadcast([P, 2 * KVH, 8, CP]),
                           ACT.Copy, scale=0.5).then_inc(sem["hidT_ready"], 1)
            act.wait_ge(sem["kcmp_bank"], 1)
            for e in range(2):
                act.activation(kcT[e * 64:e * 64 + 64, e, :, :].rearrange("p g c -> p (g c)"), psA[e * 64:e * 64 + 64, 2, 0:64],
                               ACT.Copy).then_inc(sem["kcmp_ready"], 1)
            split(C_WO)
            split(C_WO + 1)
            act.wait_ge(sem["cmp_shift"], 1)
            act.activation(cmp_p, cmp_s, ACT.Exp, scale=SCALE).then_inc(sem["cmp_exp"], 1)

            def exps(u, t, pre, waits_free):
                nk = (t + 1) * P
                act.wait_ge(sem[pre + "negmax"], u + 1)
                waits_free(u)
                for e in range(2):
                    for y in range(2):
                        act.activation(probs[:, u % 2, e, y, 0:nk], psA[:, 2 * (u % 2) + e, y * S:y * S + nk], ACT.Exp,
                                       bias=nmx[:, u, 2 * e + y:2 * e + y + 1], scale=SCALE,
                                       accum_out=den[:, u, 2 * e + y:2 * e + y + 1]).then_inc(sem[pre + "probs"], 1)

            def free_nsa(u):
                if u >= 2:
                    act.wait_ge(sem["pT_bank"], u - 1)

            NU = KVH * TT * 2

            def nsa_rest(u):
                g, t, m2 = u // 4, (u // 2) % 2, u % 2
                nb = t + 1
                act.wait_ge(sem["pT_bank"], u + 1)
                if u >= 4 and m2 == 0:
                    act.wait_ge(sem["oT_bank"], u // 2 - 1)
                act.activation(pT[:, (u // 2) % 2, 0:2 * nb, 2 * m2, :], psT[:, 0, 0:2 * nb * P].rearrange("p (i q) -> p i q", q=P),
                               ACT.Copy).then_inc(sem["pT_act"], 1)

            def oT_hi(w):
                g, t = w // TT, w % TT
                act.wait_ge(sem["oT_bank"], w + 1)
                for e in range(2):
                    act.activation(hB_hi[e * 64:e * 64 + 64, 2 * g:2 * g + 2, t * P:(t + 1) * P],
                                   psO[e * 64:e * 64 + 64, w % 2, :].rearrange("p (m e q) -> p e m q", m=2, e=2)[:, e],
                                   ACT.Copy).then_inc(sem["oT_hi"], 1)

            exps(0, 0, "", free_nsa)
            exps(1, 0, "", free_nsa)
            act.wait_ge(sem["cmpT_bank"], 1)
            act.activation(cmp_pT.rearrange("p t b q -> p (t b q)"), psO[:, 0, :], ACT.Copy).then_inc(sem["cmpT_ready"], 1)
            for u in range(NU):
                nsa_rest(u)
                if u + 2 < NU:
                    exps(u + 2, ((u + 2) // 2) % 2, "", free_nsa)
                if u >= 3 and u % 2 == 1:
                    oT_hi(u // 2 - 1)
            oT_hi(NU // 2 - 1)
            split(C_WO + 2)
            split(C_WO + 3)

            ffn(0, C_F0, lambda: normalise(1, x_new(0)))

            h_hi(hA_hi, O_KG, 2)
            norm(2, x_new(1))
            h_hi(hB_hi, O_AG + KT, 2, 2 * KT)
            act.wait_ge(sem["rstd"], 3)
            for c in range(12):
                g = c // 2
                if c % 2:
                    act.wait_ge(sem["in_used"], C_KV + c + 1)
                    for t in range(TT):
                        bank = psA[:, 2 * (g % 2) + t, :]
                        r = rstd[:, t:t + 1]
                        if g in (0, 1, 4, 5):
                            dst = tokA if g < 2 else tokB
                            last = act.activation(dst[:, t, 8 * (g % 2):8 * (g % 2) + 8, :], bank.rearrange("p (h d) -> p h d", d=HD),
                                                  ACT.Copy, scale=r)
                        elif t == 1:
                            last = act.activation(vals[:, t, (g - 2) * 512:(g - 1) * 512], bank, ACT.Copy, scale=r)
                    last.then_inc(sem["proj_act"], 1)
                if c == 7:
                    for i in range(4):
                        act.wait_ge(sem["dk_bank"], i + 1)
                        act.activation(keysT[0:64, 0, i * 512:(i + 1) * 512], free_banks[i][0:64, :], ACT.Copy).then_inc(sem["dk_act"], 1)
                split(C_KV + c + 2)
            for i in range(0, 4):
                act.wait_ge(sem["dq_bank"], i + 1)
                act.activation(qrT[:, 2 * i:2 * i + 2, :].rearrange("p m q -> p (m q)"), free_banks[i], ACT.Copy).then_inc(sem["dq_done"], 1)
            act.wait_ge(sem["lam_sum"], 2)
            act.activation(lame, lam2, ACT.Exp).then_inc(sem["lam_exp"], 1)

            def free_diff(u):
                if u >= 2:
                    act.wait_ge(sem["dT_bank"], u - 1)
            ND = DH // 2 * TT

            def head_squares(u):
                hp, t = u // TT, u % TT
                act.wait_ge(sem["do_ready"], u + 1)
                for e in range(2):
                    h = 2 * hp + e
                    act.activation(arena[:, 3072 + (2 * u + e) * P:3072 + (2 * u + e + 1) * P], o_tok[:, t, h, :], ACT.Square,
                                   accum_out=sq_sub[:, t * DH + h:t * DH + h + 1]).then_inc(sem["do_sq"], 1)
            exps(0, 0, "d", free_diff)
            exps(1, 1, "d", free_diff)
            for u in range(ND):
                if u + 2 < ND:
                    exps(u + 2, u % TT, "d", free_diff)
                if u >= 2:
                    head_squares(u - 2)
            head_squares(ND - 2)
            head_squares(ND - 1)
            for b in range(4):
                if b == 3:
                    split(C_DO + 2)
                act.wait_ge(sem["oT2_bank"], b + 1)
                act.activation(hB_hi[:, 2 * b:2 * b + 2, :].rearrange("p m q -> p (m q)"), free_banks[b], ACT.Copy,
                               scale=gain(O_SG, 0)).then_inc(sem["oT_hi"], 1)
            split(C_DO + 3)
            ffn(1, C_F1, lambda: normalise(3, x_new(2)))
            norm(4, x_new(3))

        @block.vector
        def _(dve):
            sub = ALU.subtract

            def split(s):
                n, w = stage_of(s), width_of(s)
                for h in range(2):
                    cs = slice(h * w // 2, (h + 1) * w // 2)
                    dve.wait_ge(sem["in_hi"], 2 * s + h + 1)
                    last = dve.tensor_tensor(win_lo[:, s % 2, cs], stage[:, n % 2, cs], win_hi[:, s % 2, cs].bitcast(F32), sub)
                last.then_inc(sem["in_lo"], 1)

            n_hi = [0]
            n_newton = [0]
            n_y = [0]

            def h_lo(dst, src_hi, off, inst):
                for k in range(KT):
                    n_hi[0] += 1
                    dve.wait_ge(sem["xT_hi"], n_hi[0] + n_hi[0] % 2)
                    dve.scalar_tensor_tensor(dst[:, k, :], free_banks[k // 2][:, (k % 2) * S:(k % 2 + 1) * S], gain(off, k),
                                             src_hi[:, k, :].bitcast(F32), ALU.mult, sub).then_inc(sem["xT_lo"], 1)

            def rsqrt(m, t, out, out_sem):
                def newton_done():
                    n_newton[0] += 1
                    dve.wait_ge(sem["newton"], n_newton[0])
                dve.tensor_scalar(out.bitcast(I32), m.bitcast(I32), -0.5, float(0x5F3759DF), ALU.mult, ALU.add).then_inc(sem["newton"], 1)
                for it in range(3):
                    newton_done()
                    dve.scalar_tensor_tensor(t, out, -0.5, out, ALU.mult, ALU.mult).then_inc(sem["newton"], 1)
                    newton_done()
                    dve.tensor_tensor(t, t, m, ALU.mult).then_inc(sem["newton"], 1)
                    newton_done()
                    dve.scalar_tensor_tensor(out, t, 1.5, out, ALU.add, ALU.mult).then_inc(sem["newton" if it < 2 else out_sem], 1)

            def norm(n):
                dve.wait_ge(sem["square"], TT * (n + 1))
                dve.tensor_scalar(ms, ssq, 1.0 / D, EPS, ALU.mult, ALU.add).then_inc(sem["mean_sq"], 1)
                dve.wait_ge(sem["mean_sq"], n + 1)
                rsqrt(ms, newton, rstd, "rstd")
                dve.wait_ge(sem["rstd"], n + 1)

            n_rope = [0]

            def rope(src, dst, nh):
                n_rope[0] += 1
                half = ROT // 2
                t1, t2 = rope_t[:, 0, :, 0:nh, :], rope_t[:, 1, :, 0:nh, :]
                c = cosv.unsqueeze(2).to_broadcast([P, TT, nh, ROT])
                dve.tensor_tensor(t1, src[:, :, :, 0:ROT], c, ALU.mult).then_inc(sem["rope_t1"], 1)
                for a in range(2):
                    sn = sinv[:, :, a * half:(a + 1) * half].unsqueeze(2).to_broadcast([P, TT, nh, half])
                    dve.tensor_tensor(t2[:, :, :, a * half:(a + 1) * half], src[:, :, :, (1 - a) * half:(2 - a) * half], sn,
                                      ALU.mult).then_inc(sem["rope_t2"], 1)
                dve.wait_ge(sem["rope_t1"], n_rope[0])
                dve.wait_ge(sem["rope_t2"], 2 * n_rope[0])
                dve.tensor_tensor(dst[:, :, :, 0:ROT], t1, t2, ALU.add).then_inc(sem["rope_done"], 1)
                dve.wait_ge(sem["rope_done"], n_rope[0])

            def add_y(done, count):
                n_y[0] += 1
                for t in range(TT):
                    if t == 0:
                        dve.wait_ge(sem["y0_ready"], n_y[0])
                    else:
                        dve.wait_ge(sem[done], count)
                    dve.tensor_tensor(x[:, t, :], psA[:, 2 * t:2 * t + 2, :].rearrange("p n c -> p (n c)"), x[:, t, :], ALU.add).then_inc(sem["x_new"], 1)

            def normalise(n, chunks):
                add_y("in_used", chunks)
                norm(n)
                for t in range(TT):
                    dve.tensor_scalar(xs[:, t, 0:D // 2], x[:, t, 0:D // 2], rstd[:, t:t + 1], None, ALU.mult).then_inc(sem["scaled_dve"], 1)

            def ffn(layer, first, normalise):
                f0 = layer * NJ

                def split_in(j, b, h):
                    slot = (first + b) % 2
                    dve.wait_ge(sem["in_hi"], 2 * j + (2 * first + h + 1))
                    cs = slice(h * W // 2, (h + 1) * W // 2)
                    last = dve.tensor_tensor(win_lo[:, slot, cs], stage[:, slot, cs], win_hi[:, slot, cs].bitcast(F32), sub)
                    if h == 1:
                        last.then_inc(sem["in_lo"], 1)

                def split_out(j, b):
                    dve.wait_ge(sem["out_hi"], j + (f0 + 1))
                    dve.tensor_tensor(wout_lo[:, b, :], stage_out[:, b, 0:D], wout_hi[:, b, :].bitcast(F32), sub).then_inc(sem["out_lo"], 1)
                    dve.tensor_copy(prm[:, b, :], stage_out[:, b, D:OW]).then_inc(sem["conv_params"], 1)

                def tap(j, b, g, k, wait, done):
                    wait()
                    dve.scalar_tensor_tensor(conv[:, b, g, k:S], (psT, psO)[g][:, b, 0:S - k], prm[:, b, 4 * g + 2 - k:4 * g + 3 - k],
                                             conv[:, b, g, k:S], ALU.mult, ALU.add).then_inc(sem[done], 1)

                def step(j, b, split_next=True, split_wout=True):
                    tap(j, b, 0, 1, lambda: dve.wait_ge(sem["conv0"], 2 * j + (2 * f0 + 1)), "gate1")
                    tap(j, b, 1, 1, lambda: dve.wait_ge(sem["conv0"], 2 * j + (2 * f0 + 2)), "val1")
                    tap(j, b, 0, 2, lambda: dve.wait_ge(sem["gate1"], j + (f0 + 1)), "gate2")
                    tap(j, b, 1, 2, lambda: dve.wait_ge(sem["val1"], j + (f0 + 1)), "val2")
                    if split_next:
                        split_in(j + 2, b, 0)
                    dve.wait_ge(sem["silu"], j + (f0 + 1))
                    dve.wait_ge(sem["val2"], j + (f0 + 1))
                    dve.tensor_tensor(prod[:, b, :], silu[:, b, :], conv[:, b, 1, :], ALU.mult).then_inc(sem["prod"], 1)
                    if split_next:
                        split_in(j + 2, b, 1)
                    dve.wait_ge(sem["a_hi"], j + (f0 + 1))
                    dve.tensor_tensor(act_lo[:, b, :], prod[:, b, :], act_hi[:, b, :].bitcast(F32), sub).then_inc(sem["a_lo"], 1)
                    if split_wout:
                        split_out(j + 1, 1 - b)

                split_in(0, 0, 0)
                split_in(0, 0, 1)
                normalise()
                h_lo(hA_lo, hA_hi, O_FG + layer * KT, 0)
                split_out(0, 0)
                split_in(1, 1, 0)
                split_in(1, 1, 1)
                with dve.Fori(0, NJ // 2 - 1) as i:
                    for b in range(2):
                        step(2 * i + b, b)
                step(NJ - 2, 0, layer == 0)
                step(NJ - 1, 1, False, False)

            dve.memset(keysT[64:128, 0, :], 0.0).then_inc(sem["zero"], 1)
            dve.memset(keysT[0:64, 1, :], 0.0).then_inc(sem["zero"], 1)
            dve.wait_ge(sem["params_in"], 16)
            h_lo(hA_lo, hA_hi, O_AG, 0)
            split(0)
            norm(0)
            dve.memset(kcT, 0.0).then_inc(sem["zero"], 1)
            dve.memset(blocks[:, :, :, :, NCMP:CP], 0.0).then_inc(sem["zero"], 1)
            split(1)
            for c in range(N_A):
                g = c // 2
                kind, width = GROUPS[g]
                if c % 2:
                    dve.wait_ge(sem["in_used"], c + 1)
                    if kind == "q":
                        nh, h0 = Q_HEADS[g], Q_HEAD0[g]
                        dve.wait_ge(sem["proj_act"], g + 1)
                        for t in range(TT):
                            last = dve.tensor_copy(tokB[:, t, h0:h0 + nh, ROT:HD], tokA[:, t, h0:h0 + nh, ROT:HD])
                        last.then_inc(sem["proj_dve"], 1)
                        rope(tokA[:, :, h0:h0 + nh, :], tokB[:, :, h0:h0 + nh, :], nh)
                    elif kind == "k":
                        dve.wait_ge(sem["proj_act"], g + 1)
                        dve.sem_inc(sem["proj_dve"], 1)
                        rope(k_tok, k_tok, 8)
                    elif kind == "v":
                        dve.tensor_scalar(vals_nsa[:, 0, :, :, :, :].rearrange("p y g u d -> p (y g) u d"),
                                          psA[:, 2 * (g % 2), :].rearrange("p (h d) -> p h d", d=HD).unsqueeze(2).to_broadcast([P, 8, 2, HD]),
                                          rstd[:, 0:1], None, ALU.mult).then_inc(sem["proj_dve"], 1)
                    else:
                        dve.sem_inc(sem["proj_dve"], 1)
                if c + 2 < N_A:
                    split(c + 2)
                if c == 3:
                    for v in range(2):
                        dve.wait_ge(sem["pair_T"], v + 1)
                        for r in range(2):
                            dve.tensor_copy(pairs[r * 64:r * 64 + 64, v, 1:KVH:2, :].rearrange("p h (t u) -> p h t u", t=TT),
                                            psT[64:128, v, :].rearrange("p (h t r u) -> p r h t u", h=2, t=TT, r=2)[:, r]).then_inc(sem["pair_dve"], 1)
                    dve.wait_ge(sem["pair_act"], 4)
                    dve.wait_ge(sem["pair_dve"], 4)
                    for v in range(2):
                        for mh in range(2):
                            src = pairs[:, v, :, 8 * mh:8 * mh + 8 * NCMP].rearrange("p h (i m) -> p m h i", m=8)
                            for h in range(KVH):
                                last = dve.tensor_tensor(blocks[:, v, 8 * mh:8 * mh + 8, h, 0:NCMP], src[:, :, h, :],
                                                  pe[:, v, 8 * mh:8 * mh + 8].unsqueeze(2).to_broadcast([P, 8, NCMP]), ALU.add)
                            last.then_inc(sem["blocks_ready"], 1)
                if c == 7:
                    dve.wait_ge(sem["gate_e"], 1)
                    dve.tensor_scalar(gz, gz, 1.0, None, ALU.add).then_inc(sem["gate_e1"], 1)
                    dve.wait_ge(sem["gate_e1"], 1)
                    dve.reciprocal(gates[:, :, :, :].rearrange("p t h c -> p t (h c)"), gz).then_inc(sem["gates_ready"], 1)
                if c == 9:
                    for i in range(1, 8, 2):
                        dve.wait_ge(sem["qT_bank"], i + 1)
                        dve.tensor_copy(qrT[:, i - 1:i + 1, :].rearrange("p m q -> p (m q)"), free_banks[i % 4]).then_inc(sem["qT_dve"], 1)
            dve.wait_ge(sem["zero"], 4)
            for pr in range(2):
                dve.wait_ge(sem["kT_bank"], pr + 1)
                for e in range(2):
                    dve.tensor_copy(keysT[e * 64:e * 64 + 64, e, (2 * pr + 1) * 512:(2 * pr + 2) * 512], psT[64:128, pr, :]).then_inc(sem["kT_dve"], 1)
            lam_in = cols[:, O_LAM:O_COS].rearrange("p (a b d) -> p a b d", a=2, b=2)
            dve.tensor_tensor(rope_t[:, 0, :, 0:4, :].rearrange("p a h r -> p a (h r)"), lam_in[:, :, 0, :], lam_in[:, :, 1, :], ALU.mult).then_inc(sem["lam_prod"], 1)
            dve.wait_ge(sem["lam_prod"], 1)
            dve.tensor_reduce(lam2, rope_t[:, 0, :, 0:4, :].rearrange("p a h r -> p a (h r)"), AX.X, ALU.add).then_inc(sem["lam_sum"], 2)
            dve.wait_ge(sem["phi_used"], N_PHI)
            dve.tensor_tensor(hid, psA[0:64, 0, :].rearrange("p (v f) -> p v f", v=2), b1, ALU.add).then_inc(sem["hid_z"], 1)
            dve.wait_ge(sem["hid_z"], 1)
            dve.tensor_tensor(hid_a, hid, hid, ALU.mult).then_inc(sem["hid_z2"], 1)
            dve.wait_ge(sem["hid_z2"], 1)
            dve.tensor_scalar(hid_b, hid_a, 0.044715, 1.0, ALU.mult, ALU.add).then_inc(sem["hid_w"], 1)
            dve.wait_ge(sem["hid_w"], 1)
            dve.tensor_tensor(hid_a, hid_b, hid, ALU.mult).then_inc(sem["hid_y"], 1)
            dve.wait_ge(sem["hid_t"], 1)
            dve.scalar_tensor_tensor(hid, hid_b, 1.0, hid, ALU.add, ALU.mult).then_inc(sem["hid_ready"], 1)
            dve.wait_ge(sem["vcmp_bank"], 1)
            for b in range(2):
                dve.tensor_tensor(vcmp[:, 8 * b:8 * b + 8, :].rearrange("p (g j) d -> p g j d", g=2),
                                  psA[:, 3, 2 * b * P:(2 * b + 2) * P].rearrange("p (g d) -> p g d", g=2).unsqueeze(2).to_broadcast([P, 2, 4, P]),
                                  rowmask.rearrange("p (g j) -> p g j", g=2).unsqueeze(3).to_broadcast([P, 2, 4, P]),
                                  ALU.mult).then_inc(sem["vcmp_ready"], 1)
            dve.wait_ge(sem["cmp_scores"], 1)
            for t in range(TT):
                mk = cols[:, O_CM + t * CP:O_CM + (t + 1) * CP].unsqueeze(1).unsqueeze(1).to_broadcast([P, 2, 2, CP])
                for mq in range(2):
                    for a in range(2):
                        g = 2 * mq + a
                        src = psA[:, 2 * t + mq, a * 256:(a + 1) * 256].rearrange("p (m e g c) -> p g m e c", m=2, e=2, g=KVH)[:, g]
                        dst = cmp_s[:, t, 4 * g:4 * g + 4, :].rearrange("p (m e) c -> p m e c", e=2)
                        dve.tensor_tensor(dst, src, mk, ALU.add).then_inc(sem["cmp_masked"], 1)
            dve.wait_ge(sem["cmp_masked"], 8)
            dve.tensor_reduce(cmx, cmp_s, AX.X, ALU.max).then_inc(sem["cmp_max"], 1)
            dve.wait_ge(sem["cmp_max"], 1)
            bc = [P, TT, HEADS, CP]
            dve.tensor_tensor(cmp_s, cmp_s, cmx.unsqueeze(3).to_broadcast(bc), sub).then_inc(sem["cmp_shift"], 1)
            split(C_WO)
            split(C_WO + 1)

            def maxima(u, t, pre):
                nk = (t + 1) * P
                dve.wait_ge(sem[pre + "scores"], u + 1)
                dve.tensor_reduce(mx[:, u, :], psA[:, 2 * (u % 2):2 * (u % 2) + 2, :].rearrange("p e (y k) -> p (e y) k", y=2)[:, :, 0:nk],
                                  AX.X, ALU.max).then_inc(sem[pre + "smax"], 1)
                dve.wait_ge(sem[pre + "smax"], u + 1)
                dve.tensor_scalar(nmx[:, u, :], mx[:, u, :], -SCALE, None, ALU.mult).then_inc(sem[pre + "negmax"], 1)

            def reciprocals(u, pre):
                dve.wait_ge(sem[pre + "probs"], 4 * (u + 1))
                dve.reciprocal(rec[:, u, :], den[:, u, :]).then_inc(sem[pre + "recip"], 1)
                dve.wait_ge(sem[pre + "recip"], u + 1)

            NU = KVH * TT * 2
            maxima(0, 0, "")
            dve.wait_ge(sem["cmp_exp"], 1)
            dve.tensor_reduce(csum, cmp_p, AX.X, ALU.add).then_inc(sem["cmp_sum"], 1)
            dve.wait_ge(sem["cmp_sum"], 1)
            dve.reciprocal(crec, csum).then_inc(sem["cmp_recip"], 1)
            dve.wait_ge(sem["cmp_recip"], 1)
            dve.wait_ge(sem["gates_ready"], 1)
            dve.tensor_tensor(cfac, crec, gates[:, :, :, 0], ALU.mult).then_inc(sem["cmp_gate"], 1)
            dve.wait_ge(sem["cmp_gate"], 1)
            dve.tensor_tensor(cfac, cfac, cols[:, O_CV:O_CV + TT].unsqueeze(2).to_broadcast([P, TT, HEADS]), ALU.mult).then_inc(sem["cmp_valid"], 1)
            dve.wait_ge(sem["cmp_valid"], 1)
            dve.tensor_tensor(cmp_p, cmp_p, cfac.unsqueeze(3).to_broadcast(bc), ALU.mult).then_inc(sem["cmp_p"], 1)

            def oT_lo(w):
                g, t = w // TT, w % TT
                for e in range(2):
                    dve.wait_ge(sem["oT_hi"], 2 * w + e + 1)
                    dst = slice(e * 64, e * 64 + 64)
                    dve.tensor_tensor(hB_lo[dst, 2 * g:2 * g + 2, t * P:(t + 1) * P],
                                      psO[dst, w % 2, :].rearrange("p (m e q) -> p e m q", m=2, e=2)[:, e],
                                      hB_hi[dst, 2 * g:2 * g + 2, t * P:(t + 1) * P].bitcast(F32), sub).then_inc(sem["oT_lo"], 1)

            def scale_probs(u):
                g, t, m2 = u // 4, (u // 2) % 2, u % 2
                reciprocals(u, "")
                h0 = 2 * (2 * g + m2)
                dve.tensor_tensor(fac[:, u, :].rearrange("p (e y) -> p e y", e=2), rec[:, u, :].rearrange("p (e y) -> p e y", e=2),
                                  gates[:, t, h0:h0 + 2, 1:3], ALU.mult).then_inc(sem["factor"], 1)
                dve.wait_ge(sem["factor"], u + 1)
                for e in range(2):
                    for y in range(2):
                        pr_ = probs[:, u % 2, e, y, 0:(t + 1) * P]
                        dve.tensor_scalar(pr_, pr_, fac[:, u, 2 * e + y:2 * e + y + 1], None, ALU.mult).then_inc(sem["scaled_p"], 1)

            maxima(1, 0, "")
            scale_probs(0)
            for u in range(NU):
                g, t, m2 = u // 4, (u // 2) % 2, u % 2
                nb = t + 1
                dve.wait_ge(sem["pT_bank"], u + 1)
                if u >= 4 and m2 == 0:
                    dve.wait_ge(sem["oT_bank"], u // 2 - 1)
                dve.tensor_copy(pT[:, (u // 2) % 2, 0:2 * nb, 2 * m2 + 1, :], psT[:, 1, 0:2 * nb * P].rearrange("p (i q) -> p i q", q=P)).then_inc(sem["pT_dve"], 1)
                if u >= 4 and u % 2 == 0:
                    oT_lo(u // 2 - 2)
                if u + 1 < NU:
                    scale_probs(u + 1)
                if u + 2 < NU:
                    maxima(u + 2, ((u + 2) // 2) % 2, "")
            oT_lo(NU // 2 - 2)
            oT_lo(NU // 2 - 1)
            split(C_WO + 2)
            split(C_WO + 3)

            ffn(0, C_F0, lambda: normalise(1, C_WO + N_WO))

            add_y("out_used", NJ)
            h_lo(hA_lo, hA_hi, O_KG, 2)
            split(C_KV + 1)
            norm(2)
            h_lo(hB_lo, hB_hi, O_AG + KT, 2)
            for c in range(12):
                g = c // 2
                if c % 2:
                    dve.wait_ge(sem["in_used"], C_KV + c + 1)
                    if g in (0, 1, 4, 5):
                        dst = tokA if g < 2 else tokB
                        dve.wait_ge(sem["proj_act"], NG + g + 1)
                        dve.sem_inc(sem["proj_dve"], 1)
                        v8 = dst[:, :, 8 * (g % 2):8 * (g % 2) + 8, :]
                        rope(v8, v8, 8)
                    else:
                        dve.tensor_scalar(vals[:, 0, (g - 2) * 512:(g - 1) * 512], psA[:, 2 * (g % 2), :], rstd[:, 0:1], None, ALU.mult).then_inc(sem["proj_dve"], 1)
                if c == 7:
                    for i in range(4):
                        dve.wait_ge(sem["dk_bank"], i + 1)
                        dve.tensor_copy(keysT[64:128, 1, i * 512:(i + 1) * 512], free_banks[i][64:128, :]).then_inc(sem["dk_dve"], 1)
                split(C_KV + c + 2)
            dve.wait_ge(sem["lam_exp"], 1)
            dve.tensor_tensor(neg_lam, lame[:, 1:2], lame[:, 0:1], sub).then_inc(sem["lam_diff"], 1)
            dve.wait_ge(sem["lam_diff"], 1)
            dve.tensor_scalar(neg_lam, neg_lam, -LAM_INIT, None, ALU.add).then_inc(sem["lam_ready"], 1)
            dve.wait_ge(sem["lam_ready"], 1)
            ND = DH // 2 * TT

            def out_heads(u):
                hp, t = u // TT, u % TT
                dve.wait_ge(sem["do_bank"], u + 1)
                dve.tensor_copy(o_tok[:, t, 2 * hp:2 * hp + 2, :], psO[:, u % 2, 0:2 * DV].rearrange("p (h d) -> p h d", h=2)).then_inc(sem["do_ready"], 1)

            def mix_probs(u):
                nk = (u % TT + 1) * P
                reciprocals(u, "d")
                r2 = rec[:, u, :].rearrange("p (e c) -> p e c", e=2)
                dve.tensor_scalar(fac[:, u, 0:2], r2[:, :, 1], neg_lam, None, ALU.mult).then_inc(sem["dfactor"], 1)
                dve.wait_ge(sem["dfactor"], u + 1)
                for e in range(2):
                    p1 = probs[:, u % 2, e, 1, 0:nk]
                    dve.tensor_scalar(p1, p1, fac[:, u, e:e + 1], None, ALU.mult).then_inc(sem["dscaled"], 1)
                for e in range(2):
                    p0 = probs[:, u % 2, e, 0, 0:nk]
                    dve.wait_ge(sem["dscaled"], 2 * u + e + 1)
                    dve.scalar_tensor_tensor(p0, p0, rec[:, u, 2 * e:2 * e + 1], probs[:, u % 2, e, 1, 0:nk], ALU.mult, ALU.add).then_inc(sem["dmixed"], 1)

            maxima(0, 0, "d")
            maxima(1, 1, "d")
            mix_probs(0)
            for u in range(ND):
                nb = u % TT + 1
                dve.wait_ge(sem["dT_bank"], u + 1)
                if u >= 2:
                    dve.wait_ge(sem["do_bank"], u - 1)
                dve.tensor_copy(aT[:, u % 2, :, 0:nb, :], psT[:, u % 2, :].rearrange("p (e b q) -> p e b q", e=2, b=2)[:, :, 0:nb, :]).then_inc(sem["dT_ready"], 1)
                if u >= 2:
                    out_heads(u - 2)
                if u + 1 < ND:
                    mix_probs(u + 1)
                if u + 2 < ND:
                    maxima(u + 2, u % TT, "d")
            out_heads(ND - 2)
            out_heads(ND - 1)
            dve.wait_ge(sem["do_sq"], 2 * ND)
            dve.tensor_scalar(ms_sub, sq_sub, 1.0 / (DV * LAM_OUT ** 2), EPS / LAM_OUT ** 2, ALU.mult, ALU.add).then_inc(sem["sub_ms"], 1)
            dve.wait_ge(sem["sub_ms"], 1)
            rsqrt(ms_sub, newton_sub, rstd_sub, "sub_rstd")
            dve.wait_ge(sem["sub_rstd"], 1)
            dve.wait_ge(sem["do_ready"], ND)
            r_sub = rstd_sub.rearrange("p (t h) -> p t h", t=TT)

            def scale_heads(b):
                hs = slice(2 * b, 2 * b + 2)
                dve.tensor_tensor(o_tok[:, :, hs, :], o_tok[:, :, hs, :], r_sub[:, :, hs].unsqueeze(3).to_broadcast([P, TT, 2, DV]),
                                  ALU.mult).then_inc(sem["sub_scaled"], 1)

            def heads_lo(b):
                dve.wait_ge(sem["oT_hi"], 2 * KVH * TT + b + 1)
                dve.scalar_tensor_tensor(hB_lo[:, 2 * b:2 * b + 2, :].rearrange("p m q -> p (m q)"), free_banks[b], gain(O_SG, 0),
                                         hB_hi[:, 2 * b:2 * b + 2, :].rearrange("p m q -> p (m q)").bitcast(F32), ALU.mult, sub).then_inc(sem["oT_lo"], 1)
            scale_heads(0)
            scale_heads(1)
            heads_lo(0)
            scale_heads(2)
            heads_lo(1)
            scale_heads(3)
            heads_lo(2)
            split(C_DO + 2)
            heads_lo(3)
            split(C_DO + 3)
            ffn(1, C_F1, lambda: normalise(3, C_DO + N_DO))
            add_y("out_used", 2 * NJ)
            norm(4)
            dve.wait_ge(sem["final_in"], 16)
            for t in range(TT):
                dve.scalar_tensor_tensor(x[:, t, :], x[:, t, :], rstd[:, t:t + 1], final_g, ALU.mult, ALU.mult).then_inc(sem["out_ready"], 1)


def _layout(i):
    f = np.float32

    def ktiles(w, per):
        k, n = w.shape
        return np.ascontiguousarray(w.reshape(k // P // per, per, P, n).transpose(0, 2, 1, 3).reshape(-1, P, per * n))

    def col(v):
        return v.reshape(-1, P).T

    win = i["nsa_w_in"][0]
    q, kv, gt = win[:, :HEADS * HD], win[:, HEADS * HD:HEADS * HD + 6 * KV_W], win[:, HEADS * HD + 6 * KV_W:]
    kc, vc, ks, vs, kw, vw = (kv[:, n * KV_W:(n + 1) * KV_W] for n in range(6))
    groups = [np.concatenate([kc, vc], 1), q[:, :6 * HD], q[:, 6 * HD:11 * HD], np.concatenate([q[:, 11 * HD:], gt], 1),
              np.concatenate([ks, kw], 1), np.concatenate([vs, vw], 1)]
    arrays = {f"w_group{n}": ktiles(g, 4) for n, g in enumerate(groups)}
    arrays["x_tiles"] = i["x"].reshape(TT, P, D)
    arrays["w_phi"] = ktiles(i["nsa_phi_w1"][0].reshape(2 * CMP_BLOCK * HD, PHI), 8)
    arrays["w_nsa_out"] = ktiles(i["nsa_w_out"][0], 2)

    def column_groups(w):
        return np.concatenate([ktiles(w[:, n:n + 512], 4) for n in range(0, w.shape[1], 512)], 0)

    arrays["w_kv"] = column_groups(i["kv_w"])
    arrays["w_dq"] = column_groups(i["diff_w_q"][0])
    arrays["w_dout"] = ktiles(i["diff_w_out"][0], 2)
    pad = NJ * P - FFN
    fin = np.pad(i["ffn_w_in"].reshape(2, D, 2, FFN), ((0, 0), (0, 0), (0, 0), (0, pad)))
    fin = fin.reshape(2, KT, P, 2, NJ, P).transpose(0, 4, 2, 1, 3, 5).reshape(2, NJ, P, W)
    fout = np.pad(i["ffn_w_out"], ((0, 0), (0, pad), (0, 0))).reshape(2, NJ, P, D)
    taps = np.concatenate([i["ffn_conv_w"], i["ffn_conv_b"][:, None]], 1).reshape(2, 4, 2, FFN)
    taps = np.pad(taps, ((0, 0), (0, 0), (0, 0), (0, pad))).reshape(2, 4, 2, NJ, P).transpose(0, 3, 4, 2, 1).reshape(2, NJ, P, NPRM)
    arrays["w_ffn_in"] = np.ascontiguousarray(fin)
    arrays["w_ffn_out"] = np.ascontiguousarray(np.concatenate([fout, taps], 3))
    pe = i["nsa_phi_pe"][0].reshape(2, CP, P).transpose(2, 0, 1).reshape(P, -1)
    w2 = i["nsa_phi_w2"][0].reshape(2, 2, P, 1, HD)
    w2 = np.broadcast_to(w2, (2, 2, P, 2, HD)).transpose(2, 0, 1, 3, 4).reshape(P, -1)
    rows = np.arange(P)
    rowmask = ((rows[:, None] // CP == np.arange(8)[None, :]) & (rows[:, None] % CP < NCMP)).astype(f)
    lam = np.broadcast_to(i["diff_lambda"][0].reshape(1, -1), (P, 4 * HD))
    inv = np.float32(500000.0) ** (-np.arange(ROT // 2, dtype=f) / f(ROT // 2))
    ang = np.arange(S, dtype=f)[:, None] * inv[None, :]
    cos, sin = np.cos(ang).astype(f), np.sin(ang).astype(f)

    def tok(v):
        return v.reshape(TT, P, -1).transpose(1, 0, 2).reshape(P, -1)

    pos = np.arange(S)
    visible = (np.arange(CP)[None, :] * CMP_STRIDE + CMP_BLOCK - 1 <= pos[:, None]) & (np.arange(CP)[None, :] < NCMP)
    cmp_mask = np.where(visible, 0.0, NEG).astype(f)
    cmp_any = visible.any(1, keepdims=True).astype(f)
    b1 = np.broadcast_to(i["nsa_phi_b1"][0].reshape(1, -1), (P, 2 * PHI))
    table = [col(i["attn_norm_g"][0]), col(i["attn_norm_g"][1]), col(i["ffn_norm_g"][0]), col(i["ffn_norm_g"][1]), col(i["kv_norm_g"]),
             i["diff_subln_g"][0][:, None], pe, w2, rowmask, lam, tok(np.concatenate([cos, cos], 1)), tok(np.concatenate([-sin, sin], 1)),
             tok(cmp_mask), tok(cmp_any), b1]
    arrays["param_cols"] = np.ascontiguousarray(np.concatenate(table, 1).astype(f))
    assert arrays["param_cols"].shape == (P, NCOL)
    arrays["ident"] = np.eye(P, dtype=f)
    arrays["final_g"] = np.ascontiguousarray(np.broadcast_to(i["final_norm_g"][None, :], (P, D)))
    return arrays


def kernel(**inputs):
    import ml_dtypes
    import concourse.bacc as bacc
    from concourse.bass_utils import run_bass_kernel_spmd

    arrays = _layout({k: np.asarray(v) for k, v in inputs.items()})
    arrays["identb"] = np.eye(P).astype(ml_dtypes.bfloat16)
    arrays["causal"] = np.where(np.arange(P)[None, :] <= np.arange(P)[:, None], 0.0, NEG).astype(ml_dtypes.bfloat16)
    nc = bacc.Bacc("TRN2", target_bir_lowering=False, num_devices=1)
    arrays = {f"in_{n}": a for n, a in arrays.items()}
    ap = {n[3:]: nc.dram_tensor(n, a.shape, mybir.dt.from_np(a.dtype), kind="ExternalInput").ap() for n, a in arrays.items()}
    out = nc.dram_tensor("out", (TT, P, D), F32, kind="ExternalOutput").ap()
    build(nc, ap["x_tiles"], ap["param_cols"], ap["ident"], ap["identb"], ap["causal"], [ap[f"w_group{g}"] for g in range(NG)],
          ap["w_phi"], ap["w_nsa_out"], ap["w_ffn_in"], ap["w_ffn_out"], ap["w_kv"], ap["w_dq"], ap["w_dout"], ap["final_g"], out)
    r = run_bass_kernel_spmd(nc, [arrays], core_ids=[0])
    return r.results[0]["out"].reshape(1, S, D)
```

```python
import math
from contextlib import ExitStack

import numpy as np

import concourse.bass as bass
from concourse import mybir

F32 = mybir.dt.float32
F32R = mybir.dt.float32r
BF16 = mybir.dt.bfloat16
I32 = mybir.dt.int32
ALU = mybir.AluOpType
ACT = mybir.ActivationFunctionType
AX = mybir.AxisListType

P = 128
D, S = 1024, 256
TT = S // P
KT = D // P
HEADS, KVH, GROUP, HD = 16, 4, 4, 64
CMP_BLOCK, CMP_STRIDE = 32, 16
NCMP = S // CMP_STRIDE - 1
CP = NCMP + 1
PHI = 256
DH, DV = 8, 128
ROT = HD // 4
FFN = 2752
NJ = -(-FFN // P)
LAST = FFN - (NJ - 1) * P
assert NJ % 2 == 0 and 2 * LAST == P
LAM_INIT = 0.8 - 0.6 * math.exp(-0.3)
LAM_OUT = 1 - LAM_INIT
EPS = 1e-6
OUT_PIECES = [slice(a, b) for a, b in ((0, 384), (384, D))]
NEG = -1e30
SCALE = HD ** -0.5

KV_W = KVH * HD
GROUPS = [("cmp", 2 * KV_W), ("q", 6 * HD), ("q", 5 * HD), ("q", 5 * HD + 3 * HEADS), ("k", 2 * KV_W), ("v", 2 * KV_W)]
Q_HEAD0 = [0, 0, 6, 11]
Q_HEADS = [0, 6, 5, 5]
NG = len(GROUPS)

W = 2048
NPRM = 8
OW = D + NPRM

C_A, N_A = 0, 2 * NG
C_WO, N_WO = C_A + N_A, 4
C_F0 = C_WO + N_WO
C_KV, N_KV = C_F0 + NJ, 8
C_DQ, N_DQ = C_KV + N_KV, 4
C_DO, N_DO = C_DQ + N_DQ, 4
C_F1 = C_DO + N_DO
N_PHI = 4
O_AG, O_FG, O_KG, O_SG = 0, 2 * KT, 4 * KT, 5 * KT
O_PE = O_SG + 1
O_W2 = O_PE + 2 * CP
O_RM = O_W2 + 2 * 2 * P
O_LAM = O_RM + 8
O_COS = O_LAM + 4 * HD
O_SIN = O_COS + TT * ROT
O_CM = O_SIN + TT * ROT
O_CV = O_CM + TT * CP
O_B1 = O_CV + TT
NCOL = O_B1 + 2 * PHI


def width_of(s):
    return 4 * GROUPS[s // 2][1] if s < N_A else W


def stage_of(s):
    return s if s < C_WO else s + N_PHI


SEMS = """x0_in x1_in first_in first_lo gains_in params_in ident_in mask_in identb_ready final_in stage0_full stage1_full stage_out0_full stage_out1_full phi_used
in_hi in_lo in_used out_hi last_hi out_lo out_used conv_params
newton norm_step xT_bank xT_hi xT_lo square mean_sq eps_ready root rstd scaled_dve scaled_act y_ready
proj_act proj_dve rope_t1 rope_t2 rope_done gate_z gate_e gate_e1 gates_ready
pair_T pair_act pair_dve blocks_ready zero
qT_bank qT_act qT_dve kT_bank kT_act kT_dve
hid_z hid_z2 hid_w hid_y hid_t hid_ready hidT_bank hidT_ready kcmp_bank kcmp_ready vcmp_bank vcmp_ready
cmp_scores cmp_masked cmp_max cmp_shift cmp_exp cmp_sum cmp_recip cmp_gate cmp_valid cmp_p cmpT_bank cmpT_ready
scores smax negmax probs recip factor scaled_p pT_bank pT_act pT_dve oT_bank oT_hi oT_lo
x_new u_bank conv0 gate1 val1 gate2 val2 silu prod a_hi a_lo
dk_bank dk_act dk_dve dq_bank dq_act dq_dve
lam_prod lam_sum lam_exp lam_diff lam_ready
dscores dsmax dnegmax dprobs drecip dfactor dmixed dT_bank dT_ready do_bank do_sq do_ready
sub0_step sub0_rstd sub0_scaled sub1_step sub1_rstd sub1_scaled oT2_bank
x_gain out0_ready out1_ready stored""".split()


def build(nc, a_x, a_cols, a_ident, a_mask, a_groups, a_phi, a_wo, a_ffn_in, a_ffn_out, a_kv, a_dq, a_do, a_final, a_out):
    with ExitStack() as ctx:
        def sb(name, shape, dt=F32):
            return ctx.enter_context(nc.sbuf_tensor(name, shape, dt))

        sem = {n: ctx.enter_context(nc.semaphore(n)) for n in SEMS}
        stage_full = [sem["stage0_full"], sem["stage1_full"]]
        stage_out_full = [sem["stage_out0_full"], sem["stage_out1_full"]]

        x = sb("x", [P, TT, D])
        cols = sb("cols", [P, NCOL])
        ident = sb("ident", [P, P])
        identb = sb("identb", [P, P], BF16)
        cmask = sb("cmask", [P, P], BF16)
        stage = sb("stage", [P, 2, W])
        stage_out = sb("stage_out", [P, 2, OW])
        win_hi = sb("win_hi", [P, 2, W], F32R)
        win_lo = sb("win_lo", [P, 2, W], F32R)
        wout_hi = sb("wout_hi", [P, 2, D], F32R)
        wout_lo = sb("wout_lo", [P, 2, D], F32R)
        hA_hi = sb("hA_hi", [P, KT, S], F32R)
        hA_lo = sb("hA_lo", [P, KT, S], F32R)
        hB_hi = sb("hB_hi", [P, KT, S], F32R)
        hB_lo = sb("hB_lo", [P, KT, S], F32R)
        act_hi = sb("act_hi", [P, 2, S], F32R)
        act_lo = sb("act_lo", [P, 2, S], F32R)
        prm = sb("prm", [P, 2, NPRM])
        keysT = sb("keysT", [P, 2, 2048])
        qT = sb("qT", [P, KT, S])
        qrT = sb("qrT", [P, KT, S])
        tokA = sb("tokA", [P, TT, 16, HD])
        tokB = sb("tokB", [P, TT, 16, HD])
        vals = sb("vals", [P, TT, 1024])
        arena = sb("arena", [P, 6144])
        stat = sb("stat", [P, 660])
        gates = sb("gates", [P, TT, HEADS, 3])
        rope_t = sb("rope_t", [P, 2, TT, 8, ROT])

        psA = ctx.enter_context(nc.psum_tensor("psA", [P, 4, 512], F32))
        psT = ctx.enter_context(nc.psum_tensor("psT", [P, 2, 512], F32))
        psO = ctx.enter_context(nc.psum_tensor("psO", [P, 2, 512], F32))
        free_banks = [psT[:, 0], psT[:, 1], psO[:, 0], psO[:, 1]]

        kvc = arena[:, 0:1024].rearrange("p (t c) -> p t c", t=TT)
        k_tok = arena[:, 1024:2048].rearrange("p (t h d) -> p t h d", t=TT, d=HD)
        pairs = arena[:, 2048:3072].rearrange("p (v h u) -> p v h u", v=2, h=KVH)
        blocks = arena[:, 3072:5120].rearrange("p (v m h i) -> p v m h i", v=2, m=CP, h=KVH)
        probs = arena[:, 0:2048].rearrange("p (s h t k) -> p s h t k", s=2, h=2, t=2)
        pT = arena[:, 2048:6144].rearrange("p (s t h q) -> p s t h q", s=2, t=4, h=4)
        aT = arena[:, 2048:3072].rearrange("p (s h b q) -> p s h b q", s=2, h=2, b=2)
        conv = arena[:, 0:1024].rearrange("p (s g q) -> p s g q", s=2, g=2)
        silu = arena[:, 1024:1536].rearrange("p (s q) -> p s q", s=2)
        prod = arena[:, 1536:2048].rearrange("p (s q) -> p s q", s=2)
        squares = arena[:, 2048:4096].rearrange("p (t c) -> p t c", t=TT)
        kcT = rope_t[:, 1, 1, :, :].rearrange("p (e g) c -> p e g c", e=2)
        tokA_flat = tokA[:, :, :, :].rearrange("p t h d -> p (t h d)")
        tokB_flat = tokB[:, :, :, :].rearrange("p t h d -> p (t h d)")
        cmp_s = tokA_flat[:, 0:512].rearrange("p (t h c) -> p t h c", t=TT, h=HEADS)
        cmp_p = tokA_flat[:, 512:1024].rearrange("p (t h c) -> p t h c", t=TT, h=HEADS)
        cmp_pT = tokA_flat[:, 1024:1536].rearrange("p (t b q) -> p t b q", t=TT, b=2)
        hid = tokA_flat[:, 0:512].rearrange("p (v f) -> p v f", v=2)[0:64]
        hid_a = tokA_flat[:, 512:1024].rearrange("p (v f) -> p v f", v=2)[0:64]
        hid_b = tokA_flat[:, 1024:1536].rearrange("p (v f) -> p v f", v=2)[0:64]
        hidT = tokA_flat[:, 1536:1664].rearrange("p (t c) -> p t c", t=2)
        hidTv = arena[:, 3072:4096].rearrange("p (t g r c) -> p t g r c", t=2, g=KVH, r=8)
        vcmp = tokB_flat.rearrange("p (h d) -> p h d", h=HEADS)
        xs = tokB_flat.rearrange("p (t c) -> p t c", t=TT)
        o_tok = tokB_flat.rearrange("p (t h d) -> p t h d", t=TT, h=DH)
        final_g = tokA_flat[:, 0:D]
        vals_nsa = vals[:, :, :].rearrange("p t (y g u d) -> p t y g u d", y=2, g=KVH, u=2)

        ssq = stat[:, 0:TT]
        ms = stat[:, 2:2 + TT]
        rstd = stat[:, 4:4 + TT]
        root = stat[:, 6:6 + TT]
        newton = stat[:, 610:610 + TT]
        eps = stat[:, 612:613]
        warm = stat[:, 613:614]
        mx = stat[:, 8:72].rearrange("p (u c) -> p u c", c=4)
        nmx = stat[:, 72:136].rearrange("p (u c) -> p u c", c=4)
        den = stat[:, 136:200].rearrange("p (u c) -> p u c", c=4)
        rec = stat[:, 200:264].rearrange("p (u c) -> p u c", c=4)
        fac = stat[:, 264:328].rearrange("p (u c) -> p u c", c=4)
        cmx = stat[:, 328:360].rearrange("p (t h) -> p t h", t=TT)
        csum = stat[:, 360:392].rearrange("p (t h) -> p t h", t=TT)
        crec = stat[:, 392:424].rearrange("p (t h) -> p t h", t=TT)
        cfac = stat[:, 424:456].rearrange("p (t h) -> p t h", t=TT)
        gz = stat[:, 456:552].rearrange("p (t c) -> p t c", t=TT)
        lam2 = stat[:, 552:554]
        lame = stat[:, 554:556]
        neg_lam = stat[:, 556:557]
        sq_sub = stat[:, 560:576]
        ms_sub = stat[:, 576:592]
        rstd_sub = stat[:, 592:608]
        newton_sub = stat[:, 628:644]

        cosv = cols[:, O_COS:O_SIN].rearrange("p (t r) -> p t r", t=TT)
        sinv = cols[:, O_SIN:O_CM].rearrange("p (t r) -> p t r", t=TT)
        pe = cols[:, O_PE:O_W2].rearrange("p (v m) -> p v m", v=2)
        w2 = cols[:, O_W2:O_RM].rearrange("p (v t d) -> p v t d", v=2, t=2)
        rowmask = cols[:, O_RM:O_LAM]
        b1 = cols[:, O_B1:NCOL].rearrange("p (v f) -> p v f", v=2)[0:64]

        def gain(off, k):
            return cols[:, off + k:off + k + 1]

        def rsqrt(eng, m, t, out, step, before, done, fused=True):
            n = before
            eng.tensor_scalar(out.bitcast(I32), m.bitcast(I32), -0.5, float(0x5F3759DF), ALU.mult, ALU.add).then_inc(sem[step], 1)
            for it in range(3):
                eng.wait_ge(sem[step], n + 1)
                if fused:
                    eng.scalar_tensor_tensor(t, out, -0.5, out, ALU.mult, ALU.mult).then_inc(sem[step], 1)
                    eng.wait_ge(sem[step], n + 2)
                    eng.tensor_tensor(t, t, m, ALU.mult).then_inc(sem[step], 1)
                    eng.wait_ge(sem[step], n + 3)
                    eng.scalar_tensor_tensor(out, t, 1.5, out, ALU.add, ALU.mult).then_inc(sem[step if it < 2 else done], 1)
                    n += 3
                    continue
                eng.tensor_tensor(t, out, out, ALU.mult).then_inc(sem[step], 1)
                eng.wait_ge(sem[step], n + 2)
                eng.tensor_tensor(t, t, m, ALU.mult).then_inc(sem[step], 1)
                eng.wait_ge(sem[step], n + 3)
                eng.tensor_scalar(t, t, -0.5, 1.5, ALU.mult, ALU.add).then_inc(sem[step], 1)
                eng.wait_ge(sem[step], n + 4)
                eng.tensor_tensor(out, out, t, ALU.mult).then_inc(sem[step if it < 2 else done], 1)
                n += 4

        def of_heads(v, half):
            return v.rearrange("p (t h) -> p t h", t=TT)[:, :, half * 4:half * 4 + 4]

        def heads_rstd(eng, half, step, done, fused=True):
            ms_, t_, out = of_heads(ms_sub, half), of_heads(newton_sub, half), of_heads(rstd_sub, half)
            eng.wait_ge(sem["do_sq"], DH * (half + 1))
            eng.tensor_scalar(ms_, of_heads(sq_sub, half), 1.0 / (DV * LAM_OUT ** 2), EPS / LAM_OUT ** 2, ALU.mult, ALU.add).then_inc(sem[step], 1)
            eng.wait_ge(sem[step], 1)
            rsqrt(eng, ms_, t_, out, step, 1, done, fused)
            eng.wait_ge(sem[done], 1)

        def scale_heads(eng, b, done):
            hs = slice(2 * b, 2 * b + 2)
            r_sub = rstd_sub.rearrange("p (t h) -> p t h", t=TT)
            eng.tensor_tensor(o_tok[:, :, hs, :], o_tok[:, :, hs, :], r_sub[:, :, hs].unsqueeze(3).to_broadcast([P, TT, 2, DV]),
                              ALU.mult).then_inc(sem[done], 1)

        block = ctx.enter_context(nc.Block())

        @block.sync
        def _(sp):
            sp.dma_start(ident[:, :], a_ident).then_inc(sem["ident_in"], 16)
            for t in range(TT):
                sp.dma_start(x[:, t, :], a_x[t]).then_inc(sem[f"x{t}_in"], 16)
            sp.dma_start(cols[:, 0:O_PE], a_cols[:, 0:O_PE]).then_inc(sem["gains_in"], 16)

            def load(n, dst, src, prev_s, prev_phi):
                if prev_s is not None:
                    sp.wait_ge(sem["in_lo"], prev_s + 1)
                if prev_phi is not None:
                    sp.wait_ge(sem["phi_used"], prev_phi + 1)
                sp.dma_start(dst, src).then_inc(stage_full[n % 2], 16)

            def load_main(s, src, width):
                n = stage_of(s)
                prev_phi = n - 2 - N_A if C_WO <= s < C_WO + 2 else None
                prev_s = s - 2 if s >= 2 and prev_phi is None else None
                load(n, stage[:, n % 2, 0:width], src, prev_s, prev_phi)

            for s in range(N_A):
                w4 = width_of(s)
                if s == 0:
                    src = a_groups[0][0]
                    sp.dma_start(stage[:, 0, 0:w4 // 2], src[:, 0:w4 // 2]).then_inc(sem["first_in"], 16)
                    sp.dma_start(stage[:, 0, w4 // 2:w4], src[:, w4 // 2:w4]).then_inc(sem["stage0_full"], 16)
                    continue
                load_main(s, a_groups[s // 2][s % 2], w4)
                if s == 1:
                    sp.dma_start(cols[:, O_PE:NCOL], a_cols[:, O_PE:NCOL]).then_inc(sem["params_in"], 16)
                    sp.dma_start(cmask[:, :], a_mask).then_inc(sem["mask_in"], 16)
            for i in range(N_PHI):
                load(N_A + i, stage[:, i % 2, 0:W], a_phi[i], N_A - 2 + i if i < 2 else None, i - 2 if i >= 2 else None)
            for i in range(N_WO):
                load_main(C_WO + i, a_wo[i], W)

            ffn_in = a_ffn_in.rearrange("l j p c -> (l j) p c")
            ffn_out = a_ffn_out.rearrange("l j p c -> (l j) p c")

            def load_ffn(layer, first):
                f0 = layer * NJ
                for j in range(2):
                    load_main(first + j, a_ffn_in[layer, j], W)
                    if layer:
                        sp.wait_ge(sem["out_lo"], f0 + j - 1)
                    sp.dma_start(stage_out[:, j, :], a_ffn_out[layer, j]).then_inc(stage_out_full[j], 16)
                with sp.Fori(f0, f0 + NJ - 3, 2) as n:
                    for b in range(2):
                        sp.wait_ge(sem["in_lo"], n + (first - f0 + b + 1))
                        sp.dma_start(stage[:, b, :], ffn_in[2 + b:][n]).then_inc(stage_full[b], 16)
                        sp.wait_ge(sem["out_lo"], n + (b + 1))
                        sp.dma_start(stage_out[:, b, :], ffn_out[2 + b:][n]).then_inc(stage_out_full[b], 16)

            load_ffn(0, C_F0)
            for i in range(N_KV + N_DQ):
                load_main(C_KV + i, a_dq[i - 4] if 4 <= i < 8 else a_kv[i if i < 4 else i - N_DQ], W)
            for i in range(N_DO):
                load_main(C_DO + i, a_do[i], W)
            sp.wait_ge(sem["dk_bank"], 4)
            sp.dma_start(final_g, a_final).then_inc(sem["final_in"], 16)
            load_ffn(1, C_F1)
            for i, cs in enumerate(OUT_PIECES):
                for t in range(TT):
                    sp.wait_ge(sem[("out0_ready", "out1_ready")[t]], i + 1)
                    sp.dma_start(a_out[t][:, cs], x[:, t, cs]).then_inc(sem["stored"], 16)
            sp.wait_ge(sem["stored"], 16 * len(OUT_PIECES) * TT)

        @block.tensor
        def _(pe_):
            mm = pe_.matmul
            cmask2 = cmask[:, :].unsqueeze(1).to_broadcast([P, 2, P])

            def three(out, xh, xl, wh, wl, start, stop):
                mm(out, xh, wh, start=start, stop=False)
                mm(out, xh, wl, start=False, stop=False)
                return mm(out, xl, wh, start=False, stop=stop)

            def wait_chunk(s):
                pe_.wait_ge(sem["in_hi"], 2 * (s + 1))
                pe_.wait_ge(sem["in_lo"], s + 1)

            def xT_part(src, t, ks):
                for k in ks:
                    last = pe_.transpose(free_banks[k // 2][:, (k % 2 * TT + t) * P:(k % 2 * TT + t + 1) * P],
                                         src[:, t, k * P:(k + 1) * P], ident[:, :])
                    if t == TT - 1 and k % 2 == 1:
                        last.then_inc(sem["xT_bank"], 1)

            def stay_warm(n, w, h):
                for _ in range(n):
                    mm(psO[:, 1, 0:h.shape[-1]], w, h, start=True, stop=True)

            def xsT(n):
                stay_warm(16, hB_hi[:, 0, 0:P], hB_hi[:, 0, :])
                for t in range(TT):
                    pe_.wait_ge(sem["scaled_dve"], TT * (n - 1) + t + 1)
                    xT_part(xs, t, range(KT // 2))
                for b in range(2, 4):
                    for t in range(TT):
                        pe_.wait_ge(sem["scaled_act"], TT * (n - 1) + t + 1)
                        xT_part(xs, t, (2 * b, 2 * b + 1))

            def project(s0, h_hi, h_lo, out, width, k_tiles, h_waits=None, between=None):
                for half in range(2):
                    if s0 + half > 0:
                        wait_chunk(s0 + half)
                    slot = (s0 + half) % 2
                    wh = win_hi[:, slot, 0:k_tiles * width].rearrange("p (k c) -> p k c", k=k_tiles)
                    wl = win_lo[:, slot, 0:k_tiles * width].rearrange("p (k c) -> p k c", k=k_tiles)
                    for k in range(k_tiles):
                        kk = half * k_tiles + k
                        if s0 + half == 0:
                            pe_.wait_ge(sem["in_hi"], k // 2 + 1)
                            pe_.wait_ge(sem["in_lo" if k >= 2 else "first_lo"], 1)
                        if h_waits is not None:
                            pe_.wait_ge(sem["xT_hi"], h_waits + kk + 1)
                            pe_.wait_ge(sem["xT_lo"], h_waits + kk + 1)
                        for t in range(TT):
                            last = three(out[t], h_hi[:, kk, t * P:(t + 1) * P], h_lo[:, kk, t * P:(t + 1) * P],
                                         wh[:, k, :], wl[:, k, :], kk == 0, kk == 2 * k_tiles - 1)
                    last.then_inc(sem["in_used"], 1)
                    if half == 0 and between is not None:
                        between()

            def out_project(s0, h_hi, h_lo, h_waits, per_chunk, between=None):
                for c in range(4):
                    pe_.wait_ge(sem["oT_hi"], h_waits + per_chunk * (c + 1))
                    pe_.wait_ge(sem["oT_lo"], h_waits + per_chunk * (c + 1))
                    wait_chunk(s0 + c)
                    slot = (s0 + c) % 2
                    for t in range(TT):
                        for k in range(2):
                            kk = 2 * c + k
                            for n in range(2):
                                cs = slice(k * D + n * 512, k * D + n * 512 + 512)
                                last = three(psA[:, 2 * t + n, :], h_hi[:, kk, t * P:(t + 1) * P], h_lo[:, kk, t * P:(t + 1) * P],
                                             win_hi[:, slot, cs], win_lo[:, slot, cs], kk == 0, kk == KT - 1)
                                if kk == KT - 1 and (t, n) in ((0, 1), (1, 0)):
                                    last.then_inc(sem["y_ready"], 1)
                    last.then_inc(sem["in_used"], 1)
                    if between is not None:
                        between(c)

            def ffn(layer, first):
                f0 = layer * NJ

                def up(j, b, h_waits=None):
                    slot = (first + b) % 2
                    pe_.wait_ge(sem["in_hi"], 2 * j + 2 * (first + 1))
                    pe_.wait_ge(sem["in_lo"], j + (first + 1))
                    for g in range(2):
                        for k in range(KT):
                            if h_waits is not None and g == 0:
                                pe_.wait_ge(sem["xT_hi"], h_waits + max(k + 1, 2))
                                pe_.wait_ge(sem["xT_lo"], h_waits + max(k + 1, 2))
                            cs = slice(k * 2 * P + g * P, k * 2 * P + g * P + P)
                            o = (psT, psO)[g][:, b, 0:S]
                            mm(o, win_hi[:, slot, cs], hA_hi[:, k, :], start=k == 0, stop=False)
                            mm(o, win_hi[:, slot, cs], hA_lo[:, k, :], start=False, stop=False)
                            last = mm(o, win_lo[:, slot, cs], hA_hi[:, k, :], start=False, stop=k == KT - 1)
                        if g == 0:
                            last.then_inc(sem["u_bank"], 1)
                    last.then_inc(sem["in_used"], 1)

                def up_last():
                    slot = (first + 1) % 2
                    pe_.wait_ge(sem["in_hi"], 2 * (first + NJ))
                    pe_.wait_ge(sem["in_lo"], first + NJ)
                    pe_.wait_ge(sem["gate2"], f0 + NJ - 2)
                    for k in range(KT):
                        cs = slice(k * P, (k + 1) * P)
                        o = psT[:, 1, 0:S]
                        before = mm(o, win_hi[:, slot, cs], hA_hi[:, k, :], start=k == 0, stop=False)
                        mm(o, win_hi[:, slot, cs], hA_lo[:, k, :], start=False, stop=False)
                        last = mm(o, win_lo[:, slot, cs], hA_hi[:, k, :], start=False, stop=k == KT - 1)
                    before.then_inc(sem["u_bank"], 1)
                    last.then_inc(sem["in_used"], 1)

                def down(j, b, start, stop):
                    pe_.wait_ge(sem["a_lo"], j + (f0 + 1))
                    pe_.wait_ge(sem["out_lo"], j + (f0 + 1))
                    for t in range(TT):
                        for n in range(2):
                            last = three(psA[:, 2 * t + n, :], act_hi[:, b, t * P:(t + 1) * P], act_lo[:, b, t * P:(t + 1) * P],
                                         wout_hi[:, b, n * 512:(n + 1) * 512], wout_lo[:, b, n * 512:(n + 1) * 512], start, stop)
                            if stop and (t, n) in ((0, 1), (1, 0)):
                                last.then_inc(sem["y_ready"], 1)
                    last.then_inc(sem["out_used"], 1)

                up(0, 0, KT * (1 if layer == 0 else 4))
                up(1, 1)
                down(0, 0, True, False)
                with pe_.Fori(0, NJ // 2 - 2) as i:
                    for b in range(2):
                        pe_.wait_ge(sem["val2"], 2 * i + (f0 + b + 1))
                        pe_.wait_ge(sem["gate2"], 2 * i + (f0 + b + 1))
                        up(2 * i + (2 + b), b)
                        down(2 * i + (1 + b), 1 - b, False, False)
                pe_.wait_ge(sem["val2"], f0 + NJ - 3)
                pe_.wait_ge(sem["gate2"], f0 + NJ - 3)
                up(NJ - 2, 0)
                up_last()
                down(NJ - 3, 1, False, False)
                down(NJ - 2, 0, False, False)
                down(NJ - 1, 1, False, True)

            pe_.wait_ge(sem["ident_in"], 16)

            def q_transposes(banks):
                for i in banks:
                    if i < 2:
                        pe_.wait_ge(sem["pair_act"], 4)
                        pe_.wait_ge(sem["pair_dve"], 4)
                    if i >= 4:
                        pe_.wait_ge(sem["qT_act"], i // 2 - 1)
                        pe_.wait_ge(sem["qT_dve"], i // 2 - 1)
                    src = tokB if i % 2 else tokA
                    for mi in range(2):
                        m = 2 * (i // 2) + mi
                        for t in range(TT):
                            last = pe_.transpose(free_banks[i % 4][:, (mi * TT + t) * P:(mi * TT + t + 1) * P],
                                                 src[:, t, 2 * m:2 * m + 2, :].rearrange("p h d -> p (h d)"), ident[:, :])
                    last.then_inc(sem["qT_bank"], 1)

            for t in range(TT):
                pe_.wait_ge(sem[f"x{t}_in"], 16)
                xT_part(x, t, range(KT))
            for g, (_, width) in enumerate(GROUPS):
                if g >= 2:
                    pe_.wait_ge(sem["proj_act"], g - 1)
                    pe_.wait_ge(sem["proj_dve"], g - 1)
                project(2 * g, hA_hi, hA_lo, [psA[:, 2 * (g % 2) + t, 0:width] for t in range(TT)], width, 4,
                        0 if g == 0 else None, (lambda: q_transposes(range(4, 8))) if g == 5 else None)
                if g == 1:
                    pe_.wait_ge(sem["proj_act"], 1)
                    perm = ident[:, :].rearrange("p (u r) -> p r u", r=2)
                    for v in range(2):
                        for pr in range(2):
                            for t in range(TT):
                                last = pe_.transpose(psT[:, v, (pr * TT + t) * P:(pr * TT + t + 1) * P],
                                                     kvc[:, t, v * KV_W + pr * P:v * KV_W + (pr + 1) * P], perm)
                        last.then_inc(sem["pair_T"], 1)
                if g == 4:
                    pe_.wait_ge(sem["proj_act"], 4)
                    pe_.wait_ge(sem["rope_done"], 3)
                    q_transposes(range(4))
            pe_.wait_ge(sem["rope_done"], 4)
            for pr in range(2):
                pe_.wait_ge(sem["qT_act"], 4)
                pe_.wait_ge(sem["qT_dve"], 4)
                for y in range(2):
                    for t in range(TT):
                        last = pe_.transpose(psT[:, pr, (y * TT + t) * P:(y * TT + t + 1) * P],
                                             k_tok[:, t, 4 * y + 2 * pr:4 * y + 2 * pr + 2, :].rearrange("p h d -> p (h d)"), ident[:, :])
                last.then_inc(sem["kT_bank"], 1)
            pe_.wait_ge(sem["identb_ready"], 1)
            pe_.wait_ge(sem["mask_in"], 16)

            UNITS = [(g, t, m2) for g in range(KVH) for t in range(TT) for m2 in range(2)]

            def nsa_scores(u):
                g, t, m2 = UNITS[u]
                m, nk = 2 * g + m2, (t + 1) * P
                if u < 2:
                    pe_.wait_ge(sem["proj_act"], NG - 1 + u)
                    pe_.wait_ge(sem["proj_dve"], NG - 1 + u)
                else:
                    pe_.wait_ge(sem["smax"], u - 1)
                    pe_.wait_ge(sem["probs"], 4 * (u - 1))
                pe_.wait_ge(sem[("kT_act", "kT_dve")[g % 2]], 2 * (g // 2 + 1))
                for e in range(2):
                    bank = psA[:, 2 * (u % 2) + e, :].rearrange("p (y k) -> p y k", y=2)
                    keys = keysT[:, e, g * 512:(g + 1) * 512].rearrange("p (y k) -> p y k", y=2)
                    mm(bank[:, :, 0:nk], qrT[:, m, t * P:(t + 1) * P], keys[:, :, 0:nk], start=True, stop=False)
                    last = mm(bank[:, :, t * P:nk], identb[:, :], cmask2, start=False, stop=True)
                last.then_inc(sem["scores"], 1)

            def nsa_transpose(u):
                nb = UNITS[u][1] + 1
                pe_.wait_ge(sem["scaled_p"], 4 * (u + 1))
                if u >= 1:
                    pe_.wait_ge(sem["pT_act"], u)
                    pe_.wait_ge(sem["pT_dve"], u)
                for e in range(2):
                    for y in range(2):
                        for b in range(nb):
                            i = y * nb + b
                            last = pe_.transpose(psT[:, e, i * P:(i + 1) * P], probs[:, u % 2, e, y, b * P:(b + 1) * P], ident[:, :])
                last.then_inc(sem["pT_bank"], 1)

            def nsa_pv(w, y):
                g, t = w // TT, w % TT
                nb = t + 1
                if y == 0:
                    pe_.wait_ge(sem["pT_act"], 2 * w + 2)
                    pe_.wait_ge(sem["pT_dve"], 2 * w + 2)
                    if w >= 2:
                        pe_.wait_ge(sem["oT_lo"], 2 * (w - 1))
                o = psO[:, w % 2, :]
                for b in range(nb):
                    mm(o, vals_nsa[:, b, y, g, :, :].rearrange("p u d -> p (u d)"),
                       pT[:, w % 2, y * nb + b, :, :].rearrange("p h q -> p (h q)"), start=y == 0 and b == 0, stop=False)
                if y == 1:
                    for j in range(GROUP):
                        last = mm(o[:, j * P:(j + 1) * P], vcmp[:, 4 * g + j, :], cmp_pT[:, t, g // 2, :], start=False, stop=j == GROUP - 1)
                    last.then_inc(sem["oT_bank"], 1)

            def cmp_scores(t):
                for m in range(KT):
                    last = mm(psO[:, m // 4, (m % 4) * P:(m % 4 + 1) * P], qT[:, m, t * P:(t + 1) * P],
                              kcT.rearrange("p e g c -> p (e g c)"), start=True, stop=True)
                last.then_inc(sem["cmp_scores"], 1)

            nsa_scores(0)
            nsa_scores(1)
            pe_.wait_ge(sem["blocks_ready"], 4)
            for v in range(2):
                for half in range(2):
                    i = 2 * v + half
                    pe_.wait_ge(stage_full[i % 2], 16 * ((N_A + i) // 2 + 1))
                    for m in range(8):
                        mg = 8 * half + m
                        last = mm(psO[0:64, 0, v * PHI:(v + 1) * PHI], blocks[:, v, mg, :, :].rearrange("p h i -> p (h i)"),
                                  stage[:, i % 2, m * PHI:(m + 1) * PHI], start=mg == 0, stop=mg == CP - 1)
                    last.then_inc(sem["phi_used"], 1)
                if v == 0:
                    nsa_transpose(0)
                    nsa_scores(2)
            nsa_transpose(1)
            nsa_scores(3)
            nsa_scores(4)
            nsa_transpose(2)
            pe_.wait_ge(sem["hid_ready"], 1)
            for v in range(2):
                for c in range(2):
                    last = pe_.transpose(psO[:, 1, (2 * v + c) * 64:(2 * v + c + 1) * 64], hid[:, v, c * P:(c + 1) * P], ident[0:64, 0:64])
            last.then_inc(sem["hidT_bank"], 1)
            pe_.wait_ge(sem["params_in"], 16)
            pe_.wait_ge(sem["hidT_ready"], 1)
            for c in range(2):
                last = mm(psO[:, 0, 0:64], w2[:, 0, c, :], hidT[:, c, :], start=c == 0, stop=c == 1)
            last.then_inc(sem["kcmp_bank"], 1)
            pe_.wait_ge(sem["kcmp_ready"], 2)
            pe_.wait_ge(sem["hidT_ready"], 2)
            cmp_scores(0)
            nsa_scores(5)
            pe_.wait_ge(sem["cmp_masked"], 4)
            cmp_scores(1)
            nsa_transpose(3)
            pe_.wait_ge(sem["cmp_masked"], 8)
            for g in range(KVH):
                for c in range(2):
                    last = mm(psO[:, 1, g * P:(g + 1) * P],
                              hidTv[:, c, g, :, :].rearrange("p r c -> p (r c)"),
                              w2[:, 1, c, :], start=c == 0, stop=c == 1)
            last.then_inc(sem["vcmp_bank"], 1)
            nsa_pv(0, 0)
            for u in range(4, len(UNITS)):
                if u + 2 < len(UNITS):
                    nsa_scores(u + 2)
                nsa_transpose(u)
                if u == 4:
                    pe_.wait_ge(sem["cmp_p"], 1)
                    pe_.wait_ge(sem["vcmp_ready"], 8)
                    for t in range(TT):
                        for b in range(2):
                            last = pe_.transpose(psO[:, 1, (2 * t + b) * P:(2 * t + b + 1) * P],
                                                 cmp_p[:, t, 8 * b:8 * b + 8, :].rearrange("p h c -> p (h c)"), ident[:, :])
                    last.then_inc(sem["cmpT_bank"], 1)
                    pe_.wait_ge(sem["cmpT_ready"], 1)
                    nsa_pv(0, 1)
                nsa_pv(u // 2 - 1, u % 2)
            for y in range(2):
                nsa_pv(len(UNITS) // 2 - 1, y)
            out_project(C_WO, hB_hi, hB_lo, 0, 2 * TT)

            xsT(1)
            ffn(0, C_F0)

            for t in range(TT):
                pe_.wait_ge(sem["x_new"], TT + t + 1)
                xT_part(x, t, range(KT // 2))
            for b in range(2, 4):
                for t in range(TT):
                    xT_part(x, t, (2 * b, 2 * b + 1))

            def dk_transposes():
                pe_.wait_ge(sem["rope_done"], 4 + 2)
                pe_.wait_ge(sem["xT_hi"], 4 * KT)
                pe_.wait_ge(sem["xT_lo"], 4 * KT)
                for i in range(4):
                    for mi in range(2):
                        for t in range(TT):
                            last = pe_.transpose(free_banks[i][:, (mi * TT + t) * P:(mi * TT + t + 1) * P],
                                                 tokA[:, t, 2 * (2 * i + mi):2 * (2 * i + mi) + 2, :].rearrange("p h d -> p (h d)"), ident[:, :])
                    last.then_inc(sem["dk_bank"], 1)

            def dq_transposes():
                pe_.wait_ge(sem["rope_done"], 4 + 4)
                for i in range(4):
                    pe_.wait_ge(sem["dk_act"], i + 1)
                    pe_.wait_ge(sem["dk_dve"], i + 1)
                    for mi in range(2):
                        for t in range(TT):
                            last = pe_.transpose(free_banks[i][:, (mi * TT + t) * P:(mi * TT + t + 1) * P],
                                                 tokB[:, t, 2 * (2 * i + mi):2 * (2 * i + mi) + 2, :].rearrange("p h d -> p (h d)"), ident[:, :])
                    last.then_inc(sem["dq_bank"], 1)

            for g in range(6):
                if g >= 2:
                    pe_.wait_ge(sem["proj_act"], NG + g - 1)
                    pe_.wait_ge(sem["proj_dve"], NG + g - 1)
                hh, hl = (hB_hi, hB_lo) if g in (2, 3) else (hA_hi, hA_lo)
                project(C_KV + 2 * g, hh, hl, [psA[:, 2 * (g % 2) + t, :] for t in range(TT)], 512, 4,
                        {0: 2 * KT, 2: 3 * KT}.get(g), {3: dk_transposes, 4: dq_transposes}.get(g))
            pe_.wait_ge(sem["dq_act"], 2)
            pe_.wait_ge(sem["dq_dve"], 2)

            def diff_scores(u):
                hp, t = u // TT, u % TT
                nk = (t + 1) * P
                if u < 2:
                    pe_.wait_ge(sem["proj_act"], NG + 5 + u)
                    pe_.wait_ge(sem["proj_dve"], NG + 5 + u)
                else:
                    pe_.wait_ge(sem["dsmax"], u - 1)
                    pe_.wait_ge(sem["dprobs"], 4 * (u - 1))
                for e in range(2):
                    h = 2 * hp + e
                    bank = psA[:, 2 * (u % 2) + e, :].rearrange("p (c k) -> p c k", c=2)
                    mm(bank[:, :, 0:nk], qrT[:, h, t * P:(t + 1) * P], keysT[:, :, h * S:h * S + nk], start=True, stop=False)
                    last = mm(bank[:, :, t * P:nk], identb[:, :], cmask2, start=False, stop=True)
                last.then_inc(sem["dscores"], 1)

            def diff_transpose(u):
                t = u % TT
                pe_.wait_ge(sem["dmixed"], 2 * (u + 1))
                if u >= 2:
                    pe_.wait_ge(sem["dT_ready"], u - 1)
                for e in range(2):
                    for b in range(t + 1):
                        last = pe_.transpose(psT[:, u % 2, (e * 2 + b) * P:(e * 2 + b + 1) * P], probs[:, u % 2, e, 0, b * P:(b + 1) * P], ident[:, :])
                last.then_inc(sem["dT_bank"], 1)

            def diff_pv(u):
                hp, t = u // TT, u % TT
                pe_.wait_ge(sem["dT_ready"], u + 1)
                if u >= 2:
                    pe_.wait_ge(sem["do_ready"], 2 * (u - 1))
                for e in range(2):
                    h = 2 * hp + e
                    for b in range(t + 1):
                        last = mm(psO[:, u % 2, e * DV:(e + 1) * DV], aT[:, u % 2, e, b, :], vals[:, b, h * DV:(h + 1) * DV],
                                  start=b == 0, stop=b == t)
                last.then_inc(sem["do_bank"], 1)

            ND = DH // 2 * TT
            diff_scores(0)
            diff_scores(1)
            for u in range(ND):
                if u + 2 < ND:
                    diff_scores(u + 2)
                diff_transpose(u)
                if u >= 1:
                    diff_pv(u - 1)
            def heads_T(b):
                pe_.wait_ge(sem[f"sub{b // 2}_scaled"], b % 2 + 1)
                for kk in range(2):
                    for t in range(TT):
                        last = pe_.transpose(free_banks[b][:, (kk * TT + t) * P:(kk * TT + t + 1) * P], o_tok[:, t, 2 * b + kk, :], ident[:, :])
                last.then_inc(sem["oT2_bank"], 1)

            def next_heads(c):
                if c < 2:
                    heads_T(c + 2)

            diff_pv(ND - 1)
            heads_T(0)
            heads_T(1)
            out_project(C_DO, hB_hi, hB_lo, 2 * KVH * TT, 1, next_heads)

            xsT(2)
            ffn(1, C_F1)

        @block.gpsimd
        def _(pool):
            def split(s):
                n = stage_of(s)
                pool.wait_ge(stage_full[n % 2], 16 * (n // 2 + 1))
                pool.wait_ge(sem["in_used"], s - 1)
                pool.wait_ge(sem["in_lo"], s)
                for h in range(2):
                    cs = slice(h * W // 2, (h + 1) * W // 2)
                    pool.tensor_copy(win_hi[:, s % 2, cs], stage[:, n % 2, cs]).then_inc(sem["in_hi"], 1)
                for h in range(2):
                    cs = slice(h * W // 2, (h + 1) * W // 2)
                    pool.wait_ge(sem["in_hi"], 2 * s + h + 1)
                    last = pool.tensor_tensor(win_lo[:, s % 2, cs], stage[:, n % 2, cs], win_hi[:, s % 2, cs].bitcast(F32), ALU.subtract)
                last.then_inc(sem["in_lo"], 1)

            def norm(n):
                pool.wait_ge(sem["square"], TT * (n + 1))
                pool.tensor_scalar(ms, ssq, 1.0 / D, EPS, ALU.mult, ALU.add).then_inc(sem["mean_sq"], 1)
                pool.wait_ge(sem["mean_sq"], n // 2 + 1)
                rsqrt(pool, ms, newton, rstd, "norm_step", 12 * (n // 2), "rstd", fused=False)

            pool.memset(eps, EPS).then_inc(sem["eps_ready"], 1)
            norm(0)
            split(C_WO)
            split(C_WO + 1)
            norm(2)
            split(C_DO + 1)
            heads_rstd(pool, 0, "sub0_step", "sub0_rstd", fused=False)
            pool.wait_ge(sem["do_ready"], DH)
            scale_heads(pool, 0, "sub0_scaled")
            scale_heads(pool, 1, "sub0_scaled")

        @block.scalar
        def _(act):
            def split(s, halves=(0, 1)):
                n, w = stage_of(s), width_of(s)
                if s >= 2:
                    act.wait_ge(sem["in_used"], s - 1)
                for h in halves:
                    if s == 0 and h == 0:
                        act.wait_ge(sem["first_in"], 16)
                    else:
                        act.wait_ge(stage_full[n % 2], 16 * (n // 2 + 1))
                    cs = slice(h * w // 2, (h + 1) * w // 2)
                    act.activation(win_hi[:, s % 2, cs], stage[:, n % 2, cs], ACT.Copy).then_inc(sem["in_hi"], 1)

            def h_hi(dst, off, inst, lo_done=0, ks=range(KT)):
                for k in ks:
                    if k % 2 == 0:
                        act.wait_ge(sem["xT_bank"], 4 * inst + k // 2 + 1)
                        if lo_done:
                            act.wait_ge(sem["xT_lo"], lo_done + k + 2)
                    act.activation(dst[:, k, :], free_banks[k // 2][:, (k % 2) * S:(k % 2 + 1) * S], ACT.Copy,
                                   scale=gain(off, k)).then_inc(sem["xT_hi"], 1)

            def norm(n, wait_x, roots=None):
                if roots == 0:
                    act.wait_ge(sem["eps_ready"], 1)
                if roots is not None:
                    act.activation(warm, eps, ACT.Sqrt)
                for t in range(TT):
                    wait_x(t)
                    act.activation(squares[:, t, :], x[:, t, :], ACT.Square, accum_out=ssq[:, t:t + 1]).then_inc(sem["square"], 1)
                    if roots is not None:
                        act.wait_ge(sem["square"], TT * n + t + 1)
                        act.activation(root[:, t:t + 1], ssq[:, t:t + 1], ACT.Sqrt, bias=eps, scale=1.0 / D).then_inc(sem["root"], 1)

            def normalise(n, wait_x):
                norm(n, wait_x, n // 2)
                act.wait_ge(sem["rstd"], n + 1)
                for t in range(TT):
                    act.activation(xs[:, t, D // 2:D], x[:, t, D // 2:D], ACT.Copy, scale=rstd[:, t:t + 1]).then_inc(sem["scaled_act"], 1)

            def x_in(t):
                act.wait_ge(sem[f"x{t}_in"], 16)

            def x_new(n):
                def f(t):
                    act.wait_ge(sem["x_new"], TT * n + t + 1)
                return f

            def ffn(layer, first, normalise):
                f0 = layer * NJ

                def split_in(j, b, h):
                    slot = (first + b) % 2
                    if h == 0:
                        act.wait_ge(stage_full[slot], 8 * j + (16 * (stage_of(first + b) // 2 + 1) - 8 * b))
                        act.wait_ge(sem["in_used"], j + (first - 1))
                    act.activation(win_hi[:, slot, h * W // 2:(h + 1) * W // 2], stage[:, slot, h * W // 2:(h + 1) * W // 2],
                                   ACT.Copy).then_inc(sem["in_hi"], 1)

                def split_out(j, b, wait=True):
                    act.wait_ge(stage_out_full[b], 8 * j + (8 * f0 + 16 - 8 * b))
                    if wait:
                        act.wait_ge(sem["out_used"], j + (f0 - 1))
                    act.activation(wout_hi[:, b, :], stage_out[:, b, 0:D], ACT.Copy).then_inc(sem["out_hi"], 1)

                def step(j, b, split_next=True, split_wout=True):
                    act.wait_ge(sem["u_bank"], j + (f0 + 1))
                    act.wait_ge(sem["conv_params"], j + (f0 + 1))
                    act.wait_ge(sem["prod"], j + f0) if not (isinstance(j, int) and j + f0 == 0) else None
                    for g in range(2):
                        if g == 1:
                            act.wait_ge(sem["in_used"], j + (first + 1))
                        act.activation(conv[:, b, g, :], (psT, psO)[g][:, b, 0:S], ACT.Identity,
                                       bias=prm[:, b, 4 * g + 3:4 * g + 4], scale=prm[:, b, 4 * g + 2:4 * g + 3]).then_inc(sem["conv0"], 1)
                    if split_next:
                        split_in(j + 2, b, 0)
                    act.wait_ge(sem["gate2"], j + (f0 + 1))
                    act.activation(silu[:, b, :], conv[:, b, 0, :], ACT.Silu).then_inc(sem["silu"], 1)
                    if split_next:
                        split_in(j + 2, b, 1)
                    act.wait_ge(sem["prod"], j + (f0 + 1))
                    if not (isinstance(j, int) and j + f0 < 2):
                        act.wait_ge(sem["out_used"], j + (f0 - 1))
                    act.activation(act_hi[:, b, :], prod[:, b, :], ACT.Copy).then_inc(sem["a_hi"], 1)
                    if split_wout:
                        split_out(j + 1, 1 - b, not (isinstance(j, int) and j + 1 + f0 < 2))

                def last_step():
                    act.wait_ge(sem["in_used"], first + NJ)
                    act.wait_ge(sem["conv_params"], f0 + NJ)
                    act.wait_ge(sem["prod"], f0 + NJ - 1)
                    act.activation(conv[:, 1, 0, :], psT[:, 1, 0:S], ACT.Identity, bias=prm[:, 1, 3:4], scale=prm[:, 1, 2:3]).then_inc(sem["conv0"], 2)
                    act.wait_ge(sem["gate2"], f0 + NJ)
                    act.activation(silu[0:LAST, 1, :], conv[0:LAST, 1, 0, :], ACT.Silu).then_inc(sem["silu"], 1)
                    act.wait_ge(stage_out_full[1], 16 * (f0 + NJ) // 2)
                    act.wait_ge(sem["out_used"], f0 + NJ - 2)
                    for h, done in enumerate(("last_hi", "out_hi")):
                        cs = slice(h * D // 2, (h + 1) * D // 2)
                        act.activation(wout_hi[:, 1, cs], stage_out[:, 1, cs], ACT.Copy).then_inc(sem[done], 1)
                    act.wait_ge(sem["prod"], f0 + NJ)
                    act.activation(act_hi[0:LAST, 1, :], prod[0:LAST, 1, :], ACT.Copy).then_inc(sem["a_hi"], 1)
                    if layer == 0:
                        split_in(NJ + 1, 1, 0)
                        split_in(NJ + 1, 1, 1)

                split_in(0, 0, 0)
                split_in(0, 0, 1)
                split_out(0, 0, layer > 0)
                normalise()
                h_hi(hA_hi, O_FG + layer * KT, 1 if layer == 0 else 3)
                split_in(1, 1, 0)
                split_in(1, 1, 1)
                act.activation(warm, eps, ACT.Silu)
                step(0, 0)
                step(1, 1)
                with act.Fori(0, NJ // 2 - 2) as i:
                    for b in range(2):
                        step(2 * i + (2 + b), b)
                step(NJ - 2, 0, layer == 0, False)
                last_step()

            act.wait_ge(sem["ident_in"], 16)
            act.activation(identb[:, :], ident[:, :], ACT.Copy).then_inc(sem["identb_ready"], 1)
            act.wait_ge(sem["gains_in"], 16)
            h_hi(hA_hi, O_AG, 0, ks=range(2))
            split(0, (0,))
            h_hi(hA_hi, O_AG, 0, ks=range(2, 4))
            split(0, (1,))
            h_hi(hA_hi, O_AG, 0, ks=range(4, KT))
            split(1)
            norm(0, x_in)
            for c in range(N_A):
                if c % 2 and c < N_A - 1:
                    g = c // 2
                    kind, width = GROUPS[g]
                    if g == 0:
                        act.wait_ge(sem["rstd"], 1)
                    act.wait_ge(sem["in_used"], c + 1)
                    for t in range(TT):
                        bank = psA[:, 2 * (g % 2) + t, :]
                        r = rstd[:, t:t + 1]
                        if kind == "cmp":
                            last = act.activation(kvc[:, t, :], bank, ACT.Copy, scale=r)
                        if kind == "q":
                            nh, h0 = Q_HEADS[g], Q_HEAD0[g]
                            if g == 3:
                                act.activation(gz[:, t, :], bank[:, nh * HD:width], ACT.Copy, scale=r).then_inc(sem["gate_z"], 1)
                            last = act.activation(tokA[:, t, h0:h0 + nh, :], bank[:, 0:nh * HD].rearrange("p (h d) -> p h d", d=HD),
                                                  ACT.Copy, scale=r)
                        if kind == "k":
                            last = act.activation(k_tok[:, t, :, :], bank.rearrange("p (h d) -> p h d", d=HD), ACT.Copy, scale=r)
                    last.then_inc(sem["proj_act"], 1)
                    if g == 3:
                        act.wait_ge(sem["gate_z"], 2)
                        act.activation(gz, gz, ACT.Exp, scale=-1.0).then_inc(sem["gate_e"], 1)
                if c + 2 < N_A:
                    split(c + 2)
                if c == 3:
                    for v in range(2):
                        act.wait_ge(sem["pair_T"], v + 1)
                        for r in range(2):
                            act.activation(pairs[r * 64:r * 64 + 64, v, 0:KVH:2, :].rearrange("p h (t u) -> p h t u", t=TT),
                                           psT[0:64, v, :].rearrange("p (h t r u) -> p r h t u", h=2, t=TT, r=2)[:, r],
                                           ACT.Copy).then_inc(sem["pair_act"], 1)
                if c in (9, 10):
                    for i in range(4 * (c - 9), 4 * (c - 9) + 4, 2):
                        act.wait_ge(sem["qT_bank"], i + 1)
                        act.activation(qT[:, i:i + 2, :].rearrange("p m q -> p (m q)"), free_banks[i % 4], ACT.Copy).then_inc(sem["qT_act"], 1)
            act.wait_ge(sem["zero"], 3)
            for pr in range(2):
                act.wait_ge(sem["kT_bank"], pr + 1)
                for e in range(2):
                    act.activation(keysT[e * 64:e * 64 + 64, e, 2 * pr * 512:(2 * pr + 1) * 512], psT[0:64, pr, :],
                                   ACT.Copy).then_inc(sem["kT_act"], 1)
            act.wait_ge(sem["in_used"], N_A)
            act.activation(vals_nsa[:, 1, :, :, :, :].rearrange("p y g u d -> p (y g) u d"),
                           psA[:, 3, :].rearrange("p (h d) -> p h d", d=HD).unsqueeze(2).to_broadcast([P, 8, 2, HD]),
                           ACT.Copy, scale=rstd[:, 1:2]).then_inc(sem["proj_act"], 1)
            def exps(u, t, pre, waits_free):
                nk = (t + 1) * P
                act.wait_ge(sem[pre + "negmax"], u + 1)
                waits_free(u)
                for e in range(2):
                    for y in range(2):
                        act.activation(probs[:, u % 2, e, y, 0:nk], psA[:, 2 * (u % 2) + e, y * S:y * S + nk], ACT.Exp,
                                       bias=nmx[:, u, 2 * e + y:2 * e + y + 1], scale=SCALE,
                                       accum_out=den[:, u, 2 * e + y:2 * e + y + 1]).then_inc(sem[pre + "probs"], 1)

            def free_nsa(u):
                if u >= 2:
                    act.wait_ge(sem["pT_bank"], u - 1)

            NU = KVH * TT * 2

            def nsa_rest(u):
                t, m2 = (u // 2) % 2, u % 2
                nb = t + 1
                act.wait_ge(sem["pT_bank"], u + 1)
                if u >= 4 and m2 == 0:
                    act.wait_ge(sem["oT_bank"], u // 2 - 1)
                act.activation(pT[:, (u // 2) % 2, 0:2 * nb, 2 * m2, :], psT[:, 0, 0:2 * nb * P].rearrange("p (i q) -> p i q", q=P),
                               ACT.Copy).then_inc(sem["pT_act"], 1)

            def oT_hi(w):
                g, t = w // TT, w % TT
                act.wait_ge(sem["oT_bank"], w + 1)
                for e in range(2):
                    act.activation(hB_hi[e * 64:e * 64 + 64, 2 * g:2 * g + 2, t * P:(t + 1) * P],
                                   psO[e * 64:e * 64 + 64, w % 2, :].rearrange("p (m e q) -> p e m q", m=2, e=2)[:, e],
                                   ACT.Copy).then_inc(sem["oT_hi"], 1)

            exps(0, 0, "", free_nsa)
            exps(1, 0, "", free_nsa)
            nsa_rest(0)
            exps(2, 1, "", free_nsa)
            act.wait_ge(sem["hid_y"], 1)
            act.activation(hid_b, hid_a, ACT.Tanh, scale=math.sqrt(2 / math.pi)).then_inc(sem["hid_t"], 1)
            nsa_rest(1)
            act.wait_ge(sem["hidT_bank"], 1)
            act.activation(hidT.rearrange("p t c -> p (t c)"), psO[:, 1, 0:128], ACT.Copy, scale=0.5).then_inc(sem["hidT_ready"], 1)
            act.activation(hidTv.rearrange("p t g r c -> p (t g) r c"),
                           psO[:, 1, 128:256].rearrange("p (x c) -> p x c", c=CP).unsqueeze(2).to_broadcast([P, 2 * KVH, 8, CP]),
                           ACT.Copy, scale=0.5).then_inc(sem["hidT_ready"], 1)
            act.wait_ge(sem["kcmp_bank"], 1)
            for e in range(2):
                act.activation(kcT[e * 64:e * 64 + 64, e, :, :].rearrange("p g c -> p (g c)"), psO[e * 64:e * 64 + 64, 0, 0:64],
                               ACT.Copy).then_inc(sem["kcmp_ready"], 1)
            exps(3, 1, "", free_nsa)
            nsa_rest(2)
            exps(4, 0, "", free_nsa)
            act.wait_ge(sem["cmp_shift"], 1)
            act.activation(cmp_p, cmp_s, ACT.Exp, scale=SCALE).then_inc(sem["cmp_exp"], 1)
            nsa_rest(3)
            exps(5, 0, "", free_nsa)
            act.wait_ge(sem["vcmp_bank"], 1)
            act.wait_ge(sem["params_in"], 16)
            for r in range(8):
                act.activation(vcmp[:, r:HEADS:8, :], psO[:, 1, :].rearrange("p (g d) -> p g d", g=KVH)[:, r // 4:KVH:2], ACT.Copy,
                               scale=rowmask[:, r:r + 1]).then_inc(sem["vcmp_ready"], 1)
            act.wait_ge(sem["cmpT_bank"], 1)
            act.activation(cmp_pT.rearrange("p t b q -> p (t b q)"), psO[:, 1, :], ACT.Copy).then_inc(sem["cmpT_ready"], 1)
            for u in range(4, NU):
                nsa_rest(u)
                if u == 4:
                    oT_hi(0)
                if u + 2 < NU:
                    exps(u + 2, ((u + 2) // 2) % 2, "", free_nsa)
                if u >= 5 and u % 2 == 1:
                    oT_hi(u // 2 - 1)
            oT_hi(NU // 2 - 1)
            act.wait_ge(sem["in_lo"], C_WO + 2)
            split(C_WO + 2)
            split(C_WO + 3)

            ffn(0, C_F0, lambda: normalise(1, x_new(0)))

            h_hi(hA_hi, O_KG, 2)
            norm(2, x_new(1))
            h_hi(hB_hi, O_AG + KT, 2, 2 * KT)
            act.wait_ge(sem["rstd"], 3)
            for c in range(12):
                g = c // 2
                if c % 2:
                    act.wait_ge(sem["in_used"], C_KV + c + 1)
                    for t in range(TT):
                        bank = psA[:, 2 * (g % 2) + t, :]
                        r = rstd[:, t:t + 1]
                        if g < 4:
                            dst = tokA if g < 2 else tokB
                            last = act.activation(dst[:, t, 8 * (g % 2):8 * (g % 2) + 8, :], bank.rearrange("p (h d) -> p h d", d=HD),
                                                  ACT.Copy, scale=r)
                        elif t == 1:
                            last = act.activation(vals[:, t, (g - 4) * 512:(g - 3) * 512], bank, ACT.Copy, scale=r)
                    last.then_inc(sem["proj_act"], 1)
                if c == 6:
                    for i in range(4):
                        act.wait_ge(sem["dk_bank"], i + 1)
                        act.activation(keysT[0:64, 0, i * 512:(i + 1) * 512], free_banks[i][0:64, :], ACT.Copy).then_inc(sem["dk_act"], 1)
                    act.wait_ge(sem["lam_sum"], 2)
                    act.activation(lame, lam2, ACT.Exp).then_inc(sem["lam_exp"], 1)
                if c == 8:
                    for i in range(0, 4, 2):
                        act.wait_ge(sem["dq_bank"], i + 1)
                        act.activation(qrT[:, 2 * i:2 * i + 2, :].rearrange("p m q -> p (m q)"), free_banks[i], ACT.Copy).then_inc(sem["dq_act"], 1)
                if c < 11:
                    split(C_KV + c + 2)

            def free_diff(u):
                if u >= 2:
                    act.wait_ge(sem["dT_bank"], u - 1)
            ND = DH // 2 * TT

            def head_squares(u):
                hp, t = u // TT, u % TT
                for e in range(2):
                    h = 2 * hp + e
                    act.wait_ge(sem["do_ready"], 2 * u + e + 1)
                    act.activation(arena[:, 3072 + (2 * u + e) * P:3072 + (2 * u + e + 1) * P], o_tok[:, t, h, :], ACT.Square,
                                   accum_out=sq_sub[:, t * DH + h:t * DH + h + 1]).then_inc(sem["do_sq"], 1)
            exps(0, 0, "d", free_diff)
            exps(1, 1, "d", free_diff)
            for u in range(ND):
                if u + 2 < ND:
                    exps(u + 2, u % TT, "d", free_diff)
                if u >= 2:
                    head_squares(u - 2)
            head_squares(ND - 2)
            head_squares(ND - 1)
            for b in range(4):
                if b == 3:
                    act.wait_ge(sem["in_lo"], C_DO + 2)
                    split(C_DO + 2)
                act.wait_ge(sem["oT2_bank"], b + 1)
                act.activation(hB_hi[:, 2 * b:2 * b + 2, :].rearrange("p m q -> p (m q)"), free_banks[b], ACT.Copy,
                               scale=gain(O_SG, 0)).then_inc(sem["oT_hi"], 1)
            split(C_DO + 3)
            ffn(1, C_F1, lambda: normalise(3, x_new(2)))
            norm(4, x_new(3), 2)
            act.wait_ge(sem["x_gain"], 1)
            act.wait_ge(sem["rstd"], 5)
            for cs in OUT_PIECES:
                act.activation(x[:, 0, cs], xs[:, 0, cs], ACT.Copy, scale=rstd[:, 0:1]).then_inc(sem["out0_ready"], 1)

        @block.vector
        def _(dve):
            sub = ALU.subtract

            def split(s, halves=(0, 1)):
                n, w = stage_of(s), width_of(s)
                for h in halves:
                    cs = slice(h * w // 2, (h + 1) * w // 2)
                    dve.wait_ge(sem["in_hi"], 2 * s + h + 1)
                    last = dve.tensor_tensor(win_lo[:, s % 2, cs], stage[:, n % 2, cs], win_hi[:, s % 2, cs].bitcast(F32), sub)
                    if h == 1:
                        last.then_inc(sem["in_lo"], 1)
                    elif s == 0:
                        last.then_inc(sem["first_lo"], 1)

            n_hi = [0]
            n_newton = [0]
            n_y = [0]

            def h_lo(dst, src_hi, off, ks=range(KT)):
                for k in ks:
                    n_hi[0] += 1
                    dve.wait_ge(sem["xT_hi"], n_hi[0] + n_hi[0] % 2)
                    dve.scalar_tensor_tensor(dst[:, k, :], free_banks[k // 2][:, (k % 2) * S:(k % 2 + 1) * S], gain(off, k),
                                             src_hi[:, k, :].bitcast(F32), ALU.mult, sub).then_inc(sem["xT_lo"], 1)

            n_rope = [0]

            def rope(src, dst, nh):
                n_rope[0] += 1
                half = ROT // 2
                t1, t2 = rope_t[:, 0, :, 0:nh, :], rope_t[:, 1, :, 0:nh, :]
                c = cosv.unsqueeze(2).to_broadcast([P, TT, nh, ROT])
                dve.tensor_tensor(t1, src[:, :, :, 0:ROT], c, ALU.mult).then_inc(sem["rope_t1"], 1)
                for a in range(2):
                    sn = sinv[:, :, a * half:(a + 1) * half].unsqueeze(2).to_broadcast([P, TT, nh, half])
                    dve.tensor_tensor(t2[:, :, :, a * half:(a + 1) * half], src[:, :, :, (1 - a) * half:(2 - a) * half], sn,
                                      ALU.mult).then_inc(sem["rope_t2"], 1)
                dve.wait_ge(sem["rope_t1"], n_rope[0])
                dve.wait_ge(sem["rope_t2"], 2 * n_rope[0])
                dve.tensor_tensor(dst[:, :, :, 0:ROT], t1, t2, ALU.add).then_inc(sem["rope_done"], 1)
                dve.wait_ge(sem["rope_done"], n_rope[0])

            def add_y(done, count):
                n_y[0] += 2
                dve.wait_ge(sem["y_ready"], n_y[0] - 1)
                dve.tensor_tensor(x[:, 0, :], psA[:, 0:2, :].rearrange("p n c -> p (n c)"), x[:, 0, :], ALU.add).then_inc(sem["x_new"], 1)
                dve.wait_ge(sem["y_ready"], n_y[0])
                dve.tensor_tensor(x[:, 1, 0:512], psA[:, 2, :], x[:, 1, 0:512], ALU.add)
                dve.wait_ge(sem[done], count)
                dve.tensor_tensor(x[:, 1, 512:D], psA[:, 3, :], x[:, 1, 512:D], ALU.add).then_inc(sem["x_new"], 1)

            def newton_done():
                n_newton[0] += 1
                dve.wait_ge(sem["newton"], n_newton[0])

            def rstd_of_root(n, roots):
                dve.wait_ge(sem["square"], TT * (n + 1))
                dve.tensor_scalar(ms, ssq, 1.0 / D, EPS, ALU.mult, ALU.add).then_inc(sem["newton"], 1)
                newton_done()
                dve.wait_ge(sem["root"], TT * (roots + 1))
                dve.reciprocal(rstd, root).then_inc(sem["newton"], 1)
                newton_done()
                dve.scalar_tensor_tensor(newton, rstd, -0.5, rstd, ALU.mult, ALU.mult).then_inc(sem["newton"], 1)
                newton_done()
                dve.tensor_tensor(newton, newton, ms, ALU.mult).then_inc(sem["newton"], 1)
                newton_done()
                dve.scalar_tensor_tensor(rstd, newton, 1.5, rstd, ALU.add, ALU.mult).then_inc(sem["rstd"], 1)
                dve.wait_ge(sem["rstd"], n + 1)

            def normalise(n, chunks):
                add_y("in_used", chunks)
                rstd_of_root(n, n // 2)
                for t in range(TT):
                    dve.tensor_scalar(xs[:, t, 0:D // 2], x[:, t, 0:D // 2], rstd[:, t:t + 1], None, ALU.mult).then_inc(sem["scaled_dve"], 1)

            def ffn(layer, first, normalise):
                f0 = layer * NJ

                def split_in(j, b, h):
                    slot = (first + b) % 2
                    dve.wait_ge(sem["in_hi"], 2 * j + (2 * first + h + 1))
                    cs = slice(h * W // 2, (h + 1) * W // 2)
                    last = dve.tensor_tensor(win_lo[:, slot, cs], stage[:, slot, cs], win_hi[:, slot, cs].bitcast(F32), sub)
                    if h == 1:
                        last.then_inc(sem["in_lo"], 1)

                def split_out(j, b):
                    dve.wait_ge(sem["out_hi"], j + (f0 + 1))
                    dve.tensor_tensor(wout_lo[:, b, :], stage_out[:, b, 0:D], wout_hi[:, b, :].bitcast(F32), sub).then_inc(sem["out_lo"], 1)

                def take_params(j, b):
                    dve.wait_ge(stage_out_full[b], 8 * j + (8 * f0 + 16 - 8 * b))
                    dve.tensor_copy(prm[:, b, :], stage_out[:, b, D:OW]).then_inc(sem["conv_params"], 1)

                def tap(b, g, k, wait, done):
                    wait()
                    dve.scalar_tensor_tensor(conv[:, b, g, k:S], (psT, psO)[g][:, b, 0:S - k], prm[:, b, 4 * g + 2 - k:4 * g + 3 - k],
                                             conv[:, b, g, k:S], ALU.mult, ALU.add).then_inc(sem[done], 1)

                def step(j, b, split_next=True, split_wout=True):
                    tap(b, 0, 1, lambda: dve.wait_ge(sem["conv0"], 2 * j + (2 * f0 + 1)), "gate1")
                    tap(b, 1, 1, lambda: dve.wait_ge(sem["conv0"], 2 * j + (2 * f0 + 2)), "val1")
                    tap(b, 0, 2, lambda: dve.wait_ge(sem["gate1"], j + (f0 + 1)), "gate2")
                    tap(b, 1, 2, lambda: dve.wait_ge(sem["val1"], j + (f0 + 1)), "val2")
                    take_params(j + 1, 1 - b)
                    if split_next:
                        split_in(j + 2, b, 0)
                    dve.wait_ge(sem["silu"], j + (f0 + 1))
                    dve.wait_ge(sem["val2"], j + (f0 + 1))
                    dve.tensor_tensor(prod[:, b, :], silu[:, b, :], conv[:, b, 1, :], ALU.mult).then_inc(sem["prod"], 1)
                    if split_next:
                        split_in(j + 2, b, 1)
                    dve.wait_ge(sem["a_hi"], j + (f0 + 1))
                    dve.tensor_tensor(act_lo[:, b, :], prod[:, b, :], act_hi[:, b, :].bitcast(F32), sub).then_inc(sem["a_lo"], 1)
                    if split_wout:
                        split_out(j + 1, 1 - b)

                def last_step():
                    taps = [prm[:, 1, k:k + 1] for k in range(2)]
                    for k, done in ((1, "gate1"), (2, "gate2")):
                        dve.wait_ge(sem["conv0" if k == 1 else "gate1"], 2 * (f0 + NJ) if k == 1 else f0 + NJ)
                        dve.scalar_tensor_tensor(conv[:, 1, 0, k:S], psT[:, 1, 0:S - k], taps[2 - k], conv[:, 1, 0, k:S],
                                                 ALU.mult, ALU.add).then_inc(sem[done], 1)
                    dve.wait_ge(sem["gate2"], f0 + NJ)
                    dve.tensor_copy(conv[0:LAST, 1, 1, :], conv[LAST:P, 1, 0, :]).then_inc(sem["val2"], 1)
                    dve.sem_inc(sem["val1"], 1)
                    dve.wait_ge(sem["silu"], f0 + NJ)
                    dve.wait_ge(sem["val2"], f0 + NJ)
                    dve.tensor_tensor(prod[0:LAST, 1, :], silu[0:LAST, 1, :], conv[0:LAST, 1, 1, :], ALU.mult).then_inc(sem["prod"], 1)
                    for h, (ready, count) in enumerate((("last_hi", layer + 1), ("out_hi", f0 + NJ))):
                        cs = slice(h * D // 2, (h + 1) * D // 2)
                        dve.wait_ge(sem[ready], count)
                        last = dve.tensor_tensor(wout_lo[:, 1, cs], stage_out[:, 1, cs], wout_hi[:, 1, cs].bitcast(F32), sub)
                    last.then_inc(sem["out_lo"], 1)
                    dve.wait_ge(sem["a_hi"], f0 + NJ)
                    dve.tensor_tensor(act_lo[0:LAST, 1, :], prod[0:LAST, 1, :], act_hi[0:LAST, 1, :].bitcast(F32), sub).then_inc(sem["a_lo"], 1)

                split_in(0, 0, 0)
                split_in(0, 0, 1)
                normalise()
                h_lo(hA_lo, hA_hi, O_FG + layer * KT)
                take_params(0, 0)
                split_in(1, 1, 0)
                split_in(1, 1, 1)
                split_out(0, 0)
                with dve.Fori(0, NJ // 2 - 1) as i:
                    for b in range(2):
                        step(2 * i + b, b)
                step(NJ - 2, 0, layer == 0, False)
                last_step()

            dve.memset(keysT[64:128, 0, :], 0.0).then_inc(sem["zero"], 1)
            dve.memset(keysT[0:64, 1, :], 0.0).then_inc(sem["zero"], 1)
            dve.wait_ge(sem["gains_in"], 16)
            h_lo(hA_lo, hA_hi, O_AG, range(2))
            split(0, (0,))
            h_lo(hA_lo, hA_hi, O_AG, range(2, 4))
            split(0, (1,))
            h_lo(hA_lo, hA_hi, O_AG, range(4, KT))
            split(1)
            dve.wait_ge(sem["square"], TT)
            dve.wait_ge(sem["params_in"], 16)
            dve.memset(blocks[:, :, :, :, NCMP:CP], 0.0).then_inc(sem["zero"], 1)
            for c in range(N_A):
                g = c // 2
                kind, width = GROUPS[g]
                if c % 2 and kind != "v":
                    dve.wait_ge(sem["in_used"], c + 1)
                    if kind == "q":
                        nh, h0 = Q_HEADS[g], Q_HEAD0[g]
                        dve.wait_ge(sem["proj_act"], g + 1)
                        for t in range(TT):
                            last = dve.tensor_copy(tokB[:, t, h0:h0 + nh, ROT:HD], tokA[:, t, h0:h0 + nh, ROT:HD])
                        last.then_inc(sem["proj_dve"], 1)
                        rope(tokA[:, :, h0:h0 + nh, :], tokB[:, :, h0:h0 + nh, :], nh)
                    elif kind == "k":
                        dve.wait_ge(sem["proj_act"], g + 1)
                        dve.sem_inc(sem["proj_dve"], 1)
                        rope(k_tok, k_tok, 8)
                    else:
                        dve.sem_inc(sem["proj_dve"], 1)
                if c + 2 < N_A:
                    split(c + 2)
                if c == 3:
                    for v in range(2):
                        dve.wait_ge(sem["pair_T"], v + 1)
                        for r in range(2):
                            dve.tensor_copy(pairs[r * 64:r * 64 + 64, v, 1:KVH:2, :].rearrange("p h (t u) -> p h t u", t=TT),
                                            psT[64:128, v, :].rearrange("p (h t r u) -> p r h t u", h=2, t=TT, r=2)[:, r]).then_inc(sem["pair_dve"], 1)
                if c in (6, 8):
                    dve.wait_ge(sem["pair_act"], 4)
                    dve.wait_ge(sem["pair_dve"], 4)
                    for v in (c // 2 - 3,):
                        for mh in range(2):
                            src = pairs[:, v, :, 8 * mh:8 * mh + 8 * NCMP].rearrange("p h (i m) -> p m h i", m=8)
                            for h in range(KVH):
                                last = dve.tensor_tensor(blocks[:, v, 8 * mh:8 * mh + 8, h, 0:NCMP], src[:, :, h, :],
                                                  pe[:, v, 8 * mh:8 * mh + 8].unsqueeze(2).to_broadcast([P, 8, NCMP]), ALU.add)
                            last.then_inc(sem["blocks_ready"], 1)
                if c == 7:
                    dve.wait_ge(sem["gate_e"], 1)
                    dve.tensor_scalar(gz, gz, 1.0, None, ALU.add).then_inc(sem["gate_e1"], 1)
                    dve.wait_ge(sem["gate_e1"], 1)
                    dve.reciprocal(gates[:, :, :, :].rearrange("p t h c -> p t (h c)"), gz).then_inc(sem["gates_ready"], 1)
                if c in (9, 10):
                    for i in range(4 * (c - 9) + 1, 4 * (c - 9) + 5, 2):
                        dve.wait_ge(sem["qT_bank"], i + 1)
                        dve.tensor_copy(qrT[:, i - 1:i + 1, :].rearrange("p m q -> p (m q)"), free_banks[i % 4]).then_inc(sem["qT_dve"], 1)
            dve.wait_ge(sem["zero"], 3)
            for pr in range(2):
                dve.wait_ge(sem["kT_bank"], pr + 1)
                for e in range(2):
                    dve.tensor_copy(keysT[e * 64:e * 64 + 64, e, (2 * pr + 1) * 512:(2 * pr + 2) * 512], psT[64:128, pr, :]).then_inc(sem["kT_dve"], 1)
            dve.wait_ge(sem["in_used"], N_A)
            dve.wait_ge(sem["rstd"], 1)
            dve.tensor_scalar(vals_nsa[:, 0, :, :, :, :].rearrange("p y g u d -> p (y g) u d"),
                              psA[:, 2, :].rearrange("p (h d) -> p h d", d=HD).unsqueeze(2).to_broadcast([P, 8, 2, HD]),
                              rstd[:, 0:1], None, ALU.mult).then_inc(sem["proj_dve"], 1)
            lam_in = cols[:, O_LAM:O_COS].rearrange("p (a b d) -> p a b d", a=2, b=2)
            dve.tensor_tensor(rope_t[:, 0, :, 0:4, :].rearrange("p a h r -> p a (h r)"), lam_in[:, :, 0, :], lam_in[:, :, 1, :], ALU.mult).then_inc(sem["lam_prod"], 1)
            dve.wait_ge(sem["lam_prod"], 1)
            dve.tensor_reduce(lam2, rope_t[:, 0, :, 0:4, :].rearrange("p a h r -> p a (h r)"), AX.X, ALU.add).then_inc(sem["lam_sum"], 2)
            dve.memset(kcT, 0.0).then_inc(sem["zero"], 1)
            def maxima(u, t, pre):
                nk = (t + 1) * P
                dve.wait_ge(sem[pre + "scores"], u + 1)
                dve.tensor_reduce(mx[:, u, :], psA[:, 2 * (u % 2):2 * (u % 2) + 2, :].rearrange("p e (y k) -> p (e y) k", y=2)[:, :, 0:nk],
                                  AX.X, ALU.max).then_inc(sem[pre + "smax"], 1)
                dve.wait_ge(sem[pre + "smax"], u + 1)
                dve.tensor_scalar(nmx[:, u, :], mx[:, u, :], -SCALE, None, ALU.mult).then_inc(sem[pre + "negmax"], 1)

            def reciprocals(u, pre):
                dve.wait_ge(sem[pre + "probs"], 4 * (u + 1))
                dve.reciprocal(rec[:, u, :], den[:, u, :]).then_inc(sem[pre + "recip"], 1)
                dve.wait_ge(sem[pre + "recip"], u + 1)

            NU = KVH * TT * 2
            def oT_lo(w):
                g, t = w // TT, w % TT
                for e in range(2):
                    dve.wait_ge(sem["oT_hi"], 2 * w + e + 1)
                    dst = slice(e * 64, e * 64 + 64)
                    dve.tensor_tensor(hB_lo[dst, 2 * g:2 * g + 2, t * P:(t + 1) * P],
                                      psO[dst, w % 2, :].rearrange("p (m e q) -> p e m q", m=2, e=2)[:, e],
                                      hB_hi[dst, 2 * g:2 * g + 2, t * P:(t + 1) * P].bitcast(F32), sub).then_inc(sem["oT_lo"], 1)

            dve.wait_ge(sem["gates_ready"], 1)

            def scale_probs(u):
                g, t, m2 = u // 4, (u // 2) % 2, u % 2
                reciprocals(u, "")
                h0 = 2 * (2 * g + m2)
                dve.tensor_tensor(fac[:, u, :].rearrange("p (e y) -> p e y", e=2), rec[:, u, :].rearrange("p (e y) -> p e y", e=2),
                                  gates[:, t, h0:h0 + 2, 1:3], ALU.mult).then_inc(sem["factor"], 1)
                dve.wait_ge(sem["factor"], u + 1)
                for e in range(2):
                    for y in range(2):
                        pr_ = probs[:, u % 2, e, y, 0:(t + 1) * P]
                        dve.tensor_scalar(pr_, pr_, fac[:, u, 2 * e + y:2 * e + y + 1], None, ALU.mult).then_inc(sem["scaled_p"], 1)

            def copy_pT(u):
                m2, nb = u % 2, (u // 2) % 2 + 1
                dve.wait_ge(sem["pT_bank"], u + 1)
                if u >= 4 and m2 == 0:
                    dve.wait_ge(sem["oT_bank"], u // 2 - 1)
                dve.tensor_copy(pT[:, (u // 2) % 2, 0:2 * nb, 2 * m2 + 1, :], psT[:, 1, 0:2 * nb * P].rearrange("p (i q) -> p i q", q=P)).then_inc(sem["pT_dve"], 1)

            maxima(0, 0, "")
            maxima(1, 0, "")
            scale_probs(0)
            scale_probs(1)
            copy_pT(0)
            maxima(2, 1, "")
            scale_probs(2)
            dve.wait_ge(sem["phi_used"], N_PHI)
            dve.tensor_tensor(hid, psO[0:64, 0, :].rearrange("p (v f) -> p v f", v=2), b1, ALU.add).then_inc(sem["hid_z"], 1)
            dve.wait_ge(sem["hid_z"], 1)
            dve.tensor_tensor(hid_a, hid, hid, ALU.mult).then_inc(sem["hid_z2"], 1)
            dve.wait_ge(sem["hid_z2"], 1)
            dve.tensor_scalar(hid_b, hid_a, 0.044715, 1.0, ALU.mult, ALU.add).then_inc(sem["hid_w"], 1)
            dve.wait_ge(sem["hid_w"], 1)
            dve.tensor_tensor(hid_a, hid_b, hid, ALU.mult).then_inc(sem["hid_y"], 1)
            copy_pT(1)
            dve.wait_ge(sem["hid_t"], 1)
            dve.scalar_tensor_tensor(hid, hid_b, 1.0, hid, ALU.add, ALU.mult).then_inc(sem["hid_ready"], 1)
            maxima(3, 1, "")
            maxima(4, 0, "")
            copy_pT(2)

            def mask_cmp(t):
                dve.wait_ge(sem["cmp_scores"], t + 1)
                mk = cols[:, O_CM + t * CP:O_CM + (t + 1) * CP].unsqueeze(1).unsqueeze(1).to_broadcast([P, 2, 2, CP])
                for mq in range(2):
                    for a in range(2):
                        g = 2 * mq + a
                        src = psO[:, mq, a * 256:(a + 1) * 256].rearrange("p (m e g c) -> p g m e c", m=2, e=2, g=KVH)[:, g]
                        dst = cmp_s[:, t, 4 * g:4 * g + 4, :].rearrange("p (m e) c -> p m e c", e=2)
                        dve.tensor_tensor(dst, src, mk, ALU.add).then_inc(sem["cmp_masked"], 1)

            mask_cmp(0)
            scale_probs(3)
            mask_cmp(1)
            dve.wait_ge(sem["cmp_masked"], 8)
            dve.tensor_reduce(cmx, cmp_s, AX.X, ALU.max).then_inc(sem["cmp_max"], 1)
            dve.wait_ge(sem["cmp_max"], 1)
            bc = [P, TT, HEADS, CP]
            dve.tensor_tensor(cmp_s, cmp_s, cmx.unsqueeze(3).to_broadcast(bc), sub).then_inc(sem["cmp_shift"], 1)
            maxima(5, 0, "")
            copy_pT(3)
            scale_probs(4)
            dve.wait_ge(sem["cmp_exp"], 1)
            dve.tensor_reduce(csum, cmp_p, AX.X, ALU.add).then_inc(sem["cmp_sum"], 1)
            dve.wait_ge(sem["cmp_sum"], 1)
            dve.reciprocal(crec, csum).then_inc(sem["cmp_recip"], 1)
            dve.wait_ge(sem["cmp_recip"], 1)
            dve.tensor_tensor(cfac, crec, gates[:, :, :, 0], ALU.mult).then_inc(sem["cmp_gate"], 1)
            dve.wait_ge(sem["cmp_gate"], 1)
            dve.tensor_tensor(cfac, cfac, cols[:, O_CV:O_CV + TT].unsqueeze(2).to_broadcast([P, TT, HEADS]), ALU.mult).then_inc(sem["cmp_valid"], 1)
            dve.wait_ge(sem["cmp_valid"], 1)
            dve.tensor_tensor(cmp_p, cmp_p, cfac.unsqueeze(3).to_broadcast(bc), ALU.mult).then_inc(sem["cmp_p"], 1)

            for u in range(4, NU):
                if u < NU - 2:
                    maxima(u + 2, ((u + 2) // 2) % 2, "")
                if u < NU - 1:
                    scale_probs(u + 1)
                copy_pT(u)
                if u % 2 == 0:
                    oT_lo(u // 2 - 2)
            oT_lo(NU // 2 - 2)
            oT_lo(NU // 2 - 1)
            split(C_WO + 2)
            split(C_WO + 3)

            ffn(0, C_F0, lambda: normalise(1, C_WO + N_WO))

            add_y("out_used", NJ)
            h_lo(hA_lo, hA_hi, O_KG)
            split(C_KV + 1)
            h_lo(hB_lo, hB_hi, O_AG + KT)
            for c in range(12):
                g = c // 2
                if c % 2:
                    dve.wait_ge(sem["in_used"], C_KV + c + 1)
                    if g < 4:
                        dst = tokA if g < 2 else tokB
                        dve.wait_ge(sem["proj_act"], NG + g + 1)
                        dve.sem_inc(sem["proj_dve"], 1)
                        v8 = dst[:, :, 8 * (g % 2):8 * (g % 2) + 8, :]
                        rope(v8, v8, 8)
                    else:
                        dve.wait_ge(sem["rstd"], 3)
                        dve.tensor_scalar(vals[:, 0, (g - 4) * 512:(g - 3) * 512], psA[:, 2 * (g % 2), :], rstd[:, 0:1], None, ALU.mult).then_inc(sem["proj_dve"], 1)
                if c == 6:
                    for i in range(4):
                        dve.wait_ge(sem["dk_bank"], i + 1)
                        dve.tensor_copy(keysT[64:128, 1, i * 512:(i + 1) * 512], free_banks[i][64:128, :]).then_inc(sem["dk_dve"], 1)
                if c == 8:
                    for i in range(1, 4, 2):
                        dve.wait_ge(sem["dq_bank"], i + 1)
                        dve.tensor_copy(qrT[:, 2 * i:2 * i + 2, :].rearrange("p m q -> p (m q)"), free_banks[i]).then_inc(sem["dq_dve"], 1)
                if c < 11:
                    split(C_KV + c + 2)
            dve.wait_ge(sem["lam_exp"], 1)
            dve.tensor_tensor(neg_lam, lame[:, 1:2], lame[:, 0:1], sub).then_inc(sem["lam_diff"], 1)
            dve.wait_ge(sem["lam_diff"], 1)
            dve.tensor_scalar(neg_lam, neg_lam, -LAM_INIT, None, ALU.add).then_inc(sem["lam_ready"], 1)
            dve.wait_ge(sem["lam_ready"], 1)
            ND = DH // 2 * TT

            def mix_probs(u):
                nk = (u % TT + 1) * P
                reciprocals(u, "d")
                r2 = rec[:, u, :].rearrange("p (e c) -> p e c", e=2)
                d2 = den[:, u, :].rearrange("p (e c) -> p e c", e=2)
                dve.scalar_tensor_tensor(fac[:, u, 0:2], d2[:, :, 0], neg_lam, r2[:, :, 1], ALU.mult, ALU.mult).then_inc(sem["dfactor"], 1)
                dve.wait_ge(sem["dfactor"], u + 1)
                for e in range(2):
                    p0 = probs[:, u % 2, e, 0, 0:nk]
                    dve.scalar_tensor_tensor(p0, probs[:, u % 2, e, 1, 0:nk], fac[:, u, e:e + 1], p0, ALU.mult, ALU.add).then_inc(sem["dmixed"], 1)

            def out_heads(u):
                hp, t = u // TT, u % TT
                dve.wait_ge(sem["do_bank"], u + 1)
                for e in range(2):
                    dve.tensor_scalar(o_tok[:, t, 2 * hp + e, :], psO[:, u % 2, e * DV:(e + 1) * DV], rec[:, u, 2 * e:2 * e + 1],
                                      None, ALU.mult).then_inc(sem["do_ready"], 1)

            def heads_lo(b):
                dve.wait_ge(sem["oT_hi"], 2 * KVH * TT + b + 1)
                dve.scalar_tensor_tensor(hB_lo[:, 2 * b:2 * b + 2, :].rearrange("p m q -> p (m q)"), free_banks[b], gain(O_SG, 0),
                                         hB_hi[:, 2 * b:2 * b + 2, :].rearrange("p m q -> p (m q)").bitcast(F32), ALU.mult, sub).then_inc(sem["oT_lo"], 1)
            maxima(0, 0, "d")
            maxima(1, 1, "d")
            for u in range(ND):
                nb = u % TT + 1
                if u < ND - 1:
                    mix_probs(u)
                if u + 2 < ND:
                    maxima(u + 2, u % TT, "d")
                if u == ND - 2:
                    mix_probs(ND - 1)
                if u >= 2:
                    out_heads(u - 2)
                dve.wait_ge(sem["dT_bank"], u + 1)
                if u >= 2:
                    dve.wait_ge(sem["do_bank"], u - 1)
                dve.tensor_copy(aT[:, u % 2, :, 0:nb, :], psT[:, u % 2, :].rearrange("p (e b q) -> p e b q", e=2, b=2)[:, :, 0:nb, :]).then_inc(sem["dT_ready"], 1)
            out_heads(ND - 2)
            out_heads(ND - 1)
            heads_lo(0)
            heads_rstd(dve, 1, "sub1_step", "sub1_rstd")
            scale_heads(dve, 2, "sub1_scaled")
            heads_lo(1)
            scale_heads(dve, 3, "sub1_scaled")
            heads_lo(2)
            split(C_DO + 2)
            heads_lo(3)
            split(C_DO + 3)
            ffn(1, C_F1, lambda: normalise(3, C_DO + N_DO))
            dve.wait_ge(sem["final_in"], 16)
            add_y("out_used", 2 * NJ)
            dve.wait_ge(sem["x_new"], 3 * TT + 1)
            dve.tensor_tensor(xs[:, 0, :], x[:, 0, :], final_g, ALU.mult).then_inc(sem["x_gain"], 1)
            rstd_of_root(4, 2)
            for cs in OUT_PIECES:
                dve.scalar_tensor_tensor(x[:, 1, cs], x[:, 1, cs], rstd[:, 1:2], final_g[:, cs], ALU.mult, ALU.mult).then_inc(sem["out1_ready"], 1)


def _layout(i):
    f = np.float32

    def ktiles(w, per):
        k, n = w.shape
        return np.ascontiguousarray(w.reshape(k // P // per, per, P, n).transpose(0, 2, 1, 3).reshape(-1, P, per * n))

    def col(v):
        return v.reshape(-1, P).T

    win = i["nsa_w_in"][0]
    q, kv, gt = win[:, :HEADS * HD], win[:, HEADS * HD:HEADS * HD + 6 * KV_W], win[:, HEADS * HD + 6 * KV_W:]
    kc, vc, ks, vs, kw, vw = (kv[:, n * KV_W:(n + 1) * KV_W] for n in range(6))
    groups = [np.concatenate([kc, vc], 1), q[:, :6 * HD], q[:, 6 * HD:11 * HD], np.concatenate([q[:, 11 * HD:], gt], 1),
              np.concatenate([ks, kw], 1), np.concatenate([vs, vw], 1)]
    arrays = {f"w_group{n}": ktiles(g, 4) for n, g in enumerate(groups)}
    arrays["x_tiles"] = i["x"].reshape(TT, P, D)
    arrays["w_phi"] = ktiles(i["nsa_phi_w1"][0].reshape(2 * CMP_BLOCK * HD, PHI), 8)
    arrays["w_nsa_out"] = ktiles(i["nsa_w_out"][0], 2)

    def column_groups(w):
        return np.concatenate([ktiles(w[:, n:n + 512], 4) for n in range(0, w.shape[1], 512)], 0)

    arrays["w_kv"] = column_groups(i["kv_w"])
    arrays["w_dq"] = column_groups(i["diff_w_q"][0])
    arrays["w_dout"] = ktiles(i["diff_w_out"][0], 2)
    full = (NJ - 1) * P
    fin = i["ffn_w_in"].reshape(2, KT, P, 2, FFN)
    most = fin[..., :full].reshape(2, KT, P, 2, NJ - 1, P).transpose(0, 4, 2, 1, 3, 5).reshape(2, NJ - 1, P, W)
    last = fin[..., full:].transpose(0, 2, 1, 3, 4).reshape(2, 1, P, KT * P)
    fin = np.concatenate([most, np.pad(last, ((0, 0), (0, 0), (0, 0), (0, W - KT * P)))], 1)
    fout = np.pad(i["ffn_w_out"], ((0, 0), (0, NJ * P - FFN), (0, 0))).reshape(2, NJ, P, D)
    taps = np.concatenate([i["ffn_conv_w"], i["ffn_conv_b"][:, None]], 1).reshape(2, 4, 2, FFN)
    most = taps[..., :full].reshape(2, 4, 2, NJ - 1, P).transpose(0, 3, 4, 2, 1).reshape(2, NJ - 1, P, NPRM)
    last = taps[..., full:].transpose(0, 2, 3, 1).reshape(2, 1, P, 4)
    taps = np.concatenate([most, np.pad(last, ((0, 0), (0, 0), (0, 0), (0, NPRM - 4)))], 1)
    arrays["w_ffn_in"] = np.ascontiguousarray(fin)
    arrays["w_ffn_out"] = np.ascontiguousarray(np.concatenate([fout, taps], 3))
    pe = i["nsa_phi_pe"][0].reshape(2, CP, P).transpose(2, 0, 1).reshape(P, -1)
    w2 = i["nsa_phi_w2"][0].reshape(2, 2, P, 1, HD)
    w2 = np.broadcast_to(w2, (2, 2, P, 2, HD)).transpose(2, 0, 1, 3, 4).reshape(P, -1)
    rows = np.arange(P)
    rowmask = ((rows[:, None] // CP == np.arange(8)[None, :]) & (rows[:, None] % CP < NCMP)).astype(f)
    lam = np.broadcast_to(i["diff_lambda"][0].reshape(1, -1), (P, 4 * HD))
    inv = np.float32(500000.0) ** (-np.arange(ROT // 2, dtype=f) / f(ROT // 2))
    ang = np.arange(S, dtype=f)[:, None] * inv[None, :]
    cos, sin = np.cos(ang).astype(f), np.sin(ang).astype(f)

    def tok(v):
        return v.reshape(TT, P, -1).transpose(1, 0, 2).reshape(P, -1)

    pos = np.arange(S)
    visible = (np.arange(CP)[None, :] * CMP_STRIDE + CMP_BLOCK - 1 <= pos[:, None]) & (np.arange(CP)[None, :] < NCMP)
    cmp_mask = np.where(visible, 0.0, NEG).astype(f)
    cmp_any = visible.any(1, keepdims=True).astype(f)
    b1 = np.broadcast_to(i["nsa_phi_b1"][0].reshape(1, -1), (P, 2 * PHI))
    table = [col(i["attn_norm_g"][0]), col(i["attn_norm_g"][1]), col(i["ffn_norm_g"][0]), col(i["ffn_norm_g"][1]), col(i["kv_norm_g"]),
             i["diff_subln_g"][0][:, None], pe, w2, rowmask, lam, tok(np.concatenate([cos, cos], 1)), tok(np.concatenate([-sin, sin], 1)),
             tok(cmp_mask), tok(cmp_any), b1]
    arrays["param_cols"] = np.ascontiguousarray(np.concatenate(table, 1).astype(f))
    assert arrays["param_cols"].shape == (P, NCOL)
    arrays["ident"] = np.eye(P, dtype=f)
    arrays["final_g"] = np.ascontiguousarray(np.broadcast_to(i["final_norm_g"][None, :], (P, D)))
    return arrays


def kernel(**inputs):
    import ml_dtypes
    import concourse.bacc as bacc
    from concourse.bass_utils import run_bass_kernel_spmd

    arrays = _layout({k: np.asarray(v) for k, v in inputs.items()})
    arrays["causal"] = np.where(np.arange(P)[None, :] <= np.arange(P)[:, None], 0.0, NEG).astype(ml_dtypes.bfloat16)
    nc = bacc.Bacc("TRN2", target_bir_lowering=False, num_devices=1)
    arrays = {f"in_{n}": a for n, a in arrays.items()}
    ap = {n[3:]: nc.dram_tensor(n, a.shape, mybir.dt.from_np(a.dtype), kind="ExternalInput").ap() for n, a in arrays.items()}
    out = nc.dram_tensor("out", (TT, P, D), F32, kind="ExternalOutput").ap()
    build(nc, ap["x_tiles"], ap["param_cols"], ap["ident"], ap["causal"], [ap[f"w_group{g}"] for g in range(NG)],
          ap["w_phi"], ap["w_nsa_out"], ap["w_ffn_in"], ap["w_ffn_out"], ap["w_kv"], ap["w_dq"], ap["w_dout"], ap["final_g"], out)
    r = run_bass_kernel_spmd(nc, [arrays], core_ids=[0])
    return r.results[0]["out"].reshape(1, S, D)
```
